# Optimizing a Trainium2 kernel written in Bass

```python
import jax, jax.numpy as jnp
from jax import lax
import numpy as np

D_MODEL = 1024
BATCH = 1
SEQ = 512
DEPTH = 1

HEAD_DIM = 64
ROPE_DIM = HEAD_DIM // 4
ROPE_THETA = 500000.0
NORM_EPS = 1e-6
D_FF = 2816

NSA_HEADS = 8
NSA_KV_GROUPS = 2
NSA_HPG = NSA_HEADS // NSA_KV_GROUPS
CMP_BLOCK = 32
CMP_STRIDE = 16
CMP_HIDDEN = 2 * HEAD_DIM
SLC_BLOCK = 64
SLC_TOPN = 16
WIN = 512
Q_BLOCK = 128
FORCE = 1e9

DIL_PAIRS = ((128, 1), (512, 4), (2048, 16))
DIL_GROUPS = len(DIL_PAIRS)
DIL_HEADS = 4
DIL_BLOCK = 128

NSA_Q = NSA_HEADS * HEAD_DIM
NSA_KV = NSA_KV_GROUPS * HEAD_DIM
DIL_W = DIL_HEADS * HEAD_DIM
IN_SIZES = (NSA_Q, 6 * NSA_KV, 3 * NSA_HEADS, 3 * DIL_GROUPS * DIL_W, 2 * D_MODEL)
N_IN = sum(IN_SIZES)
NEG = -1e30

kernel_name = "hybrid_nsa_dilated_macaron_block"

def rmsnorm(x, g):
    x32 = x.astype(jnp.float32)
    y = x32 * lax.rsqrt(jnp.mean(x32 * x32, axis=-1, keepdims=True) + NORM_EPS) * g.astype(jnp.float32)
    return y.astype(x.dtype)

def swiglu(h, w_in, w_out):
    u, v = jnp.split(h @ w_in, 2, axis=-1)
    return (jax.nn.silu(u) * v) @ w_out

def rope_tables(positions):
    inv = jnp.power(ROPE_THETA, -jnp.arange(0, ROPE_DIM, 2, dtype=jnp.float32) / ROPE_DIM)
    ang = positions.astype(jnp.float32)[..., None] * inv
    return jnp.cos(ang), jnp.sin(ang)

def rope_partial(x, cos, sin):
    shp = cos.shape[:2] + (1,) * (x.ndim - 3) + cos.shape[-1:]
    c = cos.reshape(shp).astype(x.dtype)
    s = sin.reshape(shp).astype(x.dtype)
    half = ROPE_DIM // 2
    x1, x2, xp = x[..., :half], x[..., half:ROPE_DIM], x[..., ROPE_DIM:]
    return jnp.concatenate([x1 * c - x2 * s, x2 * c + x1 * s, xp], axis=-1)

def masked_softmax_stats(s, mask):
    s = s.astype(jnp.float32)
    m = jnp.max(jnp.where(mask, s, NEG), axis=-1, keepdims=True)
    e = jnp.exp(jnp.where(mask, s - m, NEG))
    d = jnp.sum(e, axis=-1, keepdims=True)
    return e / jnp.where(d > 0, d, 1.0), m, d

def compress(tok, pos, w1, w2):
    B, T, G, dh = tok.shape
    seg = tok.reshape(B, T // CMP_STRIDE, CMP_STRIDE, G, dh)
    blocks = jnp.concatenate([seg[:, :-1], seg[:, 1:]], axis=2) + pos[None, None, :, None, :]
    n_cmp = blocks.shape[1]
    flat = blocks.transpose(0, 1, 3, 2, 4).reshape(B, n_cmp, G, CMP_BLOCK * dh)
    return jax.nn.silu(flat @ w1) @ w2

def slc_map(n_cmp, n_slc):
    i = np.arange(n_cmp)[:, None]
    j = np.arange(n_slc)[None, :]
    lo = np.maximum(i * CMP_STRIDE, j * SLC_BLOCK)
    hi = np.minimum(i * CMP_STRIDE + CMP_BLOCK, (j + 1) * SLC_BLOCK)
    return (np.maximum(hi - lo, 0) / CMP_BLOCK).astype(np.float32)

def nsa_attention(q, q_rope, kc, vc, ks, vs, kw, vw, gates):
    B, T, G, Hg, dh = q.shape
    n_cmp = kc.shape[1]
    n_slc = T // SLC_BLOCK
    n_sel = min(SLC_TOPN, n_slc)
    scale = HEAD_DIM ** -0.5
    cmap = jnp.asarray(slc_map(n_cmp, n_slc))
    cmp_end = jnp.arange(n_cmp) * CMP_STRIDE + CMP_BLOCK - 1
    blk = jnp.arange(n_slc)
    ks_blk = ks.reshape(B, n_slc, SLC_BLOCK, G, dh).transpose(0, 3, 1, 2, 4)
    vs_blk = vs.reshape(B, n_slc, SLC_BLOCK, G, dh).transpose(0, 3, 1, 2, 4)
    kw_p = jnp.pad(kw, ((0, 0), (WIN, 0), (0, 0), (0, 0)))
    vw_p = jnp.pad(vw, ((0, 0), (WIN, 0), (0, 0), (0, 0)))
    bi = jnp.arange(B)[:, None, None, None]
    gi = jnp.arange(G)[None, :, None, None]

    def block(c):
        t0 = c * Q_BLOCK
        t = t0 + jnp.arange(Q_BLOCK)
        qc = lax.dynamic_slice_in_dim(q, t0, Q_BLOCK, axis=1)
        qr = lax.dynamic_slice_in_dim(q_rope, t0, Q_BLOCK, axis=1)
        gc = lax.dynamic_slice_in_dim(gates, t0, Q_BLOCK, axis=1)
        s = jnp.einsum('bqghd,bngd->bghqn', qc, kc) * scale
        p_c, _, _ = masked_softmax_stats(s, cmp_end[None, :] <= t[:, None])
        o_c = jnp.einsum('bghqn,bngd->bqghd', p_c.astype(vc.dtype), vc)
        imp = jnp.einsum('bghqn,nj->bgqj', p_c, cmap)
        cur = (t // SLC_BLOCK)[:, None]
        valid = blk[None, :] <= cur
        forced = (blk[None, :] == 0) | (blk[None, :] == cur) | (blk[None, :] == cur - 1)
        imp = jnp.where(forced, FORCE, jnp.where(valid, imp, -FORCE))
        top_val, idx = lax.top_k(imp, n_sel)
        sel_ok = top_val > -0.5 * FORCE
        kg = ks_blk[bi, gi, idx]
        vg = vs_blk[bi, gi, idx]
        s = jnp.einsum('bqghd,bgqnkd->bghqnk', qr, kg) * scale
        kpos = idx[..., None] * SLC_BLOCK + jnp.arange(SLC_BLOCK)
        mask_s = sel_ok[..., None] & (kpos <= t[None, None, :, None, None])
        p_s, _, _ = masked_softmax_stats(s.reshape(B, G, Hg, Q_BLOCK, n_sel * SLC_BLOCK),
                                         mask_s.reshape(B, G, 1, Q_BLOCK, n_sel * SLC_BLOCK))
        p_s = p_s.reshape(B, G, Hg, Q_BLOCK, n_sel, SLC_BLOCK)
        o_s = jnp.einsum('bghqnk,bgqnkd->bqghd', p_s.astype(vg.dtype), vg)
        kwc = lax.dynamic_slice_in_dim(kw_p, t0, Q_BLOCK + WIN, axis=1)
        vwc = lax.dynamic_slice_in_dim(vw_p, t0, Q_BLOCK + WIN, axis=1)
        s = jnp.einsum('bqghd,bkgd->bghqk', qr, kwc) * scale
        kp = t0 - WIN + jnp.arange(Q_BLOCK + WIN)
        diff = t[:, None] - kp[None, :]
        p_w, _, _ = masked_softmax_stats(s, (diff >= 0) & (diff < WIN) & (kp[None, :] >= 0))
        o_w = jnp.einsum('bghqk,bkgd->bqghd', p_w.astype(vwc.dtype), vwc)
        return gc[..., 0:1] * o_c + gc[..., 1:2] * o_s + gc[..., 2:3] * o_w

    out = lax.map(block, jnp.arange(T // Q_BLOCK))
    return out.transpose(1, 0, 2, 3, 4, 5).reshape(B, T, G * Hg * dh)

def dilated_group(q, k, v, dilation, span):
    B, T, H, dh = q.shape
    L = T // dilation
    Lp = -(-L // DIL_BLOCK) * DIL_BLOCK
    nb = Lp // DIL_BLOCK
    scale = HEAD_DIM ** -0.5

    def to_sub(a):
        a = a.reshape(B, L, dilation, H, dh).transpose(0, 2, 3, 1, 4)
        return jnp.pad(a, ((0, 0), (0, 0), (0, 0), (0, Lp - L), (0, 0)))

    def with_prev(a):
        a = jnp.pad(a, ((0, 0), (0, 0), (0, 0), (DIL_BLOCK, 0), (0, 0)))
        a = a.reshape(B, dilation, H, nb + 1, DIL_BLOCK, dh)
        return jnp.concatenate([a[:, :, :, :-1], a[:, :, :, 1:]], axis=4)

    qb = to_sub(q).reshape(B, dilation, H, nb, DIL_BLOCK, dh)
    kb = with_prev(to_sub(k))
    vb = with_prev(to_sub(v))
    s = jnp.einsum('brhnqd,brhnkd->brhnqk', qb, kb) * scale
    qi = jnp.arange(nb)[:, None] * DIL_BLOCK + jnp.arange(DIL_BLOCK)[None, :]
    kj = jnp.arange(nb)[:, None] * DIL_BLOCK - DIL_BLOCK + jnp.arange(2 * DIL_BLOCK)[None, :]
    diff = qi[:, :, None] - kj[:, None, :]
    mask = (diff >= 0) & (diff <= span) & (kj[:, None, :] >= 0)
    p, m, d = masked_softmax_stats(s, mask)
    o = jnp.einsum('brhnqk,brhnkd->brhnqd', p.astype(vb.dtype), vb)
    o = o.reshape(B, dilation, H, Lp, dh)[:, :, :, :L].transpose(0, 3, 1, 2, 4).reshape(B, T, H, dh)
    lse = (m + jnp.log(d))[..., 0].reshape(B, dilation, H, Lp)[..., :L]
    lse = lse.transpose(0, 3, 1, 2).reshape(B, T, H)
    return o, lse

def hybrid_mixer(h, cos, sin, w_in, cmp_pos, cmp_w1, cmp_w2, w_branch_nsa, w_branch_dil, w_out):
    B, T, _ = h.shape
    G, Hg, dh = NSA_KV_GROUPS, NSA_HPG, HEAD_DIM
    cuts = np.cumsum(IN_SIZES)[:-1].tolist()
    q_n, kv_n, g_n, qkv_d, g_m = jnp.split(h @ w_in, cuts, axis=-1)
    q_n = q_n.reshape(B, T, NSA_HEADS, dh)
    q_r = rope_partial(q_n, cos, sin).reshape(B, T, G, Hg, dh)
    q_n = q_n.reshape(B, T, G, Hg, dh)
    kv_n = kv_n.reshape(B, T, 6, G, dh)
    kc = compress(kv_n[:, :, 0], cmp_pos[0], cmp_w1[0], cmp_w2[0])
    vc = compress(kv_n[:, :, 1], cmp_pos[1], cmp_w1[1], cmp_w2[1])
    ks = rope_partial(kv_n[:, :, 2], cos, sin)
    kw = rope_partial(kv_n[:, :, 4], cos, sin)
    gates = jax.nn.sigmoid(g_n.astype(jnp.float32)).astype(h.dtype).reshape(B, T, G, Hg, 3)
    y_nsa = nsa_attention(q_n, q_r, kc, vc, ks, kv_n[:, :, 3], kw, kv_n[:, :, 5], gates)
    qkv_d = qkv_d.reshape(B, T, 3, DIL_GROUPS, DIL_HEADS, dh)
    q_d = rope_partial(qkv_d[:, :, 0], cos, sin)
    k_d = rope_partial(qkv_d[:, :, 1], cos, sin)
    outs, lses = [], []
    for gidx, (window, dil) in enumerate(DIL_PAIRS):
        o, lse = dilated_group(q_d[:, :, gidx], k_d[:, :, gidx], qkv_d[:, :, 2, gidx], dil, window // dil)
        outs.append(o)
        lses.append(lse)
    alpha = jax.nn.softmax(jnp.stack(lses, axis=2), axis=2).astype(h.dtype)
    y_dil = jnp.sum(alpha[..., None] * jnp.stack(outs, axis=2), axis=2).reshape(B, T, DIL_W)
    g_m = jax.nn.sigmoid(g_m.astype(jnp.float32)).astype(h.dtype).reshape(B, T, 2, D_MODEL)
    merged = g_m[:, :, 0] * (y_nsa @ w_branch_nsa) + g_m[:, :, 1] * (y_dil @ w_branch_dil)
    return merged @ w_out

def setup_inputs(seed: int = 0) -> dict:
    key = jax.random.key(seed)
    ks = jax.random.split(key, 20)
    f32 = jnp.float32

    def w(k, shape, fan_in):
        return jax.random.normal(k, shape, f32) * fan_in ** -0.5

    def gain(k, shape):
        return 1.0 + 0.02 * jax.random.normal(k, shape, f32)

    x = jax.random.normal(ks[0], (BATCH, SEQ, D_MODEL), f32)
    offset = jax.random.randint(ks[1], (BATCH, 1), 0, 4096, dtype=jnp.int32)
    positions = (offset + jnp.arange(SEQ, dtype=jnp.int32)[None, :]).astype(jnp.int32)
    return {
        "x": x,
        "positions": positions,
        "norm_ffn1": gain(ks[2], (DEPTH, D_MODEL)),
        "ffn1_w_in": w(ks[3], (DEPTH, D_MODEL, 2 * D_FF), D_MODEL),
        "ffn1_w_out": w(ks[4], (DEPTH, D_FF, D_MODEL), D_FF),
        "norm_mix": gain(ks[5], (DEPTH, D_MODEL)),
        "w_in": w(ks[6], (DEPTH, D_MODEL, N_IN), D_MODEL),
        "cmp_pos": 0.02 * jax.random.normal(ks[7], (DEPTH, 2, CMP_BLOCK, HEAD_DIM), f32),
        "cmp_w1": w(ks[8], (DEPTH, 2, CMP_BLOCK * HEAD_DIM, CMP_HIDDEN), CMP_BLOCK * HEAD_DIM),
        "cmp_w2": w(ks[9], (DEPTH, 2, CMP_HIDDEN, HEAD_DIM), CMP_HIDDEN),
        "w_branch_nsa": w(ks[10], (DEPTH, NSA_Q, D_MODEL), NSA_Q),
        "w_branch_dil": w(ks[11], (DEPTH, DIL_W, D_MODEL), DIL_W),
        "w_out": w(ks[12], (DEPTH, D_MODEL, D_MODEL), D_MODEL),
        "norm_ffn2": gain(ks[13], (DEPTH, D_MODEL)),
        "ffn2_w_in": w(ks[14], (DEPTH, D_MODEL, 2 * D_FF), D_MODEL),
        "ffn2_w_out": w(ks[15], (DEPTH, D_FF, D_MODEL), D_FF),
        "norm_final": gain(ks[16], (D_MODEL,)),
    }

def reference(x, positions, norm_ffn1, ffn1_w_in, ffn1_w_out, norm_mix, w_in, cmp_pos, cmp_w1, cmp_w2,
              w_branch_nsa, w_branch_dil, w_out, norm_ffn2, ffn2_w_in, ffn2_w_out, norm_final):
    cos, sin = rope_tables(positions)
    for l in range(DEPTH):
        x = x + 0.5 * swiglu(rmsnorm(x, norm_ffn1[l]), ffn1_w_in[l], ffn1_w_out[l])
        x = x + hybrid_mixer(rmsnorm(x, norm_mix[l]), cos, sin, w_in[l], cmp_pos[l], cmp_w1[l], cmp_w2[l],
                             w_branch_nsa[l], w_branch_dil[l], w_out[l])
        x = x + 0.5 * swiglu(rmsnorm(x, norm_ffn2[l]), ffn2_w_in[l], ffn2_w_out[l])
    return rmsnorm(x, norm_final)


_drawn_inputs = setup_inputs


def setup_inputs(seed=0):
    import zlib

    import numpy as np

    out = dict(_drawn_inputs(seed))
    spreads = {}
    factors = {'norm_ffn1': 6.455,
     'norm_mix': 8.0,
     'cmp_pos': 37.616,
     'norm_ffn2': 18.692,
     'norm_final': 8.163}
    for name, (base, spread) in spreads.items():
        noise = np.random.default_rng([zlib.crc32(name.encode()), seed]).standard_normal(out[name].shape)
        drawn = base * np.exp(spread * noise) if base else spread * noise
        out[name] = __import__('jax').numpy.asarray(drawn.astype(out[name].dtype))
    for name, factor in factors.items():
        out[name] = (out[name] * factor).astype(out[name].dtype)
    return out
```

```python
from contextlib import ExitStack

import numpy as np

import concourse.bass as bass
from concourse import mybir

ALU = mybir.AluOpType
ACT = mybir.ActivationFunctionType
AX = mybir.AxisListType
F32 = mybir.dt.float32
F32R = mybir.dt.float32r
BF16 = mybir.dt.bfloat16
I32 = mybir.dt.int32

P = 128
T = 512
D = 1024
FF = 2816
TT = T // P
KD = D // P
FT = FF // P
HALF = FT // 2
DH = 64
HPG = 4
NCMP = 31
NC = 32
KCOL = 512
GCOL = KCOL + 6 * P
DCOL = GCOL + 24
DW = 3 * 256
MCOL = DCOL + 3 * DW
SCALE = DH ** -0.5
EPS = 1e-6
BIG = 2.0 ** 100
THETA = 500000.0
TWO_PI = (6.28125, 0.0019350051879882812, 3.0199159819e-07)
MAGIC = 12582912.0
SLOT = 16 * P


def shape_constants():
    f = np.zeros((P, 3 * P + 4), np.float32)
    f[:, 0:P] = np.eye(P)
    f[:, P:2 * P] = 1.0
    for head in range(2):
        for i in range(8):
            f[head * DH + 8 + i, 2 * P + head * DH + i] = -1.0
            f[head * DH + i, 2 * P + head * DH + 8 + i] = 1.0
            freq = np.float32(THETA) ** np.float32(-2 * i / 16)
            f[head * DH + i, 3 * P] = freq
            f[head * DH + 8 + i, 3 * P] = freq
    q = np.arange(P)[:, None]
    k = np.arange(P)[None, :]
    b = np.zeros((P, 4 * P + 2 * P + 2 * T), np.float32)
    b[:, 0:P] = np.eye(P)
    b[:, P:2 * P] = np.where(k <= q, 0, -BIG)
    b[:, 2 * P:3 * P] = np.where(k >= q, 0, -BIG)
    n = np.arange(NC)[None, :]
    for qt in range(TT):
        ok = (n * 16 + 31 <= qt * P + q) & (n < NCMP)
        b[:, 3 * P + qt * NC:3 * P + (qt + 1) * NC] = np.where(ok, 0, -BIG)
    kk = np.arange(T)[None, :]
    for i, dil in enumerate((4, 16)):
        r = np.arange(dil)[:, None]
        b[0:dil, (4 + i) * P:(5 + i) * P] = (k % dil == r)
        b[0:dil, 6 * P + i * T:6 * P + (i + 1) * T] = np.where(kk % dil == r, 0, -BIG)
    return f, b


def build(nc, x, positions, norm_ffn1, ffn1_w_in, ffn1_w_out, norm_mix, w_in, cmp_pos, cmp_w1, cmp_w2,
          w_branch_nsa, w_branch_dil, w_out, norm_ffn2, ffn2_w_in, ffn2_w_out, norm_final,
          consts, masks, out):
    outer = ExitStack()
    with outer:
        def sem(name):
            return outer.enter_context(nc.semaphore(name))

        def sb(name, shape, dt=F32, scope=outer):
            return scope.enter_context(nc.sbuf_tensor(name, shape, dt))

        xT = sb("xT", [P, KD, T])
        xg_hi = sb("xg_hi", [P, KD, T], F32R)
        xg_lo = sb("xg_lo", [P, KD, T], F32R)
        w_raw = sb("w_raw", [P, 2, SLOT])
        w_hi = sb("w_hi", [P, 2, SLOT], F32R)
        w_lo = sb("w_lo", [P, 2, SLOT], F32R)
        rstd_row = sb("rstd_row", [P, T])
        rstd_col = sb("rstd_col", [P, TT])
        cos_t = sb("cos_t", [P, T])
        sin_t = sb("sin_t", [P, T])
        sumsq = sb("sumsq", [P, T])
        square = sb("square", [P, 2, T])
        tmp_a = sb("tmp_a", [P, T])
        tmp_b = sb("tmp_b", [P, T])
        const = sb("const", [P, 3 * P + 4])
        vec_rows = sb("vec_rows", [64, P])
        vec_cols = sb("vec_cols", [P, 64])
        norm_s = sb("norm_s", [P, 4, TT])
        gains = vec_cols[:, 0:32].rearrange("p (n m) -> p n m", n=4)
        pos_t = vec_cols[:, 32:64].rearrange("p (v j) -> p v j", v=2)
        ident = const[:, 0:P]
        ones = const[:, P:2 * P]
        swap_perm = const[:, 2 * P:3 * P]
        freq = const[:, 3 * P:3 * P + 1]

        with ExitStack() as scope:
            x_nat = sb("x_nat", [P, TT, D], F32, scope)
        with ExitStack() as scope:
            p_hi = sb("p_hi", [P, FT, T], F32R, scope)
            p_lo = sb("p_lo", [P, FT, T], F32R, scope)
        y_scope = ExitStack()
        y = sb("y", [P, 6, T], F32, y_scope)
        with ExitStack() as scope:
            pool = sb("pool", [P, 16, T], F32, scope)
            v_nsa = sb("v_nsa", [P, TT, 2, P], F32, scope)
            v_dil = sb("v_dil", [P, TT, 3, 256], F32, scope)
            k_cmp = sb("k_cmp", [P, P], F32, scope)
            v_cmp = sb("v_cmp", [NC, 2, DH], F32, scope)
            probs = sb("probs", [P, 2, 1280], F32, scope)
            probs_t = sb("probs_t", [P, 2, 1280], F32, scope)
            gates = sb("gates", [P, TT, 24], F32, scope)
            stat = sb("stat", [P, 2, 4, 4], F32, scope)
            mask = sb("mask", [P, 6 * P + 2 * T], BF16, scope)
            w2 = sb("w2", [P, 2, DH], F32, scope)
            hid = sb("hid", [DH, 2, P], F32, scope)
            hid_t = sb("hid_t", [P, 2, DH], F32, scope)
        with ExitStack() as scope:
            y_hi = sb("y_hi", [P, 6, T], F32R, scope)
            y_lo = sb("y_lo", [P, 6, T], F32R, scope)
            merged_hi = sb("merged_hi", [P, KD, T], F32R, scope)
            merged_lo = sb("merged_lo", [P, KD, T], F32R, scope)
        y_scope.close()
        ident_b = mask[:, 0:P]
        causal_b = mask[:, P:2 * P]
        prev_b = mask[:, 2 * P:3 * P]
        cmp_b = mask[:, 3 * P:4 * P]

        def residue(i):
            dil = (4, 16)[i]
            return mask[0:dil, (4 + i) * P:(5 + i) * P], mask[0:dil, 6 * P + i * T:6 * P + (i + 1) * T]

        ps = outer.enter_context(nc.psum_tensor("ps", [P, 8, T], F32))

        def ktiles(w):
            return w.rearrange("(k p) c -> p k c", p=P)

        win = ktiles(w_in[0])
        MU = []

        def columns(cols, c):
            MU.append((c * len(cols) * KD, [((i * KD * c, KD, c), win[:, :, at:at + c])
                                            for i, at in enumerate(cols)], True))
            return len(MU) - 1

        U_CTOK = columns([KCOL, KCOL + P], P)
        U_K = columns([KCOL + 2 * P, KCOL + 4 * P], P)
        U_GATE = columns([GCOL], P)
        U_V = columns([KCOL + 3 * P, KCOL + 5 * P], P)
        U_Q = []
        wq = win[:, :, 0:KCOL].rearrange("p k (g c) -> p k g c", g=2)
        for u in range(2):
            MU.append((SLOT, [((i * KD * P, KD, P), wq[:, :, g, (2 * u + i) * DH:(2 * u + i + 1) * DH], 0, g)
                              for i in range(2) for g in range(2)], True))
            U_Q.append(len(MU) - 1)
        U_W1 = []
        for kv in range(2):
            w1 = cmp_w1[0, kv].rearrange("(j q) h -> q j h", q=P)
            MU.append((SLOT, [((h * 1024, 8, P), w1[:, 8 * h:8 * h + 8, :]) for h in range(2)], False))
            U_W1.append(len(MU) - 1)
        U_VD = [columns([DCOL + 2 * DW + g * 256, DCOL + 2 * DW + g * 256 + P], P) for g in range(3)]
        U_QK = [[columns([DCOL + g * 256 + hp * P, DCOL + DW + g * 256 + hp * P], P) for g in range(3)]
                for hp in range(2)]
        nsa_w = w_branch_nsa[0].rearrange("(g h d) c -> g d h c", g=2, d=DH)
        dil_w = ktiles(w_branch_dil[0])
        U_GM, U_BR = {}, {}
        for mm in range(KD // 2):
            U_GM[2 * mm] = columns([MCOL + 2 * mm * P, MCOL + D + 2 * mm * P], P)
            cs = slice(mm * 256, mm * 256 + 256)
            MU.append((6 * 256, [((0, 4, 256), nsa_w[0][:, :, cs], 0), ((0, 4, 256), nsa_w[1][:, :, cs], DH),
                                 ((1024, 2, 256), dil_w[:, :, cs])], True))
            U_BR[mm] = len(MU) - 1
            U_GM[2 * mm + 1] = columns([MCOL + (2 * mm + 1) * P, MCOL + D + (2 * mm + 1) * P], P)
        wo = ktiles(w_out[0])
        U_WO = []
        for mm in range(KD // 2):
            cs = slice(mm * 256, mm * 256 + 256)
            MU.append((SLOT, [((h * 1024, 4, 256), wo[:, 4 * h:4 * h + 4, cs]) for h in range(2)], True))
            U_WO.append(len(MU) - 1)

        FU = FT + 2 * KD
        MIX0 = FU
        FFN2 = MIX0 + len(MU)
        N_UNITS = FFN2 + FU
        UNSPLIT = [MIX0 + u for u in U_W1]

        def split_no(j):
            return j - sum(u < j for u in UNSPLIT)

        landed_at = []
        total = [0, 0]
        for j in range(N_UNITS):
            n = len(MU[j - MIX0][1]) if MIX0 <= j < FFN2 else 2
            total[j % 2] += 16 * n
            landed_at.append(total[j % 2])

        landed = [sem("weights_landed_0"), sem("weights_landed_1")]
        hi_ready = sem("weight_hi_ready")
        lo_ready = sem("weight_lo_ready")
        cmp_w1_used = sem("cmp_w1_used")
        const_landed = sem("const_landed")
        vec_landed = sem("gains_and_cmp_pos_landed")
        x_landed = sem("x_landed")
        gains_psum = sem("gains_in_psum")
        gains_ready = sem("gains_ready")
        pos_landed = sem("positions_landed")
        small_landed = sem("mixer_constants_landed")
        tokens_landed = sem("shifted_tokens_landed")
        out_landed = sem("out_landed")
        xt_psum = sem("x_transposed_in_psum")
        x_new = sem("residual_ready")
        g_hi = sem("xg_hi_ready")
        g_lo = sem("xg_lo_ready")
        sq_ready = sem("square_ready")
        acc_done = sem("square_added")
        col_psum = sem("mean_square_in_psum")
        var_ready = sem("variance_ready")
        std_ready = sem("std_ready")
        diag_ready = sem("rstd_diagonal_ready")
        row_psum = sem("rstd_row_in_psum")
        row_ready = sem("rstd_row_ready")
        dve_chain = sem("vector_step")
        rope_args = sem("rope_arguments_ready")
        rope_sines = sem("rope_sines_ready")
        ffn_sems = [{n: sem(f"ffn{i}_{n}") for n in
                     ("unit_done", "gate_scaled", "value_scaled", "silu_ready", "prod_ready", "prod_hi",
                      "prod_lo")} for i in range(2)]
        proj_psum = sem("projection_in_psum")
        proj_read = sem("projection_read")
        swap_psum = sem("rope_swap_in_psum")
        cos_ready = sem("rope_cos_part_ready")
        rope_done = sem("rope_done")
        padded = sem("padding_cleared")
        tok_ready = sem("cmp_tokens_ready")
        hid_psum = sem("cmp_hidden_in_psum")
        hid_ready = sem("cmp_hidden_ready")
        hidt_psum = sem("cmp_hidden_t_in_psum")
        hidt_ready = sem("cmp_hidden_t_ready")
        cmp_psum = sem("cmp_kv_in_psum")
        cmp_ready = sem("cmp_kv_ready")
        gate_ready = sem("gates_ready")
        gatet_psum = sem("gates_t_in_psum")
        gatet_ready = sem("gates_t_ready")
        scores_psum = sem("scores_in_psum")
        bias_ready = sem("minus_max_ready")
        exp_ready = sem("exp_ready")
        factor_ready = sem("factor_ready")
        scaled_ready = sem("probs_scaled")
        trans_psum = sem("probs_t_in_psum")
        near_psum = sem("near_probs_t_in_psum")
        pt_near = sem("near_probs_t_copied")
        pt_act = sem("probs_t_copied_by_scalar")
        pt_dve = sem("probs_t_copied_by_vector")
        pv_psum = sem("pv_in_psum")
        y_read = sem("y_read")
        y_hi_ready = sem("y_hi_ready")
        y_lo_ready = sem("y_lo_ready")
        gm_psum = sem("merge_gate_in_psum")
        br_psum = sem("branches_in_psum")
        gm_scaled = sem("merge_gate_scaled")
        sig_ready = sem("merge_gate_ready")
        merge_read = sem("merge_banks_read")
        merged_ready = sem("merged_ready")
        m_hi = sem("merged_hi_ready")
        m_lo = sem("merged_lo_ready")
        wo_psum = sem("w_out_in_psum")
        z_ready = sem("final_gained")
        fin_psum = sem("final_in_psum")
        fin_act = sem("final_by_scalar")
        fin_dve = sem("final_by_vector")

        ITEMS = []
        for hh in range(HPG):
            for g in range(2):
                ITEMS.append(("cmp", hh, g))
                ITEMS += [("nsa", hh, g, qt) for qt in range(TT)]
        N_NSA = len(ITEMS)
        for hp in range(2):
            for hl in range(2):
                ITEMS += [("dil", hp, hl, qt) for qt in range(TT)]
        per_pair = {"nsa": 10, "dil": 8}

        def ends_pair(n):
            if n < N_NSA:
                return n // 10 if n % 10 == 9 else None
            return 4 + (n - N_NSA) // 8 if (n - N_NSA) % 8 == 7 else None

        Q_ROPE, Q_RAW, KS, KW = 0, 4, 8, 9
        QD = [10, 0]
        KDS = [13, 3]

        CH = [("t", U_CTOK, 0, "tok0"), ("t", U_CTOK, 1, "tok1"), ("t", U_K, 0, "ks"), ("t", U_K, 1, "kw"),
              ("t", U_GATE, 0, "gate")]
        CH += [("n", U_V, tt, "v") for tt in range(TT)]
        CH += [("t", U_Q[u], i, f"q{2 * u + i}") for u in range(2) for i in range(2)]
        N_CH1 = len(CH)
        CH += [("n", U_VD[g], tt, f"vd{g}") for g in range(3) for tt in range(TT)]
        CH += [("t", U_QK[0][g], i, f"{'qk'[i]}d0{g}") for g in range(3) for i in range(2)]
        N_CH2 = len(CH)
        CH += [("t", U_QK[1][g], i, f"{'qk'[i]}d1{g}") for g in range(3) for i in range(2)]
        slot_of = {"tok0": 10, "tok1": 11, "ks": KS, "kw": KW}
        slot_of |= {f"q{i}": Q_RAW + i for i in range(4)}
        slot_of |= {f"{'qk'[i]}d{hp}{g}": (QD, KDS)[i][hp] + g for i in range(2) for hp in range(2) for g in range(3)}
        roped_slot = {n: (Q_ROPE + int(n[1]) if n[0] == "q" and len(n) == 2 else s)
                      for n, s in slot_of.items() if not n.startswith("tok")}
        ROPED = [c for c, ch in enumerate(CH) if ch[3] in roped_slot]
        last_chunk = {}
        for c, ch in enumerate(CH):
            last_chunk[ch[1]] = c

        def final_view(tt):
            return w_raw[:, tt // 2, (tt % 2) * D:(tt % 2) * D + D]

        def tile_of(t, m):
            return t[:, bass.ds(m, 1), :].rearrange("p a t -> p (a t)")

        def before_in_slot(j):
            return [i for i in range(j) if i not in UNSPLIT][-2]

        def release(j):
            if j < MIX0:
                return ffn_sems[0]["unit_done"], j + 1
            if j >= FFN2:
                return ffn_sems[1]["unit_done"], j - FFN2 + 1
            u = j - MIX0
            if u in last_chunk:
                return proj_psum, last_chunk[u] + 1
            for m, unit in U_GM.items():
                if u == unit:
                    return gm_psum, m + 1
            for m2, unit in U_BR.items():
                if u == unit:
                    return br_psum, 2 * m2 + 2
            return wo_psum, 2 * U_WO.index(u) + 2

        def width_of(j):
            if MIX0 <= j < FFN2:
                return MU[j - MIX0][0]
            return SLOT if j - (FFN2 if j >= FFN2 else 0) < FT else HALF * P

        def merge_units_before(m):
            return [U_GM[m], U_BR[m // 2]] if m % 2 == 0 else [U_GM[m]]

        STEPS = [("proj", U_CTOK), ("rstd",), ("proj", U_K), ("row",), ("proj", U_GATE), ("proj", U_V), ("gates",),
                 ("proj", U_Q[0]), ("proj", U_Q[1]), ("tokens",), ("hidden",),
                 ("proj", U_VD[0]), ("hidden_t",), ("proj", U_VD[1]), ("cmp_kv",), ("proj", U_VD[2])]
        STEPS += [("proj", U_QK[0][g]) for g in range(3)]
        STEPS += [("rope_rest", N_CH2), ("attend", 0, N_NSA)]
        STEPS += [("proj", U_QK[1][g]) for g in range(3)]
        STEPS += [("rope_rest", len(CH)), ("attend", N_NSA, len(ITEMS))]

        def merge_banks(m):
            return (2, 0) if m % 2 == 0 else (6, 4)

        block = outer.enter_context(nc.Block())

        def load(sp, j, s, pieces):
            for piece in pieces:
                (at, k, c), src = piece[0], piece[1]
                p0 = piece[2] if len(piece) > 2 else 0
                rows = src.shape[0]
                dst = w_raw[p0:p0 + rows, s, at:at + k * c].rearrange("p (k c) -> p k c", k=k)
                if len(piece) > 3:
                    dst = dst[:, :, piece[3] * DH:piece[3] * DH + DH]
                sp.dma_start(dst, src).then_inc(landed[s], 16)

        def sync_ffn(sp, base, wi, wd):
            wi, wd = ktiles(wi[0]), ktiles(wd[0])
            k0 = split_no(base)

            def up(i, s, wait):
                f = 2 * i + s
                if wait:
                    sp.wait_ge(lo_ready, k0 + f - 1)
                load(sp, None, (base + s) % 2,
                     [((0, KD, P), wi[:, :, bass.ds(f * P, P)]), ((KD * P, KD, P), wi[:, :, bass.ds(f * P + FF, P)])])

            for s in range(2):
                up(0, s, base > 0)
            with sp.Fori(1, FT // 2) as i:
                for s in range(2):
                    up(i, s, True)
            with sp.Fori(0, KD) as m:
                for s in range(2):
                    sp.wait_ge(lo_ready, k0 + FT + 2 * m + s - 1)
                    load(sp, None, (base + s) % 2,
                         [((0, 6, P), wd[:, s * HALF:s * HALF + 6, bass.ds(m * P, P)]),
                          ((6 * P, 5, P), wd[:, s * HALF + 6:(s + 1) * HALF, bass.ds(m * P, P)])])

        @block.sync
        def _(sp):
            sp.dma_start(const[:, :], consts).then_inc(const_landed, 16)
            sp.dma_start(square[:, 0, :].bitcast(I32), positions.broadcast_to([P, T])).then_inc(pos_landed, 16)
            xv = x[0].rearrange("(t p) d -> p t d", p=P)
            for tt in range(TT):
                sp.dma_start(x_nat[:, tt, :], xv[:, tt, :]).then_inc(x_landed, 16)
            sync_ffn(sp, 0, ffn1_w_in, ffn1_w_out)
            for u, (_, pieces, _) in enumerate(MU):
                j = MIX0 + u
                if j - 2 in UNSPLIT:
                    sp.wait_ge(cmp_w1_used, UNSPLIT.index(j - 2) + 1)
                else:
                    sp.wait_ge(lo_ready, split_no(j - 2) + 1)
                load(sp, j, j % 2, pieces)
                if u == U_Q[0]:
                    sp.wait_ge(proj_read, 2)
                    for kv in range(2):
                        for par in range(2):
                            for g in range(2):
                                sp.dma_start(pool[par * DH:par * DH + DH, 12 + 2 * kv + g, 0:T - par],
                                             pool[g * DH:g * DH + DH, 10 + kv, par:T]).then_inc(tokens_landed, 16)
            sync_ffn(sp, FFN2, ffn2_w_in, ffn2_w_out)
            ov = out[0].rearrange("(t p) d -> p t d", p=P)
            for tt in range(TT):
                sp.wait_ge(fin_act, tt + 1)
                sp.wait_ge(fin_dve, tt + 1)
                sp.dma_start(ov[:, tt, :], final_view(tt)).then_inc(out_landed, 16)
            sp.wait_ge(out_landed, 16 * TT)

        def pool_squares(pe, n):
            for m in range(KD):
                v = KD * n + m
                pe.wait_ge(sq_ready, v + 1)
                if m == 0:
                    if n:
                        pe.wait_ge(col_psum, n)
                    nc.gpsimd.tensor_copy(sumsq[:, :], square[:, m % 2, :]).then_inc(acc_done, 1)
                else:
                    pe.wait_ge(acc_done, v)
                    nc.gpsimd.tensor_tensor(sumsq[:, :], sumsq[:, :], square[:, m % 2, :], ALU.add).then_inc(acc_done, 1)

        def pool_rope(pe, c):
            r = ROPED.index(c)
            name = CH[c][3]
            pe.wait_ge(proj_read, c + 1)
            if r:
                pe.wait_ge(rope_done, r)
            nc.gpsimd.tensor_tensor(tmp_b[:, :], pool[:, slot_of[name], :], cos_t[:, :], ALU.mult).then_inc(cos_ready, 1)

        def pool_scale(pe, n):
            it, e = ITEMS[n], n % 2
            pe.wait_ge(factor_ready, n + 1)
            if it[0] == "cmp":
                v = probs[:, e, 0:P].rearrange("p (q n) -> p q n", q=TT)
                f = stat[:, e, 3, 0:4].unsqueeze(2).broadcast_to([P, TT, NC])
                nc.gpsimd.tensor_tensor(v, v, f, ALU.mult).then_inc(scaled_ready, 1)
            elif it[0] == "nsa":
                nk = (it[3] + 1) * P
                nc.gpsimd.tensor_scalar(probs[:, e, 0:nk], probs[:, e, 0:nk], stat[:, e, 3, 0:1], None, ALU.mult)
                nc.gpsimd.tensor_scalar(probs[:, e, T:T + nk], probs[:, e, T:T + nk], stat[:, e, 3, 1:2], None,
                                        ALU.mult).then_inc(scaled_ready, 1)
            else:
                nk, n0 = (it[3] + 1) * P, min(it[3] + 1, 2) * P
                v = probs[:, e, 0:2 * T].rearrange("p (b k) -> p b k", b=2)[:, :, 0:nk]
                nc.gpsimd.tensor_scalar(v, v, stat[:, e, 3, 0:1], None, ALU.mult)
                nc.gpsimd.tensor_scalar(probs[:, e, 2 * T:2 * T + n0], probs[:, e, 2 * T:2 * T + n0],
                                        stat[:, e, 3, 0:1], None, ALU.mult).then_inc(scaled_ready, 1)

        @block.gpsimd
        def _(pl):
            gv = [norm_ffn1[0], norm_mix[0], norm_ffn2[0], norm_final]
            for i, g in enumerate(gv):
                pl.dma_start(vec_rows[i * KD:i * KD + KD, :], g.rearrange("(m p) -> m p", p=P)).then_inc(vec_landed, 16)
            pl.dma_start(vec_rows[32:64, :], cmp_pos[0].rearrange("v (j r) d -> (v j) (r d)", r=2)).then_inc(vec_landed, 16)
            pool_squares(pl, 0)
            pool_squares(pl, 1)
            pl.wait_ge(ffn_sems[0]["unit_done"], FU)
            pl.dma_start(mask[:, :], masks).then_inc(small_landed, 16)
            pl.dma_start(w2[:, :, :], cmp_w2[0].rearrange("v h d -> h v d")).then_inc(small_landed, 16)
            nc.gpsimd.memset(k_cmp[:, :], 0.0)
            nc.gpsimd.memset(probs_t[:, :, :], 0.0).then_inc(padded, 1)
            for c in range(N_CH2):
                if c in ROPED:
                    pool_rope(pl, c)
            for n in range(N_NSA):
                pool_scale(pl, n)
            for c in range(N_CH2, len(CH)):
                pool_rope(pl, c)
            for n in range(N_NSA, len(ITEMS)):
                pool_scale(pl, n)
            pool_squares(pl, 2)
            pool_squares(pl, 3)

        def act_split(act, j, it=0):
            s, k = j % 2, split_no(j)
            if j in UNSPLIT or j >= N_UNITS:
                return
            act.wait_ge(landed[s], landed_at[j] + 32 * it)
            if k >= 2:
                done, value = release(before_in_slot(j))
                act.wait_ge(done, value + 2 * it)
            w = width_of(j)
            nc.scalar.activation(w_hi[:, s, 0:w], w_raw[:, s, 0:w], ACT.Copy).then_inc(hi_ready, 1)

        def act_gain(act, n, m0, it=0):
            m, v = m0 + it, KD * n + m0 + it
            act.wait_ge(x_new, v + 1)
            if KD * n + m0 >= 2:
                act.wait_ge(acc_done, v - 1)
            if n < 3:
                nc.scalar.activation(tile_of(xg_hi, m), tile_of(xT, m), ACT.Copy,
                                     scale=gains[:, n, bass.ds(m, 1)]).then_inc(g_hi, 1)
            nc.scalar.activation(square[:, m0 % 2, :], tile_of(xT, m), ACT.Square).then_inc(sq_ready, 1)
            if n == 3:
                nc.scalar.activation(tile_of(xT, m), tile_of(xT, m), ACT.Copy,
                                     scale=gains[:, n, bass.ds(m, 1)]).then_inc(z_ready, 1)

        def act_std(act, n):
            act.wait_ge(var_ready, n + 1)
            nc.scalar.activation(norm_s[:, 1, :], norm_s[:, 0, :], ACT.Sqrt).then_inc(std_ready, 1)

        def act_ffn(act, i, base, norm):
            S = ffn_sems[i]

            def evac(f):
                act.wait_ge(S["gate_scaled"], f + 1)
                nc.scalar.activation(tmp_a[:, :], tmp_a[:, :], ACT.Silu).then_inc(S["silu_ready"], 1)
                act.wait_ge(S["prod_ready"], f + 1)
                nc.scalar.activation(tile_of(p_hi, f), tmp_b[:, :], ACT.Copy).then_inc(S["prod_hi"], 1)

            act_split(act, base + 2)
            act_std(act, norm)
            act_split(act, base + 3)
            evac(0)
            evac(1)
            with act.Fori(1, FT // 2 - 1) as it:
                for s in range(2):
                    act_split(act, base + s + 2, it)
                    evac(2 * it + s)
            for s in range(2):
                act_split(act, base + FT + s)
                evac(FT - 2 + s)
            with act.Fori(0, KD // 2 - 1) as it:
                for ml in range(2):
                    act_split(act, base + FT + 2 * ml + 2, 2 * it)
                    act_split(act, base + FT + 2 * ml + 3, 2 * it)
                    act_gain(act, norm + 1, ml, 2 * it)
            for ml in range(2):
                for h in range(2):
                    act_split(act, base + FU - 2 + 2 * ml + h)
                act_gain(act, norm + 1, KD - 2 + ml)

        def act_exp(act, n):
            it, e, b = ITEMS[n], n % 2, 2 * (n % 2)
            act.wait_ge(bias_ready, n + 1)
            if n >= 2:
                act.wait_ge(trans_psum, n - 1)
            if n >= N_NSA + 2:
                act.wait_ge(near_psum, n - N_NSA - 1)
            if it[0] == "cmp":
                nc.scalar.activation(probs[:, e, 0:P], probs[:, e, 0:P], ACT.Exp, scale=SCALE).then_inc(exp_ready, 1)
                return
            nk = (it[3] + 1) * P
            own = it[0] == "nsa"
            for i in range(2):
                last = nc.scalar.activation(probs[:, e, i * T:i * T + nk], ps[:, b + i, 0:nk], ACT.Exp,
                                            bias=stat[:, e, 1, (i if own else 0):(i if own else 0) + 1],
                                            scale=SCALE, accum_out=stat[:, e, 2, i:i + 1])
            if not own:
                n0 = min(it[3] + 1, 2) * P
                last = nc.scalar.activation(probs[:, e, 2 * T:2 * T + n0], ps[:, 7, 0:n0], ACT.Exp,
                                            bias=stat[:, e, 1, 0:1], scale=SCALE, accum_out=stat[:, e, 2, 2:3])
            last.then_inc(exp_ready, 1)

        def act_copy_probs(act, n):
            it, e = ITEMS[n], n % 2
            act.wait_ge(trans_psum, n + 1)
            if n >= 2:
                act.wait_ge(pv_psum, n - 1)
            if it[0] == "cmp":
                nc.scalar.activation(probs_t[0:NC, e, 0:256], ps[0:NC, 4, 0:256], ACT.Copy).then_inc(pt_act, 1)
            else:
                nk = (it[3] + 1) * P
                nc.scalar.activation(probs_t[:, e, 0:nk], ps[:, 4, 0:nk], ACT.Copy).then_inc(pt_act, 1)

        def act_copy_near(act, n):
            if n < N_NSA:
                return
            it, e = ITEMS[n], n % 2
            n0 = min(it[3] + 1, 2) * P
            act.wait_ge(near_psum, n - N_NSA + 1)
            nc.scalar.activation(probs_t[:, e, 2 * T:2 * T + n0], ps[:, 4, 0:n0], ACT.Copy).then_inc(pt_near, 1)

        def act_y(act, n):
            act.wait_ge(pv_psum, n + 1)
            nc.scalar.activation(y[:, ends_pair(n), :], ps[:, 6, :], ACT.Copy).then_inc(y_read, 1)

        def act_attend(act, a, b):
            act_exp(act, a)
            for n in range(a, b):
                if n + 1 < b:
                    act_exp(act, n + 1)
                act_copy_probs(act, n)
                act_copy_near(act, n)
                if n > a and ends_pair(n - 1) is not None:
                    act_y(act, n - 1)
            act_y(act, b - 1)

        @block.scalar
        def _(act):
            act.wait_ge(rope_args, 1)
            nc.scalar.activation(sin_t[:, :], sin_t[:, :], ACT.Sin, scale=0.5).then_inc(rope_sines, 1)
            nc.scalar.activation(cos_t[:, :], cos_t[:, :], ACT.Sin).then_inc(rope_sines, 1)
            act.wait_ge(gains_ready, 1)
            act_split(act, 0)
            act_split(act, 1)
            for m in range(KD):
                act_gain(act, 0, m)
            act_ffn(act, 0, 0, 0)
            for step in STEPS:
                if step[0] == "proj":
                    act_split(act, MIX0 + step[1] + 2)
                elif step[0] == "rstd":
                    act_std(act, 1)
                elif step[0] == "gates":
                    act.wait_ge(proj_read, 5)
                    nc.scalar.activation(probs[0:24, 0, 0:T], probs[0:24, 0, 0:T], ACT.Sigmoid).then_inc(gate_ready, 1)
                elif step[0] == "hidden":
                    for kv in range(2):
                        act.wait_ge(cmp_w1_used, 2)
                        nc.scalar.activation(hid[:, kv, :], ps[0:DH, 7, kv * P:kv * P + P],
                                             ACT.Silu).then_inc(hid_ready, 1)
                    for kv in range(2):
                        act_split(act, MIX0 + U_W1[kv] + 2)
                elif step[0] == "attend":
                    act_attend(act, step[1], step[2])
            for c in range(6):
                nc.scalar.activation(y_hi[:, c, :], y[:, c, :], ACT.Copy).then_inc(y_hi_ready, 1) if c else (
                    act.wait_ge(y_read, 6),
                    nc.scalar.activation(y_hi[:, c, :], y[:, c, :], ACT.Copy).then_inc(y_hi_ready, 1))
            for m in range(KD):
                for u in merge_units_before(m):
                    act_split(act, MIX0 + u + 2)
                act.wait_ge(gm_scaled, m + 1)
                nc.scalar.activation(tmp_a[:, :], tmp_a[:, :], ACT.Sigmoid)
                nc.scalar.activation(tmp_b[:, :], tmp_b[:, :], ACT.Sigmoid).then_inc(sig_ready, 1)
                act.wait_ge(merged_ready, m + 1)
                nc.scalar.activation(merged_hi[:, m, :], tmp_a[:, :], ACT.Copy).then_inc(m_hi, 1)
            for m in range(KD):
                if m % 2 == 0:
                    act_split(act, MIX0 + U_WO[m // 2] + 2)
                act_gain(act, 2, m)
            act_ffn(act, 1, FFN2, 2)
            for tt in range(TT):
                if tt == 0:
                    act_std(act, 3)
                act.wait_ge(fin_psum, tt + 1)
                act.wait_ge(row_ready, 4)
                nc.scalar.activation(final_view(tt)[:, 0:T], ps[:, 2 * tt, :], ACT.Copy,
                                     scale=rstd_col[:, tt:tt + 1]).then_inc(fin_act, 1)

        chain = [0]

        def link(dve, ins):
            chain[0] += 1
            ins.then_inc(dve_chain, 1)
            dve.wait_ge(dve_chain, chain[0])

        V = nc.vector

        def dve_split(dve, j, it=0):
            s, k = j % 2, split_no(j)
            if j in UNSPLIT or j >= N_UNITS:
                return
            w = width_of(j)
            dve.wait_ge(hi_ready, k + 1 + 2 * it)
            V.tensor_tensor(w_lo[:, s, 0:w], w_raw[:, s, 0:w], w_hi[:, s, 0:w].bitcast(F32),
                            ALU.subtract).then_inc(lo_ready, 1)

        def dve_gain(dve, n, m0, it=0):
            m, v = m0 + it, KD * n + m0 + it
            if n < 3:
                dve.wait_ge(g_hi, v + 1)
                V.scalar_tensor_tensor(out=tile_of(xg_lo, m), in0=tile_of(xT, m), scalar=gains[:, n, bass.ds(m, 1)],
                                       in1=tile_of(xg_hi, m).bitcast(F32), op0=ALU.mult,
                                       op1=ALU.subtract).then_inc(g_lo, 1)

        def dve_rstd(dve, n):
            dve.wait_ge(col_psum, n + 1)
            V.tensor_scalar(norm_s[:, 0, :], ps[:, 7, 0:2 * TT].rearrange("p (t two) -> p t two", two=2)[:, :, 0],
                            1.0 / D, EPS, ALU.mult, ALU.add).then_inc(var_ready, 1)
            dve.wait_ge(std_ready, n + 1)
            link(dve, V.reciprocal(norm_s[:, 2, :], norm_s[:, 1, :]))
            link(dve, V.tensor_tensor(norm_s[:, 3, :], norm_s[:, 2, :], norm_s[:, 2, :], ALU.mult))
            link(dve, V.tensor_tensor(norm_s[:, 3, :], norm_s[:, 3, :], norm_s[:, 0, :], ALU.mult))
            link(dve, V.tensor_scalar(norm_s[:, 3, :], norm_s[:, 3, :], -0.5, 1.5, ALU.mult, ALU.add))
            if n == 3:
                V.tensor_tensor(rstd_col[:, :], norm_s[:, 2, :], norm_s[:, 3, :], ALU.mult).then_inc(row_ready, 1)
                return
            link(dve, V.tensor_tensor(rstd_col[:, :], norm_s[:, 2, :], norm_s[:, 3, :], ALU.mult))
            for tt in range(TT):
                last = V.tensor_scalar(tmp_a[:, tt * P:tt * P + P], ident, rstd_col[:, tt:tt + 1], None, ALU.mult)
            last.then_inc(diag_ready, 1)

        def dve_row(dve, n):
            dve.wait_ge(row_psum, n + 1)
            V.tensor_copy(rstd_row[:, :], ps[:, 6, :]).then_inc(row_ready, 1)
            dve.wait_ge(row_ready, n + 1)

        def dve_ffn(dve, i, base, norm):
            S = ffn_sems[i]

            def evac(f, s):
                dve.wait_ge(S["unit_done"], f + 1)
                V.tensor_tensor(tmp_a[:, :], ps[:, 2 * s, :], rstd_row[:, :], ALU.mult).then_inc(S["gate_scaled"], 1)
                if not (isinstance(f, int) and f == 0):
                    dve.wait_ge(S["prod_lo"], f)
                V.tensor_tensor(tmp_b[:, :], ps[:, 2 * s + 1, :], rstd_row[:, :], ALU.mult).then_inc(S["value_scaled"], 1)
                dve.wait_ge(S["silu_ready"], f + 1)
                dve.wait_ge(S["value_scaled"], f + 1)
                V.tensor_tensor(tmp_b[:, :], tmp_a[:, :], tmp_b[:, :], ALU.mult).then_inc(S["prod_ready"], 1)
                dve.wait_ge(S["prod_hi"], f + 1)
                V.tensor_tensor(tile_of(p_lo, f), tmp_b[:, :], tile_of(p_hi, f).bitcast(F32),
                                ALU.subtract).then_inc(S["prod_lo"], 1)

            def residual(m0, it=0):
                v = KD * (norm + 1) + m0 + it
                dve.wait_ge(S["unit_done"], FT + 2 * (m0 + it + 1))
                V.scalar_tensor_tensor(out=tile_of(xT, m0 + it), in0=ps[:, 4 + m0 % 2, :], scalar=0.5,
                                       in1=tile_of(xT, m0 + it), op0=ALU.mult, op1=ALU.add).then_inc(x_new, 1)
                dve_gain(dve, norm + 1, m0, it)

            dve_split(dve, base + 2)
            dve_rstd(dve, norm)
            dve_split(dve, base + 3)
            dve_row(dve, norm)
            evac(0, 0)
            evac(1, 1)
            with dve.Fori(1, FT // 2 - 1) as it:
                for s in range(2):
                    dve_split(dve, base + s + 2, it)
                    evac(2 * it + s, s)
            for s in range(2):
                dve_split(dve, base + FT + s)
                evac(FT - 2 + s, s)
            with dve.Fori(0, KD // 2 - 1) as it:
                for ml in range(2):
                    dve_split(dve, base + FT + 2 * ml + 2, 2 * it)
                    dve_split(dve, base + FT + 2 * ml + 3, 2 * it)
                    residual(ml, 2 * it)
            for ml in range(2):
                for h in range(2):
                    dve_split(dve, base + FU - 2 + 2 * ml + h)
                residual(KD - 2 + ml)

        def dve_chunk(dve, c):
            kind, _, i, name = CH[c]
            dve.wait_ge(proj_psum, c + 1)
            b = c % 4
            if kind == "n":
                dst = v_nsa[:, i, :, :].rearrange("p a c -> p (a c)") if name == "v" else v_dil[:, i, int(name[2]), :]
                V.tensor_scalar(dst, ps[:, b, 0:256], rstd_col[:, i:i + 1], None, ALU.mult).then_inc(proj_read, 1)
            elif name == "gate":
                V.tensor_tensor(probs[0:24, 0, 0:T], ps[0:24, b, :], rstd_row[0:24, :], ALU.mult).then_inc(proj_read, 1)
            else:
                V.tensor_tensor(pool[:, slot_of[name], :], ps[:, b, :], rstd_row[:, :], ALU.mult).then_inc(proj_read, 1)

        def dve_rope(dve, c):
            r = ROPED.index(c)
            dve.wait_ge(swap_psum, r + 1)
            if r:
                dve.wait_ge(rope_done, r)
            link(dve, V.tensor_tensor(tmp_a[:, :], ps[:, 4 + r % 2, :], sin_t[:, :], ALU.mult))
            dve.wait_ge(cos_ready, r + 1)
            V.tensor_tensor(pool[:, roped_slot[CH[c][3]], :], tmp_a[:, :], tmp_b[:, :], ALU.add).then_inc(rope_done, 1)

        def dve_prepare(dve, n):
            it, e, b = ITEMS[n], n % 2, 2 * (n % 2)
            dve.wait_ge(scores_psum, n + 1)
            if it[0] == "cmp":
                sc = ps[:, b, :].rearrange("p (q k) -> p q k", q=TT)[:, :, 0:NC]
                link(dve, V.tensor_reduce(stat[:, e, 0, 0:4], sc, AX.X, ALU.max))
                link(dve, V.tensor_scalar(stat[:, e, 0, 0:4], stat[:, e, 0, 0:4], -1e28, None, ALU.max))
                if n >= 2:
                    dve.wait_ge(trans_psum, n - 1)
                V.tensor_tensor(probs[:, e, 0:P].rearrange("p (q n) -> p q n", q=TT), sc,
                                stat[:, e, 0, 0:4].unsqueeze(2).broadcast_to([P, TT, NC]),
                                ALU.subtract).then_inc(bias_ready, 1)
                return
            nk = (it[3] + 1) * P
            link(dve, V.tensor_reduce(stat[:, e, 0, 0:2], ps[:, b:b + 2, 0:nk], AX.X, ALU.max))
            if it[0] == "nsa":
                V.tensor_scalar(stat[:, e, 1, 0:2], stat[:, e, 0, 0:2], -SCALE, None, ALU.mult).then_inc(bias_ready, 1)
            else:
                n0 = min(it[3] + 1, 2) * P
                link(dve, V.tensor_reduce(stat[:, e, 0, 2:3], ps[:, 7, 0:n0], AX.X, ALU.max))
                link(dve, V.tensor_reduce(stat[:, e, 0, 3:4], stat[:, e, 0, 0:3], AX.X, ALU.max))
                V.tensor_scalar(stat[:, e, 1, 0:1], stat[:, e, 0, 3:4], -SCALE, None, ALU.mult).then_inc(bias_ready, 1)

        def dve_factor(dve, n):
            it, e = ITEMS[n], n % 2
            dve.wait_ge(exp_ready, n + 1)
            if n >= 2:
                dve.wait_ge(scaled_ready, n - 1)
            if it[0] == "cmp":
                h = it[2] * HPG + it[1]
                link(dve, V.tensor_reduce(stat[:, e, 2, 0:4], probs[:, e, 0:P].rearrange("p (q n) -> p q n", q=TT),
                                          AX.X, ALU.add))
                link(dve, V.tensor_scalar(stat[:, e, 2, 0:4], stat[:, e, 2, 0:4], 0.5, None, ALU.max))
                link(dve, V.reciprocal(stat[:, e, 0, 0:4], stat[:, e, 2, 0:4]))
                V.tensor_tensor(stat[:, e, 3, 0:4], stat[:, e, 0, 0:4], gates[:, :, 3 * h], ALU.mult).then_inc(factor_ready, 1)
            elif it[0] == "nsa":
                h = it[2] * HPG + it[1]
                link(dve, V.reciprocal(stat[:, e, 0, 0:2], stat[:, e, 2, 0:2]))
                V.tensor_tensor(stat[:, e, 3, 0:2], stat[:, e, 0, 0:2], gates[:, it[3], 3 * h + 1:3 * h + 3],
                                ALU.mult).then_inc(factor_ready, 1)
            else:
                link(dve, V.tensor_reduce(stat[:, e, 2, 3:4], stat[:, e, 2, 0:3], AX.X, ALU.add))
                V.reciprocal(stat[:, e, 3, 0:1], stat[:, e, 2, 3:4]).then_inc(factor_ready, 1)

        def dve_copy_probs(dve, n):
            it, e = ITEMS[n], n % 2
            dve.wait_ge(trans_psum, n + 1)
            if n >= 2:
                dve.wait_ge(pv_psum, n - 1)
            if it[0] == "cmp":
                V.tensor_copy(probs_t[0:NC, e, 256:T], ps[0:NC, 5, 256:T]).then_inc(pt_dve, 1)
                return
            nk = (it[3] + 1) * P
            V.tensor_copy(probs_t[:, e, T:T + nk], ps[:, 5, 0:nk]).then_inc(pt_dve, 1)

        def dve_attend(dve, a, b):
            dve_prepare(dve, a)
            dve_factor(dve, a)
            for n in range(a, b):
                if n + 1 < b:
                    dve_prepare(dve, n + 1)
                dve_copy_probs(dve, n)
                if n + 1 < b:
                    dve_factor(dve, n + 1)

        @block.vector
        def _(dve):
            dve.wait_ge(const_landed, 16)
            dve.wait_ge(pos_landed, 16)
            link(dve, V.tensor_copy(cos_t[:, :], square[:, 0, :].bitcast(I32)))
            link(dve, V.tensor_scalar(sin_t[:, :], cos_t[:, :], freq, None, ALU.mult))
            link(dve, V.tensor_scalar(tmp_a[:, :], sin_t[:, :], float(1 / (2 * np.pi)), MAGIC, ALU.mult, ALU.add))
            link(dve, V.tensor_scalar(tmp_a[:, :], tmp_a[:, :], MAGIC, None, ALU.subtract))
            for part in TWO_PI:
                link(dve, V.scalar_tensor_tensor(out=sin_t[:, :], in0=tmp_a[:, :], scalar=-part, in1=sin_t[:, :],
                                                 op0=ALU.mult, op1=ALU.add))
            link(dve, V.scalar_tensor_tensor(out=tmp_a[:, :], in0=sin_t[:, :], scalar=-1.0, in1=sin_t[:, :],
                                             op0=ALU.mult, op1=ALU.max))
            V.tensor_scalar(cos_t[:, :], tmp_a[:, :], -0.5, float(np.pi / 2), ALU.mult, ALU.add).then_inc(rope_args, 1)
            dve.wait_ge(rope_sines, 2)
            link(dve, V.scalar_tensor_tensor(out=tmp_a[:, :], in0=sin_t[:, :], scalar=2.0, in1=cos_t[:, :],
                                             op0=ALU.mult, op1=ALU.mult))
            link(dve, V.tensor_tensor(cos_t[:, :], sin_t[:, :], sin_t[:, :], ALU.mult))
            link(dve, V.tensor_scalar(cos_t[:, :], cos_t[:, :], -2.0, 1.0, ALU.mult, ALU.add))
            link(dve, V.tensor_copy(sin_t[:, :], tmp_a[:, :]))
            dve.wait_ge(gains_psum, 1)
            V.tensor_copy(vec_cols[:, :], ps[:, 7, 0:64]).then_inc(gains_ready, 1)
            dve.wait_ge(gains_ready, 1)
            dve_split(dve, 0)
            dve_split(dve, 1)
            for m in range(KD):
                dve.wait_ge(xt_psum, m + 1)
                V.tensor_copy(xT[:, m, :], ps[:, m, :]).then_inc(x_new, 1)
                dve_gain(dve, 0, m)
            dve_ffn(dve, 0, 0, 0)
            rope_pending = []

            def rope_flush(upto):
                while rope_pending and rope_pending[0] < upto:
                    dve_rope(dve, rope_pending.pop(0))

            def chunks_of(u):
                for c in [c for c, ch in enumerate(CH) if ch[1] == u]:
                    dve_chunk(dve, c)
                    rope_flush(c)
                    if c in ROPED:
                        rope_pending.append(c)

            for step in STEPS:
                if step[0] == "proj":
                    u = step[1]
                    if u == U_CTOK:
                        dve_split(dve, MIX0 + 2)
                        dve_rstd(dve, 1)
                    elif u == U_K:
                        dve_split(dve, MIX0 + 3)
                        dve_row(dve, 1)
                        chunks_of(U_CTOK)
                        chunks_of(U_K)
                    else:
                        dve_split(dve, MIX0 + u + 2)
                        chunks_of(u)
                elif step[0] == "gates":
                    dve.wait_ge(gatet_psum, 1)
                    V.tensor_copy(gates[:, :, :].rearrange("p t c -> p (t c)"), ps[:, 6, 0:TT * 24]).then_inc(gatet_ready, 1)
                elif step[0] == "tokens":
                    dve.wait_ge(tokens_landed, 16 * 8)
                    dve.wait_ge(padded, 1)
                    for kv in range(2):
                        for g in range(2):
                            tv = pool[:, 12 + 2 * kv + g, :].rearrange("p (n j two) -> p j n two", n=NC, j=8)
                            av = probs_t[:, kv, 0:2 * 512].rearrange("p (j g n) -> p j g n", j=16, g=2)
                            for h in range(2):
                                last = V.tensor_tensor(
                                    av[:, 8 * h:8 * h + 8, g, 0:NCMP], tv[:, :, h:h + NCMP, 0],
                                    pos_t[:, kv, 8 * h:8 * h + 8].unsqueeze(2).broadcast_to([P, 8, NCMP]), ALU.add)
                    last.then_inc(tok_ready, 1)
                elif step[0] == "hidden":
                    for kv in range(2):
                        dve_split(dve, MIX0 + U_W1[kv] + 2)
                elif step[0] == "hidden_t":
                    dve.wait_ge(hidt_psum, 1)
                    V.tensor_copy(hid_t[:, :, :].rearrange("p a c -> p (a c)"), ps[:, 7, 256:384]).then_inc(hidt_ready, 1)
                elif step[0] == "cmp_kv":
                    dve.wait_ge(cmp_psum, 1)
                    V.tensor_copy(k_cmp[:, 0:NC], ps[:, 7, 384:384 + NC])
                    V.tensor_copy(v_cmp[:, :, :].rearrange("p a c -> p (a c)"), ps[0:NC, 7, 0:P]).then_inc(cmp_ready, 1)
                elif step[0] == "rope_rest":
                    rope_flush(step[1])
                elif step[0] == "attend":
                    dve_attend(dve, step[1], step[2])
            for c in range(6):
                dve.wait_ge(y_hi_ready, c + 1)
                V.tensor_tensor(y_lo[:, c, :], y[:, c, :], y_hi[:, c, :].bitcast(F32), ALU.subtract).then_inc(y_lo_ready, 1)
            for m in range(KD):
                for u in merge_units_before(m):
                    dve_split(dve, MIX0 + u + 2)
                g0, b0 = merge_banks(m)
                dve.wait_ge(gm_psum, m + 1)
                if m:
                    dve.wait_ge(m_lo, m)
                V.tensor_tensor(tmp_a[:, :], ps[:, g0, :], rstd_row[:, :], ALU.mult)
                V.tensor_tensor(tmp_b[:, :], ps[:, g0 + 1, :], rstd_row[:, :], ALU.mult).then_inc(gm_scaled, 1)
                dve.wait_ge(sig_ready, m + 1)
                dve.wait_ge(br_psum, m + 1)
                V.tensor_tensor(tmp_a[:, :], ps[:, b0, :], tmp_a[:, :], ALU.mult)
                V.tensor_tensor(tmp_b[:, :], ps[:, b0 + 1, :], tmp_b[:, :], ALU.mult).then_inc(merge_read, 1)
                dve.wait_ge(merge_read, m + 1)
                V.tensor_tensor(tmp_a[:, :], tmp_a[:, :], tmp_b[:, :], ALU.add).then_inc(merged_ready, 1)
                dve.wait_ge(m_hi, m + 1)
                V.tensor_tensor(merged_lo[:, m, :], tmp_a[:, :], merged_hi[:, m, :].bitcast(F32),
                                ALU.subtract).then_inc(m_lo, 1)
            for m in range(KD):
                if m % 2 == 0:
                    dve_split(dve, MIX0 + U_WO[m // 2] + 2)
                dve.wait_ge(wo_psum, m + 1)
                V.tensor_tensor(xT[:, m, :], ps[:, 4 + m % 2, :], xT[:, m, :], ALU.add).then_inc(x_new, 1)
                dve_gain(dve, 2, m)
            dve_ffn(dve, 1, FFN2, 2)
            dve_rstd(dve, 3)
            dve.wait_ge(row_ready, 4)
            for tt in range(TT):
                dve.wait_ge(fin_psum, tt + 1)
                V.tensor_scalar(final_view(tt)[:, T:D], ps[:, 2 * tt + 1, :], rstd_col[:, tt:tt + 1], None,
                                ALU.mult).then_inc(fin_dve, 1)

        mm = nc.tensor.matmul

        def three_pass(out, pairs, before=None):
            for i, ((ah, al), (bh, bl)) in enumerate(pairs):
                if before:
                    before(i)
                mm(out, ah, bh, start=(i == 0), stop=False)
                mm(out, ah, bl, start=False, stop=False)
                last = mm(out, al, bh, start=False, stop=(i == len(pairs) - 1))
            return last

        def wtile(s, at, c=P):
            return w_hi[:, s, at:at + c], w_lo[:, s, at:at + c]

        def pe_col(pe, n):
            pe.wait_ge(acc_done, KD * (n + 1))
            for tt in range(TT):
                last = mm(ps[:, 7, 2 * tt:2 * tt + 2], sumsq[:, tt * P:tt * P + P], ones[:, 0:2], start=True, stop=True)
            last.then_inc(col_psum, 1)

        def pe_row(pe, n):
            pe.wait_ge(diag_ready, n + 1)
            for tt in range(TT):
                last = mm(ps[:, 6, tt * P:tt * P + P], ones, tmp_a[:, tt * P:tt * P + P], start=True, stop=True)
            last.then_inc(row_psum, 1)

        def moving(k):
            return xg_hi[:, k, :], xg_lo[:, k, :]

        def pe_ffn(pe, i, base, norm):
            S = ffn_sems[i]
            k0 = split_no(base)

            def up(f, s, first=False):
                sl = (base + s) % 2
                pe.wait_ge(lo_ready, k0 + f + 1)
                if not (isinstance(f, int) and f < 2):
                    pe.wait_ge(S["value_scaled"], f - 1)
                before = (lambda k: pe.wait_ge(g_lo, KD * norm + k + 1)) if first else None
                three_pass(ps[:, 2 * s, :], [(wtile(sl, k * P), moving(k)) for k in range(KD)], before)
                last = three_pass(ps[:, 2 * s + 1, :], [(wtile(sl, (KD + k) * P), moving(k)) for k in range(KD)])
                last.then_inc(S["unit_done"], 1)

            def down(m0, it=0, first=False):
                bank = ps[:, 4 + m0 % 2, :]
                v = KD * (norm + 1) + m0 + it
                if not first:
                    pe.wait_ge(x_new, v - 1)
                for h in range(2):
                    sl = (base + h) % 2
                    pe.wait_ge(lo_ready, k0 + FT + 2 * (m0 + it) + h + 1)
                    if first:
                        pe.wait_ge(S["prod_lo"], (h + 1) * HALF)
                    for t in range(HALF):
                        (ah, al), f = wtile(sl, t * P), h * HALF + t
                        mm(bank, ah, p_hi[:, f, :], start=(f == 0), stop=False)
                        mm(bank, ah, p_lo[:, f, :], start=False, stop=False)
                        last = mm(bank, al, p_hi[:, f, :], start=False, stop=(f == FT - 1))
                    last.then_inc(S["unit_done"], 1)

            up(0, 0, True)
            pe_col(pe, norm)
            up(1, 1)
            pe_row(pe, norm)
            with pe.Fori(1, FT // 2) as it:
                for s in range(2):
                    up(2 * it + s, s)
            down(0, 0, True)
            down(1, 0, True)
            with pe.Fori(1, KD // 2) as it:
                for ml in range(2):
                    down(ml, 2 * it)

        def pe_chunk(pe, c):
            kind, u, i, name = CH[c]
            sl = (MIX0 + u) % 2
            bank = ps[:, c % 4, :]
            if c >= 4:
                pe.wait_ge(proj_read, c - 3)
            if kind == "t":
                before = (lambda k: pe.wait_ge(g_lo, KD + k + 1)) if c == 0 else None
                pairs = [(wtile(sl, (i * KD + k) * P), moving(k)) for k in range(KD)]
                last = three_pass(bank, pairs, before)
            else:
                def wm(t, k):
                    return t[:, sl, :].rearrange("p (i k r) -> p i k r", i=2, k=KD)[:, :, k, :]
                ts = slice(i * P, i * P + P)
                out_ = bank[:, 0:256].rearrange("p (i r) -> p i r", i=2)
                last = three_pass(out_, [((xg_hi[:, k, ts], xg_lo[:, k, ts]), (wm(w_hi, k), wm(w_lo, k)))
                                         for k in range(KD)])
            last.then_inc(proj_psum, 1)

        def pe_swap(pe, c):
            r = ROPED.index(c)
            pe.wait_ge(proj_read, c + 1)
            if r >= 2:
                pe.wait_ge(rope_done, r - 1)
            mm(ps[:, 4 + r % 2, :], swap_perm, pool[:, slot_of[CH[c][3]], :], start=True, stop=True).then_inc(swap_psum, 1)

        def pe_scores(pe, n):
            it, b = ITEMS[n], 2 * (n % 2)
            if n >= 2:
                pe.wait_ge(exp_ready, n - 1)
            if it[0] == "cmp":
                _, hh, g = it
                rows = slice(g * DH, g * DH + DH)
                for qt in range(TT):
                    mm(ps[:, b, qt * P:qt * P + P], pool[rows, Q_RAW + hh, qt * P:qt * P + P], k_cmp[rows, :],
                       start=True, stop=False)
                    last = mm(ps[:, b, qt * P:qt * P + NC], ident_b, cmp_b[:, qt * NC:qt * NC + NC],
                              start=False, stop=True)
                last.then_inc(scores_psum, 1)
                return
            if it[0] == "nsa":
                _, hh, g, qt = it
                rows, nk = slice(g * DH, g * DH + DH), (qt + 1) * P
                for i, keys in enumerate((KS, KW)):
                    mm(ps[:, b + i, 0:nk], pool[rows, Q_ROPE + hh, qt * P:qt * P + P], pool[rows, keys, 0:nk],
                       start=True, stop=False)
                    last = mm(ps[:, b + i, nk - P:nk], ident_b, causal_b, start=False, stop=True)
                last.then_inc(scores_psum, 1)
                return
            _, hp, hl, qt = it
            rows, nk, k0 = slice(hl * DH, hl * DH + DH), (qt + 1) * P, max(qt - 1, 0) * P
            for i in range(2):
                mm(ps[:, b + i, 0:nk], pool[rows, QD[hp] + 1 + i, qt * P:qt * P + P],
                   pool[rows, KDS[hp] + 1 + i, 0:nk], start=True, stop=False)
                one_hot, other = residue(i)
                mm(ps[:, b + i, 0:nk], one_hot, other[:, 0:nk], start=False, stop=False)
                mm(ps[:, b + i, nk - P:nk], ident_b, causal_b, start=False, stop=True)
            if n > N_NSA:
                pe.wait_ge(exp_ready, n)
            n0 = nk - k0
            mm(ps[:, 7, 0:n0], pool[rows, QD[hp], qt * P:qt * P + P], pool[rows, KDS[hp], k0:nk], start=True, stop=False)
            if qt:
                mm(ps[:, 7, 0:P], ident_b, prev_b, start=False, stop=False)
            mm(ps[:, 7, n0 - P:n0], ident_b, causal_b, start=False, stop=True).then_inc(scores_psum, 1)

        def pe_transpose_probs(pe, n):
            it, e = ITEMS[n], n % 2
            pe.wait_ge(scaled_ready, n + 1)
            if n:
                pe.wait_ge(pt_act, n)
                pe.wait_ge(pt_dve, n)
            if n > N_NSA:
                pe.wait_ge(pt_near, n - N_NSA)
            if it[0] == "cmp":
                for qt in range(TT):
                    last = nc.tensor.transpose(ps[0:NC, 4 + qt // 2, qt * P:qt * P + P],
                                               probs[:, e, qt * NC:qt * NC + NC], ident)
                last.then_inc(trans_psum, 1)
                return
            qt = it[3]
            for i in range(2):
                for kt in range(qt + 1):
                    last = nc.tensor.transpose(ps[:, 4 + i, kt * P:kt * P + P],
                                               probs[:, e, i * T + kt * P:i * T + kt * P + P], ident)
            last.then_inc(trans_psum, 1)

        def pe_transpose_near(pe, n):
            if n < N_NSA:
                return
            it, e = ITEMS[n], n % 2
            pe.wait_ge(pt_act, n + 1)
            for kt in range(min(it[3] + 1, 2)):
                last = nc.tensor.transpose(ps[:, 4, kt * P:kt * P + P],
                                           probs[:, e, 2 * T + kt * P:2 * T + kt * P + P], ident)
            last.then_inc(near_psum, 1)

        def pe_values(pe, n):
            it, e = ITEMS[n], n % 2
            pe.wait_ge(pt_act, n + 1)
            pe.wait_ge(pt_dve, n + 1)
            if n >= N_NSA:
                pe.wait_ge(pt_near, n - N_NSA + 1)
            pair = n // 10 if n < N_NSA else 4 + (n - N_NSA) // 8
            if pair:
                pe.wait_ge(y_read, pair)
            if it[0] == "cmp":
                g = it[2]
                mm(ps[g * DH:g * DH + DH, 6, :], v_cmp[:, g, :], probs_t[0:NC, e, 0:T],
                   start=True, stop=False).then_inc(pv_psum, 1)
                return
            if it[0] == "nsa":
                _, hh, g, qt = it
                out_ = ps[g * DH:g * DH + DH, 6, qt * P:qt * P + P]
                for i in range(2):
                    for kt in range(qt + 1):
                        last = mm(out_, v_nsa[:, kt, i, g * DH:g * DH + DH],
                                  probs_t[:, e, i * T + kt * P:i * T + kt * P + P],
                                  start=False, stop=(i == 1 and kt == qt and qt == TT - 1))
                last.then_inc(pv_psum, 1)
                return
            _, hp, hl, qt = it
            out_ = ps[hl * DH:hl * DH + DH, 6, qt * P:qt * P + P]
            cols = slice(hp * P + hl * DH, hp * P + hl * DH + DH)
            terms = [(1 + i, kt, i * T + kt * P) for i in range(2) for kt in range(qt + 1)]
            terms += [(0, max(qt - 1, 0) + i, 2 * T + i * P) for i in range(min(qt + 1, 2))]
            for j, (g, kt, at) in enumerate(terms):
                last = mm(out_, v_dil[:, kt, g, cols], probs_t[:, e, at:at + P], start=(j == 0), stop=(j == len(terms) - 1))
            last.then_inc(pv_psum, 1)

        def pe_attend(pe, a, b):
            pe_scores(pe, a)
            for n in range(a, b):
                if n + 1 < b:
                    pe_scores(pe, n + 1)
                pe_transpose_probs(pe, n)
                if n > a:
                    pe_values(pe, n - 1)
                pe_transpose_near(pe, n)
            pe_values(pe, b - 1)

        @block.tensor
        def _(pe):
            pe.wait_ge(const_landed, 16)
            pe.wait_ge(vec_landed, 16 * 5)
            nc.tensor.transpose(ps[:, 7, 0:64], vec_rows[:, :], ident[0:64, 0:64]).then_inc(gains_psum, 1)
            pe.wait_ge(x_landed, 16 * TT)
            for m in range(KD):
                if m == KD - 1:
                    pe.wait_ge(gains_ready, 1)
                for tt in range(TT):
                    last = nc.tensor.transpose(ps[:, m, tt * P:tt * P + P], x_nat[:, tt, m * P:m * P + P], ident)
                last.then_inc(xt_psum, 1)
            pe_ffn(pe, 0, 0, 0)
            swaps = []

            def swap_flush(upto):
                while swaps and swaps[0] < upto:
                    pe_swap(pe, swaps.pop(0))

            for step in STEPS:
                if step[0] == "proj":
                    u = step[1]
                    pe.wait_ge(lo_ready, split_no(MIX0 + u) + 1)
                    if u == U_QK[1][0]:
                        pe.wait_ge(exp_ready, N_NSA)
                        pe.wait_ge(pt_act, N_NSA)
                        pe.wait_ge(pt_dve, N_NSA)
                    for c in [c for c, ch in enumerate(CH) if ch[1] == u]:
                        pe_chunk(pe, c)
                        if c >= 4:
                            swap_flush(c)
                        if c in ROPED:
                            swaps.append(c)
                elif step[0] == "rstd":
                    pe_col(pe, 1)
                elif step[0] == "row":
                    pe_row(pe, 1)
                elif step[0] == "gates":
                    pe.wait_ge(gate_ready, 1)
                    pe.wait_ge(row_ready, 2)
                    for tt in range(TT):
                        last = nc.tensor.transpose(ps[:, 6, tt * 24:tt * 24 + 24], probs[0:24, 0, tt * P:tt * P + P],
                                                   ident[0:24, 0:24])
                    last.then_inc(gatet_psum, 1)
                elif step[0] == "hidden":
                    pe.wait_ge(tok_ready, 1)
                    pe.wait_ge(var_ready, 2)
                    for kv in range(2):
                        j = MIX0 + U_W1[kv]
                        pe.wait_ge(landed[j % 2], landed_at[j])
                        for p in range(16):
                            last = mm(ps[0:DH, 7, kv * P:kv * P + P], probs_t[:, kv, p * DH:p * DH + DH],
                                      w_raw[:, j % 2, p * P:p * P + P], start=(p == 0), stop=(p == 15))
                        last.then_inc(cmp_w1_used, 1)
                elif step[0] == "hidden_t":
                    pe.wait_ge(hid_ready, 2)
                    for kv in range(2):
                        last = nc.tensor.transpose(ps[:, 7, 256 + kv * DH:256 + kv * DH + DH], hid[:, kv, :],
                                                   ident[0:DH, 0:DH])
                    last.then_inc(hidt_psum, 1)
                elif step[0] == "cmp_kv":
                    pe.wait_ge(hidt_ready, 1)
                    pe.wait_ge(small_landed, 16 * 2)
                    for g in range(2):
                        mm(ps[g * DH:g * DH + DH, 7, 384:384 + NC], w2[:, 0, :], hid_t[:, 0, g * NC:g * NC + NC],
                           start=True, stop=True)
                    for g in range(2):
                        last = mm(ps[0:NC, 7, g * DH:g * DH + DH], hid_t[:, 1, g * NC:g * NC + NC], w2[:, 1, :],
                                  start=True, stop=True)
                    last.then_inc(cmp_psum, 1)
                elif step[0] == "rope_rest":
                    swap_flush(step[1])
                    pe.wait_ge(proj_read, step[1])
                    pe.wait_ge(rope_done, sum(c < step[1] for c in ROPED))
                    pe.wait_ge(gatet_ready, 1)
                    pe.wait_ge(cmp_ready, 1)
                elif step[0] == "attend":
                    if step[1] == 0:
                        pe.wait_ge(small_landed, 16 * 2)
                    pe_attend(pe, step[1], step[2])
            pe.wait_ge(exp_ready, len(ITEMS))
            pe.wait_ge(pt_act, len(ITEMS))
            pe.wait_ge(pt_dve, len(ITEMS))
            pe.wait_ge(y_read, 6)
            for m in range(KD):
                g0, b0 = merge_banks(m)
                for u in merge_units_before(m):
                    j = MIX0 + u
                    pe.wait_ge(lo_ready, split_no(j) + 1)
                    if u == U_GM[m]:
                        if m >= 2:
                            pe.wait_ge(gm_scaled, m - 1)
                        three_pass(ps[:, g0, :], [(wtile(j % 2, k * P), moving(k)) for k in range(KD)])
                        last = three_pass(ps[:, g0 + 1, :], [(wtile(j % 2, (KD + k) * P), moving(k)) for k in range(KD)])
                        last.then_inc(gm_psum, 1)
                        continue
                    for ml in range(2):
                        b0 = merge_banks(m + ml)[1]
                        if m:
                            pe.wait_ge(merge_read, m + ml - 1)
                        else:
                            pe.wait_ge(y_lo_ready, 6)
                        three_pass(ps[:, b0, :], [(wtile(j % 2, c * 256 + ml * P), (y_hi[:, c, :], y_lo[:, c, :]))
                                                  for c in range(4)])
                        last = three_pass(ps[:, b0 + 1, :], [(wtile(j % 2, c * 256 + ml * P), (y_hi[:, c, :], y_lo[:, c, :]))
                                                             for c in range(4, 6)])
                        last.then_inc(br_psum, 1)
            for m in range(KD):
                j = MIX0 + U_WO[m // 2]
                pe.wait_ge(lo_ready, split_no(j) + 1)
                if m < 2:
                    pe.wait_ge(merge_read, KD)
                else:
                    pe.wait_ge(x_new, 2 * KD + m - 1)
                before = (lambda k: pe.wait_ge(m_lo, k + 1)) if m == 0 else None
                three_pass(ps[:, 4 + m % 2, :], [(wtile(j % 2, k * 256 + (m % 2) * P), (merged_hi[:, k, :], merged_lo[:, k, :]))
                                                 for k in range(KD)], before).then_inc(wo_psum, 1)
            pe_ffn(pe, 1, FFN2, 2)
            pe_col(pe, 3)
            pe.wait_ge(z_ready, KD)
            pe.wait_ge(var_ready, 4)
            for tt in range(TT):
                for m in range(KD):
                    last = nc.tensor.transpose(ps[:, 2 * tt + m // 4, (m % 4) * P:(m % 4) * P + P],
                                               xT[:, m, tt * P:tt * P + P], ident)
                last.then_inc(fin_psum, 1)


_INS = ["x", "positions", "norm_ffn1", "ffn1_w_in", "ffn1_w_out", "norm_mix", "w_in", "cmp_pos", "cmp_w1",
        "cmp_w2", "w_branch_nsa", "w_branch_dil", "w_out", "norm_ffn2", "ffn2_w_in", "ffn2_w_out", "norm_final"]


def kernel(**inputs):
    import concourse.bacc as bacc
    from concourse.bass_utils import run_bass_kernel_spmd

    nc = bacc.Bacc("TRN2", target_bir_lowering=False, num_devices=1)
    arrays, args = {}, []

    def give(name, a):
        arrays[name] = a
        args.append(nc.dram_tensor(name, a.shape, mybir.dt.from_np(a.dtype), kind="ExternalInput").ap())

    for name in _INS:
        give(f"in_{name}", np.ascontiguousarray(inputs[name]))
    f, b = shape_constants()
    give("shape_constants", f)
    give("shape_masks", b)
    args.append(nc.dram_tensor("out_0", (1, T, D), F32, kind="ExternalOutput").ap())
    build(nc, *args)
    r = run_bass_kernel_spmd(nc, [arrays], core_ids=[0])
    return r.results[0]["out_0"]
```

```python
from contextlib import ExitStack

import numpy as np

import concourse.bass as bass
from concourse import mybir

ALU = mybir.AluOpType
ACT = mybir.ActivationFunctionType
AX = mybir.AxisListType
F32 = mybir.dt.float32
F32R = mybir.dt.float32r
BF16 = mybir.dt.bfloat16
I32 = mybir.dt.int32

P = 128
T = 512
D = 1024
FF = 2816
TT = T // P
KD = D // P
FT = FF // P
HALF = FT // 2
DH = 64
HPG = 4
NCMP = 31
NC = 32
KCOL = 512
GCOL = KCOL + 6 * P
DCOL = GCOL + 24
DW = 3 * 256
MCOL = DCOL + 3 * DW
SCALE = DH ** -0.5
EPS = 1e-6
BIG = 2.0 ** 100
THETA = 500000.0
TWO_PI = (6.28125, 0.0019350051879882812, 3.0199159819e-07)
MAGIC = 12582912.0
SLOT = 16 * P


def shape_constants():
    f = np.zeros((P, 3 * P + 4), np.float32)
    f[:, 0:P] = np.eye(P)
    f[:, P:2 * P] = 1.0
    for head in range(2):
        for i in range(8):
            f[head * DH + 8 + i, 2 * P + head * DH + i] = -1.0
            f[head * DH + i, 2 * P + head * DH + 8 + i] = 1.0
            freq = np.float32(THETA) ** np.float32(-2 * i / 16)
            f[head * DH + i, 3 * P] = freq
            f[head * DH + 8 + i, 3 * P] = freq
    q = np.arange(P)[:, None]
    k = np.arange(P)[None, :]
    b = np.zeros((P, 4 * P + 2 * P + 2 * T), np.float32)
    b[:, 0:P] = np.eye(P)
    b[:, P:2 * P] = np.where(k <= q, 0, -BIG)
    b[:, 2 * P:3 * P] = np.where(k >= q, 0, -BIG)
    n = np.arange(NC)[None, :]
    for qt in range(TT):
        ok = (n * 16 + 31 <= qt * P + q) & (n < NCMP)
        b[:, 3 * P + qt * NC:3 * P + (qt + 1) * NC] = np.where(ok, 0, -BIG)
    kk = np.arange(T)[None, :]
    for i, dil in enumerate((4, 16)):
        r = np.arange(dil)[:, None]
        b[0:dil, (4 + i) * P:(5 + i) * P] = (k % dil == r)
        b[0:dil, 6 * P + i * T:6 * P + (i + 1) * T] = np.where(kk % dil == r, 0, -BIG)
    return f, b


def build(nc, x, positions, norm_ffn1, ffn1_w_in, ffn1_w_out, norm_mix, w_in, cmp_pos, cmp_w1, cmp_w2,
          w_branch_nsa, w_branch_dil, w_out, norm_ffn2, ffn2_w_in, ffn2_w_out, norm_final,
          consts, masks, out):
    outer = ExitStack()
    with outer:
        def sem(name):
            return outer.enter_context(nc.semaphore(name))

        def sb(name, shape, dt=F32, scope=outer):
            return scope.enter_context(nc.sbuf_tensor(name, shape, dt))

        xT = sb("xT", [P, KD, T])
        xg_hi = sb("xg_hi", [P, KD, T], F32R)
        xg_lo = sb("xg_lo", [P, KD, T], F32R)
        w_raw = sb("w_raw", [P, 2, SLOT])
        w_hi = sb("w_hi", [P, 2, SLOT], F32R)
        w_lo = sb("w_lo", [P, 2, SLOT], F32R)
        rstd_row = sb("rstd_row", [P, T])
        rstd_col = sb("rstd_col", [P, TT])
        cos_t = sb("cos_t", [P, T])
        sin_t = sb("sin_t", [P, T])
        sumsq = sb("sumsq", [P, T])
        square = sb("square", [P, 2, T])
        tmp_a = sb("tmp_a", [P, T])
        tmp_b = sb("tmp_b", [P, T])
        const = sb("const", [P, 3 * P + 4])
        vec_rows = sb("vec_rows", [64, P])
        vec_cols = sb("vec_cols", [P, 64])
        norm_s = sb("norm_s", [P, 4, TT])
        gains = vec_cols[:, 0:32].rearrange("p (n m) -> p n m", n=4)
        pos_t = vec_cols[:, 32:64].rearrange("p (v j) -> p v j", v=2)
        ident = const[:, 0:P]
        ones = const[:, P:2 * P]
        swap_perm = const[:, 2 * P:3 * P]
        freq = const[:, 3 * P:3 * P + 1]

        with ExitStack() as scope:
            x_nat = sb("x_nat", [P, TT, D], F32, scope)
        with ExitStack() as scope:
            p_hi = sb("p_hi", [P, FT, T], F32R, scope)
            p_lo = sb("p_lo", [P, FT, T], F32R, scope)
        y_scope = ExitStack()
        y = sb("y", [P, 6, T], F32, y_scope)
        with ExitStack() as scope:
            pool = sb("pool", [P, 16, T], F32, scope)
            v_nsa = sb("v_nsa", [P, TT, 2, P], F32, scope)
            v_dil = sb("v_dil", [P, TT, 3, 256], F32, scope)
            k_cmp = sb("k_cmp", [P, P], F32, scope)
            v_cmp = sb("v_cmp", [NC, 2, DH], F32, scope)
            probs = sb("probs", [P, 2, 1280], F32, scope)
            probs_t = sb("probs_t", [P, 2, 1280], F32, scope)
            gates = sb("gates", [P, TT, 24], F32, scope)
            stat = sb("stat", [P, 2, 4, 4], F32, scope)
            mask = sb("mask", [P, 6 * P + 2 * T], BF16, scope)
            w2 = sb("w2", [P, 2, DH], F32, scope)
            hid = sb("hid", [DH, 2, P], F32, scope)
            hid_t = sb("hid_t", [P, 2, DH], F32, scope)
        with ExitStack() as scope:
            y_hi = sb("y_hi", [P, 6, T], F32R, scope)
            y_lo = sb("y_lo", [P, 6, T], F32R, scope)
            merged_hi = sb("merged_hi", [P, KD, T], F32R, scope)
            merged_lo = sb("merged_lo", [P, KD, T], F32R, scope)
        y_scope.close()
        cmp_w1_tiles = [probs[:, :, :].rearrange("p a c -> p (a c)")[:, T:T + SLOT].rearrange("p (j h) -> p j h", h=P),
                        v_dil[:, :, :, :].rearrange("p a b c -> p (a b c)")[:, 0:SLOT].rearrange("p (j h) -> p j h", h=P)]
        ident_b = mask[:, 0:P]
        causal_b = mask[:, P:2 * P]
        prev_b = mask[:, 2 * P:3 * P]
        cmp_b = mask[:, 3 * P:4 * P]

        def residue(i):
            dil = (4, 16)[i]
            return mask[0:dil, (4 + i) * P:(5 + i) * P], mask[0:dil, 6 * P + i * T:6 * P + (i + 1) * T]

        ps = outer.enter_context(nc.psum_tensor("ps", [P, 8, T], F32))

        def ktiles(w):
            return w.rearrange("(k p) c -> p k c", p=P)

        win = ktiles(w_in[0])
        MU = []

        def columns(cols, c):
            MU.append((c * len(cols) * KD, [((i * KD * c, KD, c), win[:, :, at:at + c])
                                            for i, at in enumerate(cols)], True))
            return len(MU) - 1

        U_CTOK = columns([KCOL, KCOL + P], P)
        U_K = columns([KCOL + 2 * P, KCOL + 4 * P], P)
        U_GATE = columns([GCOL], P)
        U_V = columns([KCOL + 3 * P, KCOL + 5 * P], P)
        U_Q = []
        wq = win[:, :, 0:KCOL].rearrange("p k (g c) -> p k g c", g=2)
        for u in range(2):
            MU.append((SLOT, [((i * KD * P, KD, P), wq[:, :, g, (2 * u + i) * DH:(2 * u + i + 1) * DH], 0, g)
                              for i in range(2) for g in range(2)], True))
            U_Q.append(len(MU) - 1)
        U_VD = [columns([DCOL + 2 * DW + g * 256, DCOL + 2 * DW + g * 256 + P], P) for g in range(3)]
        U_QK = [[columns([DCOL + g * 256 + hp * P, DCOL + DW + g * 256 + hp * P], P) for g in range(3)]
                for hp in range(2)]
        nsa_w = w_branch_nsa[0].rearrange("(g h d) c -> g d h c", g=2, d=DH)
        dil_w = ktiles(w_branch_dil[0])
        U_GM, U_BR = {}, {}
        for mm in range(KD // 2):
            U_GM[2 * mm] = columns([MCOL + 2 * mm * P, MCOL + D + 2 * mm * P], P)
            cs = slice(mm * 256, mm * 256 + 256)
            MU.append((6 * 256, [((0, 4, 256), nsa_w[0][:, :, cs], 0), ((0, 4, 256), nsa_w[1][:, :, cs], DH),
                                 ((1024, 2, 256), dil_w[:, :, cs])], True))
            U_BR[mm] = len(MU) - 1
            U_GM[2 * mm + 1] = columns([MCOL + (2 * mm + 1) * P, MCOL + D + (2 * mm + 1) * P], P)
        wo = ktiles(w_out[0])
        U_WO = []
        for mm in range(KD // 2):
            cs = slice(mm * 256, mm * 256 + 256)
            MU.append((SLOT, [((h * 1024, 4, 256), wo[:, 4 * h:4 * h + 4, cs]) for h in range(2)], True))
            U_WO.append(len(MU) - 1)

        FU = FT + 2 * KD
        MIX0 = FU
        FFN2 = MIX0 + len(MU)
        N_UNITS = FFN2 + FU
        landed_at = []
        total = [0, 0]
        for j in range(N_UNITS):
            n = len(MU[j - MIX0][1]) if MIX0 <= j < FFN2 else 2
            total[j % 2] += 16 * n
            landed_at.append(total[j % 2])

        landed = [sem("weights_landed_0"), sem("weights_landed_1")]
        hi_ready = sem("weight_hi_ready")
        lo_ready = sem("weight_lo_ready")
        w1_landed = sem("cmp_w1_landed")
        hidden_psum = sem("cmp_hidden_in_psum")
        const_landed = sem("const_landed")
        vec_landed = sem("gains_and_cmp_pos_landed")
        x_landed = sem("x_landed")
        gains_psum = sem("gains_in_psum")
        gains_ready = sem("gains_ready")
        pos_landed = sem("positions_landed")
        small_landed = sem("mixer_constants_landed")
        tokens_landed = sem("shifted_tokens_landed")
        out_landed = sem("out_landed")
        xt_psum = sem("x_transposed_in_psum")
        x_new = sem("residual_ready")
        g_hi = sem("xg_hi_ready")
        g_lo = sem("xg_lo_ready")
        sq_ready = sem("square_ready")
        acc_done = sem("square_added")
        col_psum = sem("mean_square_in_psum")
        var_ready = sem("variance_ready")
        std_ready = sem("std_ready")
        diag_ready = sem("rstd_diagonal_ready")
        row_psum = sem("rstd_row_in_psum")
        row_ready = sem("rstd_row_ready")
        dve_chain = sem("vector_step")
        rope_args = sem("rope_arguments_ready")
        rope_sines = sem("rope_sines_ready")
        ffn_sems = [{n: sem(f"ffn{i}_{n}") for n in
                     ("unit_done", "gate_scaled", "value_scaled", "silu_ready", "prod_ready", "prod_hi",
                      "prod_lo")} for i in range(2)]
        proj_psum = sem("projection_in_psum")
        proj_read = sem("projection_read")
        swap_psum = sem("rope_swap_in_psum")
        cos_ready = sem("rope_cos_part_ready")
        rope_done = sem("rope_done")
        padded = sem("padding_cleared")
        tok_ready = sem("cmp_tokens_ready")
        hid_ready = sem("cmp_hidden_ready")
        hidt_psum = sem("cmp_hidden_t_in_psum")
        hidt_ready = sem("cmp_hidden_t_ready")
        cmp_psum = sem("cmp_kv_in_psum")
        cmp_ready = sem("cmp_kv_ready")
        gate_ready = sem("gates_ready")
        gatet_psum = sem("gates_t_in_psum")
        gatet_ready = sem("gates_t_ready")
        scores_psum = sem("scores_in_psum")
        bias_ready = sem("minus_max_ready")
        exp_ready = sem("exp_ready")
        factor_ready = sem("factor_ready")
        scaled_ready = sem("probs_scaled")
        trans_psum = sem("probs_t_in_psum")
        near_psum = sem("near_probs_t_in_psum")
        pt_near = sem("near_probs_t_copied")
        pt_act = sem("probs_t_copied_by_scalar")
        pt_dve = sem("probs_t_copied_by_vector")
        pv_psum = sem("pv_in_psum")
        y_read = sem("y_read")
        y_hi_ready = sem("y_hi_ready")
        y_lo_ready = sem("y_lo_ready")
        gm_psum = sem("merge_gate_in_psum")
        br_psum = sem("branches_in_psum")
        gm_scaled = sem("merge_gate_scaled")
        sig_ready = sem("merge_gate_ready")
        merge_read = sem("merge_banks_read")
        merged_ready = sem("merged_ready")
        m_hi = sem("merged_hi_ready")
        m_lo = sem("merged_lo_ready")
        wo_psum = sem("w_out_in_psum")
        z_ready = sem("final_gained")
        fin_psum = sem("final_in_psum")
        fin_act = sem("final_by_scalar")
        fin_dve = sem("final_by_vector")

        ITEMS = []
        for hh in range(HPG):
            for g in range(2):
                ITEMS.append(("cmp", hh, g))
                ITEMS += [("nsa", hh, g, qt) for qt in range(TT)]
        N_NSA = len(ITEMS)
        for hp in range(2):
            for hl in range(2):
                ITEMS += [("dil", hp, hl, qt) for qt in range(TT)]
        per_pair = {"nsa": 10, "dil": 8}

        def ends_pair(n):
            if n < N_NSA:
                return n // 10 if n % 10 == 9 else None
            return 4 + (n - N_NSA) // 8 if (n - N_NSA) % 8 == 7 else None

        Q_ROPE, Q_RAW, KS, KW = 0, 4, 8, 9
        QD = [10, 0]
        KDS = [13, 4]

        CH = [("t", U_CTOK, 0, "tok0"), ("t", U_CTOK, 1, "tok1"), ("t", U_K, 0, "ks"), ("t", U_K, 1, "kw"),
              ("t", U_GATE, 0, "gate")]
        CH += [("n", U_V, tt, "v") for tt in range(TT)]
        CH += [("t", U_Q[u], i, f"q{2 * u + i}") for u in range(2) for i in range(2)]
        N_CH1 = len(CH)
        CH += [("n", U_VD[g], tt, f"vd{g}") for g in range(3) for tt in range(TT)]
        CH += [("t", U_QK[0][g], i, f"{'qk'[i]}d0{g}") for g in range(3) for i in range(2)]
        N_CH2 = len(CH)
        CH += [("t", U_QK[1][g], i, f"{'qk'[i]}d1{g}") for g in range(3) for i in range(2)]
        slot_of = {"tok0": 10, "tok1": 11, "ks": KS, "kw": KW}
        slot_of |= {f"q{i}": Q_RAW + i for i in range(4)}
        slot_of |= {f"{'qk'[i]}d{hp}{g}": (QD, KDS)[i][hp] + g for i in range(2) for hp in range(2) for g in range(3)}
        roped_slot = {n: (Q_ROPE + int(n[1]) if n[0] == "q" and len(n) == 2 else s)
                      for n, s in slot_of.items() if not n.startswith("tok")}
        ROPED = [c for c, ch in enumerate(CH) if ch[3] in roped_slot]
        last_chunk = {}
        for c, ch in enumerate(CH):
            last_chunk[ch[1]] = c

        def final_view(tt):
            return w_raw[:, tt // 2, (tt % 2) * D:(tt % 2) * D + D]

        def tile_of(t, m):
            return t[:, bass.ds(m, 1), :].rearrange("p a t -> p (a t)")

        def before_in_slot(j):
            return j - 2

        def release(j):
            if j < MIX0:
                return ffn_sems[0]["unit_done"], j + 1
            if j >= FFN2:
                return ffn_sems[1]["unit_done"], j - FFN2 + 1
            u = j - MIX0
            if u in last_chunk:
                return proj_psum, last_chunk[u] + 1
            for m, unit in U_GM.items():
                if u == unit:
                    return gm_psum, m + 1
            for m2, unit in U_BR.items():
                if u == unit:
                    return br_psum, 2 * m2 + 2
            return wo_psum, 2 * U_WO.index(u) + 2

        def width_of(j):
            if MIX0 <= j < FFN2:
                return MU[j - MIX0][0]
            return SLOT if j - (FFN2 if j >= FFN2 else 0) < FT else HALF * P

        def ends_unit(c):
            return last_chunk[CH[c][1]] == c

        def merge_units_before(m):
            return [U_GM[m], U_BR[m // 2]] if m % 2 == 0 else [U_GM[m]]

        def chunks(a, b):
            return [("chunk", c) for c in range(a, b)]

        C_V, C_Q = 5, 9
        STEPS = [("chunk", 0), ("rstd",), ("chunk", 1), ("chunk", 2), ("row",), ("chunk", 3), ("chunk", 4)]
        STEPS += chunks(C_V, C_Q + 1) + [("gates",), ("chunk", C_Q + 1), ("hidden",), ("chunk", C_Q + 2),
                                         ("hidden_t",), ("chunk", C_Q + 3), ("cmp_kv",), ("rope_rest",),
                                         ("attend", 0, N_NSA), ("attend", N_NSA, len(ITEMS))]
        FILL = {}
        at = 1
        for c in range(N_CH1, N_CH2):
            FILL[at] = ("chunk", c)
            at += 1
            if c in ROPED:
                FILL[at] = ("swap", c)
                at += 1
        for i, c in enumerate(range(N_CH2, len(CH))):
            FILL[28 + 2 * i] = ("chunk", c)
            FILL[29 + 2 * i] = ("swap", c)
        assert at <= 28 and max(FILL) < N_NSA

        def bank_of(c):
            return c % 4 if c < N_CH1 else 7

        def swap_bank(c):
            return 4 + ROPED.index(c) % 2 if c < N_CH1 else 7

        def merge_banks(m):
            return (2, 0) if m % 2 == 0 else (6, 4)

        block = outer.enter_context(nc.Block())

        def load(sp, j, s, pieces):
            for piece in pieces:
                (at, k, c), src = piece[0], piece[1]
                p0 = piece[2] if len(piece) > 2 else 0
                rows = src.shape[0]
                dst = w_raw[p0:p0 + rows, s, at:at + k * c].rearrange("p (k c) -> p k c", k=k)
                if len(piece) > 3:
                    dst = dst[:, :, piece[3] * DH:piece[3] * DH + DH]
                sp.dma_start(dst, src).then_inc(landed[s], 16)

        def sync_ffn(sp, base, wi, wd):
            wi, wd = ktiles(wi[0]), ktiles(wd[0])
            k0 = base

            def up(i, s, wait):
                f = 2 * i + s
                if wait:
                    sp.wait_ge(lo_ready, k0 + f - 1)
                load(sp, None, (base + s) % 2,
                     [((0, KD, P), wi[:, :, bass.ds(f * P, P)]), ((KD * P, KD, P), wi[:, :, bass.ds(f * P + FF, P)])])

            for s in range(2):
                up(0, s, base > 0)
            with sp.Fori(1, FT // 2) as i:
                for s in range(2):
                    up(i, s, True)
            with sp.Fori(0, KD) as m:
                for s in range(2):
                    sp.wait_ge(lo_ready, k0 + FT + 2 * m + s - 1)
                    load(sp, None, (base + s) % 2,
                         [((0, 6, P), wd[:, s * HALF:s * HALF + 6, bass.ds(m * P, P)]),
                          ((6 * P, 5, P), wd[:, s * HALF + 6:(s + 1) * HALF, bass.ds(m * P, P)])])

        @block.sync
        def _(sp):
            sp.dma_start(const[:, :], consts).then_inc(const_landed, 16)
            xv = x[0].rearrange("(t p) d -> p t d", p=P)
            for tt in range(TT):
                sp.dma_start(x_nat[:, tt, :], xv[:, tt, :]).then_inc(x_landed, 16)
            sync_ffn(sp, 0, ffn1_w_in, ffn1_w_out)
            for u, (_, pieces, _) in enumerate(MU):
                j = MIX0 + u
                sp.wait_ge(lo_ready, j - 1)
                load(sp, j, j % 2, pieces)
                if u == U_Q[0]:
                    sp.wait_ge(proj_read, 2)
                    for kv in range(2):
                        for par in range(2):
                            for g in range(2):
                                sp.dma_start(pool[par * DH:par * DH + DH, 12 + 2 * kv + g, 0:T - par],
                                             pool[g * DH:g * DH + DH, 10 + kv, par:T]).then_inc(tokens_landed, 16)
            sync_ffn(sp, FFN2, ffn2_w_in, ffn2_w_out)
            ov = out[0].rearrange("(t p) d -> p t d", p=P)
            for tt in range(TT):
                sp.wait_ge(fin_act, tt + 1)
                sp.wait_ge(fin_dve, tt + 1)
                sp.dma_start(ov[:, tt, :], final_view(tt)).then_inc(out_landed, 16)
            sp.wait_ge(out_landed, 16 * TT)

        def pool_squares(pe, n):
            for m in range(KD):
                v = KD * n + m
                pe.wait_ge(sq_ready, v + 1)
                if m == 0:
                    if n:
                        pe.wait_ge(col_psum, n)
                    nc.gpsimd.tensor_copy(sumsq[:, :], square[:, m % 2, :]).then_inc(acc_done, 1)
                else:
                    pe.wait_ge(acc_done, v)
                    nc.gpsimd.tensor_tensor(sumsq[:, :], sumsq[:, :], square[:, m % 2, :], ALU.add).then_inc(acc_done, 1)

        def pool_rope(pe, c):
            r = ROPED.index(c)
            name = CH[c][3]
            pe.wait_ge(proj_read, c + 1)
            if r:
                pe.wait_ge(rope_done, r)
            nc.gpsimd.tensor_tensor(tmp_b[:, :], pool[:, slot_of[name], :], cos_t[:, :], ALU.mult).then_inc(cos_ready, 1)

        @block.gpsimd
        def _(pl):
            gv = [norm_ffn1[0], norm_mix[0], norm_ffn2[0], norm_final]
            for i, g in enumerate(gv):
                pl.dma_start(vec_rows[i * KD:i * KD + KD, :], g.rearrange("(m p) -> m p", p=P)).then_inc(vec_landed, 16)
            pl.dma_start(vec_rows[32:64, :], cmp_pos[0].rearrange("v (j r) d -> (v j) (r d)", r=2)).then_inc(vec_landed, 16)
            pl.dma_start(cos_t[:, :].bitcast(I32), positions.broadcast_to([P, T])).then_inc(pos_landed, 16)
            pool_squares(pl, 0)
            pool_squares(pl, 1)
            pl.wait_ge(ffn_sems[0]["unit_done"], FU)
            pl.dma_start(mask[:, :], masks).then_inc(small_landed, 16)
            for kv, dst in enumerate(cmp_w1_tiles):
                pl.dma_start(dst, cmp_w1[0, kv].rearrange("(j q) h -> q j h", q=P)).then_inc(w1_landed, 16)
            pl.dma_start(w2[:, :, :], cmp_w2[0].rearrange("v h d -> h v d")).then_inc(small_landed, 16)
            nc.gpsimd.memset(k_cmp[:, :], 0.0)
            nc.gpsimd.memset(probs_t[:, :, :], 0.0).then_inc(padded, 1)
            for c in range(len(CH)):
                if c in ROPED:
                    pool_rope(pl, c)
            pool_squares(pl, 2)
            pool_squares(pl, 3)

        def act_split(act, j, it=0):
            s, k = j % 2, j
            if j >= N_UNITS:
                return
            act.wait_ge(landed[s], landed_at[j] + 32 * it)
            if k >= 2:
                done, value = release(before_in_slot(j))
                act.wait_ge(done, value + 2 * it)
            w = width_of(j)
            nc.scalar.activation(w_hi[:, s, 0:w], w_raw[:, s, 0:w], ACT.Copy).then_inc(hi_ready, 1)

        def act_gain(act, n, m0, it=0):
            m, v = m0 + it, KD * n + m0 + it
            act.wait_ge(x_new, v + 1)
            if KD * n + m0 >= 2:
                act.wait_ge(acc_done, v - 1)
            if n < 3:
                nc.scalar.activation(tile_of(xg_hi, m), tile_of(xT, m), ACT.Copy,
                                     scale=gains[:, n, bass.ds(m, 1)]).then_inc(g_hi, 1)
            nc.scalar.activation(square[:, m0 % 2, :], tile_of(xT, m), ACT.Square).then_inc(sq_ready, 1)
            if n == 3:
                nc.scalar.activation(tile_of(xT, m), tile_of(xT, m), ACT.Copy,
                                     scale=gains[:, n, bass.ds(m, 1)]).then_inc(z_ready, 1)

        def act_std(act, n):
            act.wait_ge(var_ready, n + 1)
            nc.scalar.activation(norm_s[:, 1, :], norm_s[:, 0, :], ACT.Sqrt).then_inc(std_ready, 1)

        def act_ffn(act, i, base, norm):
            S = ffn_sems[i]

            def evac(f):
                act.wait_ge(S["gate_scaled"], f + 1)
                nc.scalar.activation(tmp_a[:, :], tmp_a[:, :], ACT.Silu).then_inc(S["silu_ready"], 1)
                act.wait_ge(S["prod_ready"], f + 1)
                nc.scalar.activation(tile_of(p_hi, f), tmp_b[:, :], ACT.Copy).then_inc(S["prod_hi"], 1)

            act_std(act, norm)
            act_split(act, base + 2)
            act_split(act, base + 3)
            evac(0)
            evac(1)
            if i == 0:
                act.wait_ge(rope_args, 1)
                nc.scalar.activation(sin_t[:, :], sin_t[:, :], ACT.Sin, scale=0.5).then_inc(rope_sines, 1)
                nc.scalar.activation(cos_t[:, :], cos_t[:, :], ACT.Sin).then_inc(rope_sines, 1)
            with act.Fori(1, FT // 2 - 1) as it:
                for s in range(2):
                    act_split(act, base + s + 2, it)
                    evac(2 * it + s)
            for s in range(2):
                act_split(act, base + FT + s)
                evac(FT - 2 + s)
            with act.Fori(0, KD // 2 - 1) as it:
                for ml in range(2):
                    act_split(act, base + FT + 2 * ml + 2, 2 * it)
                    act_split(act, base + FT + 2 * ml + 3, 2 * it)
                    act_gain(act, norm + 1, ml, 2 * it)
            for ml in range(2):
                for h in range(2):
                    act_split(act, base + FU - 2 + 2 * ml + h)
                act_gain(act, norm + 1, KD - 2 + ml)

        def act_exp(act, n):
            it, e, b = ITEMS[n], n % 2, 2 * (n % 2)
            act.wait_ge(bias_ready, n + 1)
            if n >= 2:
                act.wait_ge(trans_psum, n - 1)
            if n >= N_NSA + 2:
                act.wait_ge(near_psum, n - N_NSA - 1)
            if it[0] == "cmp":
                nc.scalar.activation(probs[:, e, 0:P], probs[:, e, 0:P], ACT.Exp, scale=SCALE).then_inc(exp_ready, 1)
                return
            nk = (it[3] + 1) * P
            own = it[0] == "nsa"
            for i in range(2):
                last = nc.scalar.activation(probs[:, e, i * T:i * T + nk], ps[:, b + i, 0:nk], ACT.Exp,
                                            bias=stat[:, e, 1, (i if own else 0):(i if own else 0) + 1],
                                            scale=SCALE, accum_out=stat[:, e, 2, i:i + 1])
            if not own:
                n0 = min(it[3] + 1, 2) * P
                last = nc.scalar.activation(probs[:, e, 2 * T:2 * T + n0], ps[:, 7, 0:n0], ACT.Exp,
                                            bias=stat[:, e, 1, 0:1], scale=SCALE, accum_out=stat[:, e, 2, 2:3])
            last.then_inc(exp_ready, 1)

        def act_copy_probs(act, n):
            it, e = ITEMS[n], n % 2
            act.wait_ge(trans_psum, n + 1)
            if n >= 2:
                act.wait_ge(pv_psum, n - 1)
            if it[0] == "cmp":
                nc.scalar.activation(probs_t[0:NC, e, 0:256], ps[0:NC, 4, 0:256], ACT.Copy).then_inc(pt_act, 1)
            else:
                nk = (it[3] + 1) * P
                nc.scalar.activation(probs_t[:, e, 0:nk], ps[:, 4, 0:nk], ACT.Copy).then_inc(pt_act, 1)

        def act_copy_near(act, n):
            if n < N_NSA:
                return
            it, e = ITEMS[n], n % 2
            n0 = min(it[3] + 1, 2) * P
            act.wait_ge(near_psum, n - N_NSA + 1)
            nc.scalar.activation(probs_t[:, e, 2 * T:2 * T + n0], ps[:, 4, 0:n0], ACT.Copy).then_inc(pt_near, 1)

        def act_y(act, n):
            act.wait_ge(pv_psum, n + 1)
            nc.scalar.activation(y[:, ends_pair(n), :], ps[:, 6, :], ACT.Copy).then_inc(y_read, 1)

        def act_attend(act, a, b):
            act_exp(act, a)
            act_exp(act, a + 1)
            for n in range(a, b):
                act_copy_probs(act, n)
                act_copy_near(act, n)
                if n + 2 < b:
                    act_exp(act, n + 2)
                if n > a and ends_pair(n - 1) is not None:
                    act_y(act, n - 1)
                kind, c = FILL.get(n, (None, None))
                if kind == "chunk" and ends_unit(c):
                    act_split(act, MIX0 + CH[c][1] + 2)
            act_y(act, b - 1)

        @block.scalar
        def _(act):
            act.wait_ge(gains_ready, 1)
            for m in range(KD):
                act_gain(act, 0, m)
                if m == 1:
                    act_split(act, 0)
            act_split(act, 1)
            act_ffn(act, 0, 0, 0)
            for step in STEPS:
                if step[0] == "chunk":
                    if ends_unit(step[1]):
                        act_split(act, MIX0 + CH[step[1]][1] + 2)
                elif step[0] == "rstd":
                    act_std(act, 1)
                elif step[0] == "gates":
                    act.wait_ge(proj_read, 5)
                    nc.scalar.activation(probs[0:24, 0, 0:T], probs[0:24, 0, 0:T], ACT.Sigmoid).then_inc(gate_ready, 1)
                elif step[0] == "hidden":
                    for kv in range(2):
                        act.wait_ge(hidden_psum, 2)
                        nc.scalar.activation(hid[:, kv, :], ps[0:DH, 7, kv * P:kv * P + P],
                                             ACT.Silu).then_inc(hid_ready, 1)
                elif step[0] == "attend":
                    act_attend(act, step[1], step[2])
            for c in range(6):
                nc.scalar.activation(y_hi[:, c, :], y[:, c, :], ACT.Copy).then_inc(y_hi_ready, 1) if c else (
                    act.wait_ge(y_read, 6),
                    nc.scalar.activation(y_hi[:, c, :], y[:, c, :], ACT.Copy).then_inc(y_hi_ready, 1))
            for m in range(KD):
                for u in merge_units_before(m):
                    act_split(act, MIX0 + u + 2)
                act.wait_ge(gm_scaled, m + 1)
                nc.scalar.activation(tmp_a[:, :], tmp_a[:, :], ACT.Sigmoid)
                nc.scalar.activation(tmp_b[:, :], tmp_b[:, :], ACT.Sigmoid).then_inc(sig_ready, 1)
                act.wait_ge(merged_ready, m + 1)
                nc.scalar.activation(merged_hi[:, m, :], tmp_a[:, :], ACT.Copy).then_inc(m_hi, 1)
            for m in range(KD):
                act_gain(act, 2, m)
                if m % 2:
                    act_split(act, MIX0 + U_WO[m // 2] + 2)
            act_ffn(act, 1, FFN2, 2)
            for tt in range(TT):
                if tt == 0:
                    act_std(act, 3)
                act.wait_ge(fin_psum, tt + 1)
                act.wait_ge(row_ready, 4)
                nc.scalar.activation(final_view(tt)[:, 0:T], ps[:, 2 * tt, :], ACT.Copy,
                                     scale=rstd_col[:, tt:tt + 1]).then_inc(fin_act, 1)

        chain = [0]

        def link(dve, ins):
            chain[0] += 1
            ins.then_inc(dve_chain, 1)
            dve.wait_ge(dve_chain, chain[0])

        V = nc.vector

        def dve_split(dve, j, it=0):
            s, k = j % 2, j
            if j >= N_UNITS:
                return
            w = width_of(j)
            dve.wait_ge(hi_ready, k + 1 + 2 * it)
            V.tensor_tensor(w_lo[:, s, 0:w], w_raw[:, s, 0:w], w_hi[:, s, 0:w].bitcast(F32),
                            ALU.subtract).then_inc(lo_ready, 1)

        def dve_gain(dve, n, m0, it=0):
            m, v = m0 + it, KD * n + m0 + it
            if n < 3:
                dve.wait_ge(g_hi, v + 1)
                V.scalar_tensor_tensor(out=tile_of(xg_lo, m), in0=tile_of(xT, m), scalar=gains[:, n, bass.ds(m, 1)],
                                       in1=tile_of(xg_hi, m).bitcast(F32), op0=ALU.mult,
                                       op1=ALU.subtract).then_inc(g_lo, 1)

        def dve_rstd(dve, n):
            dve.wait_ge(col_psum, n + 1)
            V.tensor_scalar(norm_s[:, 0, :], ps[:, 7, 0:2 * TT].rearrange("p (t two) -> p t two", two=2)[:, :, 0],
                            1.0 / D, EPS, ALU.mult, ALU.add).then_inc(var_ready, 1)
            dve.wait_ge(std_ready, n + 1)
            link(dve, V.reciprocal(norm_s[:, 2, :], norm_s[:, 1, :]))
            link(dve, V.tensor_tensor(norm_s[:, 3, :], norm_s[:, 2, :], norm_s[:, 2, :], ALU.mult))
            link(dve, V.tensor_tensor(norm_s[:, 3, :], norm_s[:, 3, :], norm_s[:, 0, :], ALU.mult))
            link(dve, V.tensor_scalar(norm_s[:, 3, :], norm_s[:, 3, :], -0.5, 1.5, ALU.mult, ALU.add))
            if n == 3:
                V.tensor_tensor(rstd_col[:, :], norm_s[:, 2, :], norm_s[:, 3, :], ALU.mult).then_inc(row_ready, 1)
                return
            link(dve, V.tensor_tensor(rstd_col[:, :], norm_s[:, 2, :], norm_s[:, 3, :], ALU.mult))
            for tt in range(TT):
                last = V.tensor_scalar(tmp_a[:, tt * P:tt * P + P], ident, rstd_col[:, tt:tt + 1], None, ALU.mult)
            last.then_inc(diag_ready, 1)

        def dve_row(dve, n):
            dve.wait_ge(row_psum, n + 1)
            V.tensor_copy(rstd_row[:, :], ps[:, 6, :]).then_inc(row_ready, 1)
            dve.wait_ge(row_ready, n + 1)

        def dve_ffn(dve, i, base, norm):
            S = ffn_sems[i]

            def evac(f, s):
                dve.wait_ge(S["unit_done"], f + 1)
                V.tensor_tensor(tmp_a[:, :], ps[:, 2 * s, :], rstd_row[:, :], ALU.mult).then_inc(S["gate_scaled"], 1)
                if not (isinstance(f, int) and f == 0):
                    dve.wait_ge(S["prod_lo"], f)
                V.tensor_tensor(tmp_b[:, :], ps[:, 2 * s + 1, :], rstd_row[:, :], ALU.mult).then_inc(S["value_scaled"], 1)
                dve.wait_ge(S["silu_ready"], f + 1)
                dve.wait_ge(S["value_scaled"], f + 1)
                V.tensor_tensor(tmp_b[:, :], tmp_a[:, :], tmp_b[:, :], ALU.mult).then_inc(S["prod_ready"], 1)
                dve.wait_ge(S["prod_hi"], f + 1)
                V.tensor_tensor(tile_of(p_lo, f), tmp_b[:, :], tile_of(p_hi, f).bitcast(F32),
                                ALU.subtract).then_inc(S["prod_lo"], 1)

            def residual(m0, it=0):
                v = KD * (norm + 1) + m0 + it
                dve.wait_ge(S["unit_done"], FT + 2 * (m0 + it + 1))
                V.scalar_tensor_tensor(out=tile_of(xT, m0 + it), in0=ps[:, 4 + m0 % 2, :], scalar=0.5,
                                       in1=tile_of(xT, m0 + it), op0=ALU.mult, op1=ALU.add).then_inc(x_new, 1)
                dve_gain(dve, norm + 1, m0, it)

            dve_rstd(dve, norm)
            dve_split(dve, base + 2)
            dve_row(dve, norm)
            evac(0, 0)
            dve_split(dve, base + 3)
            evac(1, 1)
            if i == 0:
                dve_rope_tables(dve)
            with dve.Fori(1, FT // 2 - 1) as it:
                for s in range(2):
                    dve_split(dve, base + s + 2, it)
                    evac(2 * it + s, s)
            for s in range(2):
                dve_split(dve, base + FT + s)
                evac(FT - 2 + s, s)
            with dve.Fori(0, KD // 2 - 1) as it:
                for ml in range(2):
                    dve_split(dve, base + FT + 2 * ml + 2, 2 * it)
                    dve_split(dve, base + FT + 2 * ml + 3, 2 * it)
                    residual(ml, 2 * it)
            for ml in range(2):
                for h in range(2):
                    dve_split(dve, base + FU - 2 + 2 * ml + h)
                residual(KD - 2 + ml)

        def dve_rope_tables(dve):
            dve.wait_ge(pos_landed, 16)
            link(dve, V.tensor_copy(sin_t[:, :], cos_t[:, :].bitcast(I32)))
            link(dve, V.tensor_scalar(sin_t[:, :], sin_t[:, :], freq, None, ALU.mult))
            link(dve, V.tensor_scalar(tmp_a[:, :], sin_t[:, :], float(1 / (2 * np.pi)), MAGIC, ALU.mult, ALU.add))
            link(dve, V.tensor_scalar(tmp_a[:, :], tmp_a[:, :], MAGIC, None, ALU.subtract))
            for part in TWO_PI:
                link(dve, V.scalar_tensor_tensor(out=sin_t[:, :], in0=tmp_a[:, :], scalar=-part, in1=sin_t[:, :],
                                                 op0=ALU.mult, op1=ALU.add))
            link(dve, V.scalar_tensor_tensor(out=tmp_a[:, :], in0=sin_t[:, :], scalar=-1.0, in1=sin_t[:, :],
                                             op0=ALU.mult, op1=ALU.max))
            V.tensor_scalar(cos_t[:, :], tmp_a[:, :], -0.5, float(np.pi / 2), ALU.mult, ALU.add).then_inc(rope_args, 1)
            dve.wait_ge(rope_sines, 2)
            link(dve, V.scalar_tensor_tensor(out=tmp_a[:, :], in0=sin_t[:, :], scalar=2.0, in1=cos_t[:, :],
                                             op0=ALU.mult, op1=ALU.mult))
            link(dve, V.tensor_tensor(cos_t[:, :], sin_t[:, :], sin_t[:, :], ALU.mult))
            link(dve, V.tensor_scalar(cos_t[:, :], cos_t[:, :], -2.0, 1.0, ALU.mult, ALU.add))
            link(dve, V.tensor_copy(sin_t[:, :], tmp_a[:, :]))

        def dve_chunk(dve, c):
            kind, _, i, name = CH[c]
            dve.wait_ge(proj_psum, c + 1)
            b = bank_of(c)
            if kind == "n":
                dst = v_nsa[:, i, :, :].rearrange("p a c -> p (a c)") if name == "v" else v_dil[:, i, int(name[2]), :]
                V.tensor_scalar(dst, ps[:, b, 0:256], rstd_col[:, i:i + 1], None, ALU.mult).then_inc(proj_read, 1)
            elif name == "gate":
                V.tensor_tensor(probs[0:24, 0, 0:T], ps[0:24, b, :], rstd_row[0:24, :], ALU.mult).then_inc(proj_read, 1)
            else:
                V.tensor_tensor(pool[:, slot_of[name], :], ps[:, b, :], rstd_row[:, :], ALU.mult).then_inc(proj_read, 1)

        def dve_rope(dve, c):
            r = ROPED.index(c)
            dve.wait_ge(swap_psum, r + 1)
            if r:
                dve.wait_ge(rope_done, r)
            link(dve, V.tensor_tensor(tmp_a[:, :], ps[:, swap_bank(c), :], sin_t[:, :], ALU.mult))
            dve.wait_ge(cos_ready, r + 1)
            V.tensor_tensor(pool[:, roped_slot[CH[c][3]], :], tmp_a[:, :], tmp_b[:, :], ALU.add).then_inc(rope_done, 1)

        def dve_tokens(dve):
            dve.wait_ge(tokens_landed, 16 * 8)
            dve.wait_ge(padded, 1)
            for kv in range(2):
                for g in range(2):
                    tv = pool[:, 12 + 2 * kv + g, :].rearrange("p (n j two) -> p j n two", n=NC, j=8)
                    av = probs_t[:, kv, 0:2 * 512].rearrange("p (j g n) -> p j g n", j=16, g=2)
                    for h in range(2):
                        last = V.tensor_tensor(
                            av[:, 8 * h:8 * h + 8, g, 0:NCMP], tv[:, :, h:h + NCMP, 0],
                            pos_t[:, kv, 8 * h:8 * h + 8].unsqueeze(2).broadcast_to([P, 8, NCMP]), ALU.add)
            last.then_inc(tok_ready, 1)

        def dve_prepare(dve, n):
            it, e, b = ITEMS[n], n % 2, 2 * (n % 2)
            dve.wait_ge(scores_psum, n + 1)
            if it[0] == "cmp":
                sc = ps[:, b, :].rearrange("p (q k) -> p q k", q=TT)[:, :, 0:NC]
                link(dve, V.tensor_reduce(stat[:, e, 0, 0:4], sc, AX.X, ALU.max))
                link(dve, V.tensor_scalar(stat[:, e, 0, 0:4], stat[:, e, 0, 0:4], -1e28, None, ALU.max))
                if n >= 2:
                    dve.wait_ge(trans_psum, n - 1)
                V.tensor_tensor(probs[:, e, 0:P].rearrange("p (q n) -> p q n", q=TT), sc,
                                stat[:, e, 0, 0:4].unsqueeze(2).broadcast_to([P, TT, NC]),
                                ALU.subtract).then_inc(bias_ready, 1)
                return
            nk = (it[3] + 1) * P
            link(dve, V.tensor_reduce(stat[:, e, 0, 0:2], ps[:, b:b + 2, 0:nk], AX.X, ALU.max))
            if it[0] == "nsa":
                V.tensor_scalar(stat[:, e, 1, 0:2], stat[:, e, 0, 0:2], -SCALE, None, ALU.mult).then_inc(bias_ready, 1)
            else:
                n0 = min(it[3] + 1, 2) * P
                link(dve, V.tensor_reduce(stat[:, e, 0, 2:3], ps[:, 7, 0:n0], AX.X, ALU.max))
                link(dve, V.tensor_reduce(stat[:, e, 0, 3:4], stat[:, e, 0, 0:3], AX.X, ALU.max))
                V.tensor_scalar(stat[:, e, 1, 0:1], stat[:, e, 0, 3:4], -SCALE, None, ALU.mult).then_inc(bias_ready, 1)

        def dve_factor(dve, n):
            it, e = ITEMS[n], n % 2
            dve.wait_ge(exp_ready, n + 1)
            if it[0] == "cmp":
                h = it[2] * HPG + it[1]
                link(dve, V.tensor_reduce(stat[:, e, 2, 0:4], probs[:, e, 0:P].rearrange("p (q n) -> p q n", q=TT),
                                          AX.X, ALU.add))
                link(dve, V.tensor_scalar(stat[:, e, 2, 0:4], stat[:, e, 2, 0:4], 0.5, None, ALU.max))
                link(dve, V.reciprocal(stat[:, e, 0, 0:4], stat[:, e, 2, 0:4]))
                V.tensor_tensor(stat[:, e, 3, 0:4], stat[:, e, 0, 0:4], gates[:, :, 3 * h], ALU.mult).then_inc(factor_ready, 1)
                dve.wait_ge(factor_ready, n + 1)
                v = probs[:, e, 0:P].rearrange("p (q n) -> p q n", q=TT)
                V.tensor_tensor(v, v, stat[:, e, 3, 0:4].unsqueeze(2).broadcast_to([P, TT, NC]),
                                ALU.mult).then_inc(scaled_ready, 1)
            elif it[0] == "nsa":
                h = it[2] * HPG + it[1]
                link(dve, V.reciprocal(stat[:, e, 0, 0:2], stat[:, e, 2, 0:2]))
                V.tensor_tensor(stat[:, e, 3, 0:2], stat[:, e, 0, 0:2], gates[:, it[3], 3 * h + 1:3 * h + 3],
                                ALU.mult).then_inc(factor_ready, 1)
                dve.wait_ge(factor_ready, n + 1)
                nk = (it[3] + 1) * P
                V.tensor_scalar(probs[:, e, 0:nk], probs[:, e, 0:nk], stat[:, e, 3, 0:1], None, ALU.mult)
                V.tensor_scalar(probs[:, e, T:T + nk], probs[:, e, T:T + nk], stat[:, e, 3, 1:2], None,
                                ALU.mult).then_inc(scaled_ready, 1)
            else:
                link(dve, V.tensor_reduce(stat[:, e, 2, 3:4], stat[:, e, 2, 0:3], AX.X, ALU.add))
                V.reciprocal(stat[:, e, 3, 0:1], stat[:, e, 2, 3:4]).then_inc(factor_ready, 1)
                dve.wait_ge(factor_ready, n + 1)
                nk, n0 = (it[3] + 1) * P, min(it[3] + 1, 2) * P
                v = probs[:, e, 0:2 * T].rearrange("p (b k) -> p b k", b=2)[:, :, 0:nk]
                V.tensor_scalar(v, v, stat[:, e, 3, 0:1], None, ALU.mult)
                V.tensor_scalar(probs[:, e, 2 * T:2 * T + n0], probs[:, e, 2 * T:2 * T + n0],
                                stat[:, e, 3, 0:1], None, ALU.mult).then_inc(scaled_ready, 1)

        def dve_copy_probs(dve, n):
            it, e = ITEMS[n], n % 2
            dve.wait_ge(trans_psum, n + 1)
            if n >= 2:
                dve.wait_ge(pv_psum, n - 1)
            if it[0] == "cmp":
                V.tensor_copy(probs_t[0:NC, e, 256:T], ps[0:NC, 5, 256:T]).then_inc(pt_dve, 1)
                return
            nk = (it[3] + 1) * P
            V.tensor_copy(probs_t[:, e, T:T + nk], ps[:, 5, 0:nk]).then_inc(pt_dve, 1)

        def dve_attend(dve, a, b):
            dve_prepare(dve, a)
            dve_prepare(dve, a + 1)
            dve_factor(dve, a)
            for n in range(a, b):
                if n + 1 < b:
                    dve_factor(dve, n + 1)
                dve_copy_probs(dve, n)
                if n + 2 < b:
                    dve_prepare(dve, n + 2)
                kind, c = FILL.get(n, (None, None))
                if kind == "chunk":
                    dve_chunk(dve, c)
                    if ends_unit(c):
                        dve_split(dve, MIX0 + CH[c][1] + 2)
                elif kind == "swap":
                    dve_rope(dve, c)

        @block.vector
        def _(dve):
            dve.wait_ge(const_landed, 16)
            dve.wait_ge(gains_psum, 1)
            V.tensor_copy(vec_cols[:, :], ps[:, 7, 0:64]).then_inc(gains_ready, 1)
            dve.wait_ge(gains_ready, 1)
            for m in range(KD):
                dve.wait_ge(xt_psum, m + 1)
                V.tensor_copy(xT[:, m, :], ps[:, m, :]).then_inc(x_new, 1)
                dve_gain(dve, 0, m)
                if m == 1:
                    dve_split(dve, 0)
            dve_split(dve, 1)
            dve_ffn(dve, 0, 0, 0)
            rope_pending = []

            def rope_flush(upto):
                while rope_pending and rope_pending[0] < upto:
                    dve_rope(dve, rope_pending.pop(0))

            for step in STEPS:
                if step[0] == "chunk" and step[1] < 2:
                    if step[1] == 1:
                        dve_split(dve, MIX0 + 2)
                elif step[0] == "rstd":
                    dve_rstd(dve, 1)
                elif step[0] == "row":
                    dve_row(dve, 1)
                    dve_chunk(dve, 0)
                    dve_chunk(dve, 1)
                    dve_chunk(dve, 2)
                    rope_pending.append(2)
                elif step[0] == "chunk":
                    c = step[1]
                    if c > 2:
                        dve_chunk(dve, c)
                        rope_flush(c)
                        if c in ROPED:
                            rope_pending.append(c)
                        if ends_unit(c):
                            dve_split(dve, MIX0 + CH[c][1] + 2)
                    if c == C_Q:
                        dve_tokens(dve)
                elif step[0] == "gates":
                    dve.wait_ge(gatet_psum, 1)
                    V.tensor_copy(gates[:, :, :].rearrange("p t c -> p (t c)"), ps[:, 6, 0:TT * 24]).then_inc(gatet_ready, 1)
                elif step[0] == "hidden_t":
                    dve.wait_ge(hidt_psum, 1)
                    V.tensor_copy(hid_t[:, :, :].rearrange("p a c -> p (a c)"), ps[:, 7, 256:384]).then_inc(hidt_ready, 1)
                elif step[0] == "cmp_kv":
                    dve.wait_ge(cmp_psum, 1)
                    V.tensor_copy(k_cmp[:, 0:NC], ps[:, 7, 384:384 + NC])
                    V.tensor_copy(v_cmp[:, :, :].rearrange("p a c -> p (a c)"), ps[0:NC, 7, 0:P]).then_inc(cmp_ready, 1)
                elif step[0] == "rope_rest":
                    rope_flush(len(CH))
                elif step[0] == "attend":
                    dve_attend(dve, step[1], step[2])
            for c in range(6):
                dve.wait_ge(y_hi_ready, c + 1)
                V.tensor_tensor(y_lo[:, c, :], y[:, c, :], y_hi[:, c, :].bitcast(F32), ALU.subtract).then_inc(y_lo_ready, 1)
            for m in range(KD):
                for u in merge_units_before(m):
                    dve_split(dve, MIX0 + u + 2)
                g0, b0 = merge_banks(m)
                dve.wait_ge(gm_psum, m + 1)
                if m:
                    dve.wait_ge(m_lo, m)
                V.tensor_tensor(tmp_a[:, :], ps[:, g0, :], rstd_row[:, :], ALU.mult)
                V.tensor_tensor(tmp_b[:, :], ps[:, g0 + 1, :], rstd_row[:, :], ALU.mult).then_inc(gm_scaled, 1)
                dve.wait_ge(sig_ready, m + 1)
                dve.wait_ge(br_psum, m + 1)
                V.tensor_tensor(tmp_a[:, :], ps[:, b0, :], tmp_a[:, :], ALU.mult)
                V.tensor_tensor(tmp_b[:, :], ps[:, b0 + 1, :], tmp_b[:, :], ALU.mult).then_inc(merge_read, 1)
                dve.wait_ge(merge_read, m + 1)
                V.tensor_tensor(tmp_a[:, :], tmp_a[:, :], tmp_b[:, :], ALU.add).then_inc(merged_ready, 1)
                dve.wait_ge(m_hi, m + 1)
                V.tensor_tensor(merged_lo[:, m, :], tmp_a[:, :], merged_hi[:, m, :].bitcast(F32),
                                ALU.subtract).then_inc(m_lo, 1)
            for m in range(KD):
                dve.wait_ge(wo_psum, m + 1)
                V.tensor_tensor(xT[:, m, :], ps[:, 4 + m % 2, :], xT[:, m, :], ALU.add).then_inc(x_new, 1)
                dve_gain(dve, 2, m)
                if m % 2:
                    dve_split(dve, MIX0 + U_WO[m // 2] + 2)
            dve_ffn(dve, 1, FFN2, 2)
            dve_rstd(dve, 3)
            dve.wait_ge(row_ready, 4)
            for tt in range(TT):
                dve.wait_ge(fin_psum, tt + 1)
                V.tensor_scalar(final_view(tt)[:, T:D], ps[:, 2 * tt + 1, :], rstd_col[:, tt:tt + 1], None,
                                ALU.mult).then_inc(fin_dve, 1)

        mm = nc.tensor.matmul

        def three_pass(out, pairs, before=None):
            for i, ((ah, al), (bh, bl)) in enumerate(pairs):
                if before:
                    before(i)
                mm(out, ah, bh, start=(i == 0), stop=False)
                mm(out, ah, bl, start=False, stop=False)
                last = mm(out, al, bh, start=False, stop=(i == len(pairs) - 1))
            return last

        def wtile(s, at, c=P):
            return w_hi[:, s, at:at + c], w_lo[:, s, at:at + c]

        def pe_col(pe, n):
            pe.wait_ge(acc_done, KD * (n + 1))
            for tt in range(TT):
                last = mm(ps[:, 7, 2 * tt:2 * tt + 2], sumsq[:, tt * P:tt * P + P], ones[:, 0:2], start=True, stop=True)
            last.then_inc(col_psum, 1)

        def pe_row(pe, n):
            pe.wait_ge(diag_ready, n + 1)
            for tt in range(TT):
                last = mm(ps[:, 6, tt * P:tt * P + P], ones, tmp_a[:, tt * P:tt * P + P], start=True, stop=True)
            last.then_inc(row_psum, 1)

        def moving(k):
            return xg_hi[:, k, :], xg_lo[:, k, :]

        def pe_ffn(pe, i, base, norm):
            S = ffn_sems[i]
            k0 = base

            def up(f, s, first=False, between=None):
                sl = (base + s) % 2
                pe.wait_ge(lo_ready, k0 + f + 1)
                if not (isinstance(f, int) and f < 2):
                    pe.wait_ge(S["value_scaled"], f - 1)
                before = (lambda k: pe.wait_ge(g_lo, KD * norm + k + 1)) if first else None
                three_pass(ps[:, 2 * s, :], [(wtile(sl, k * P), moving(k)) for k in range(KD)], before)
                if between:
                    between()
                last = three_pass(ps[:, 2 * s + 1, :], [(wtile(sl, (KD + k) * P), moving(k)) for k in range(KD)])
                last.then_inc(S["unit_done"], 1)

            def down(m0, it=0, first=False):
                bank = ps[:, 4 + m0 % 2, :]
                v = KD * (norm + 1) + m0 + it
                if not first:
                    pe.wait_ge(x_new, v - 1)
                for h in range(2):
                    sl = (base + h) % 2
                    pe.wait_ge(lo_ready, k0 + FT + 2 * (m0 + it) + h + 1)
                    if first:
                        pe.wait_ge(S["prod_lo"], (h + 1) * HALF)
                    for t in range(HALF):
                        (ah, al), f = wtile(sl, t * P), h * HALF + t
                        mm(bank, ah, p_hi[:, f, :], start=(f == 0), stop=False)
                        mm(bank, ah, p_lo[:, f, :], start=False, stop=False)
                        last = mm(bank, al, p_hi[:, f, :], start=False, stop=(f == FT - 1))
                    last.then_inc(S["unit_done"], 1)

            up(0, 0, True, between=lambda: pe_col(pe, norm))
            up(1, 1, between=lambda: pe_row(pe, norm))
            with pe.Fori(1, FT // 2) as it:
                for s in range(2):
                    up(2 * it + s, s)
            down(0, 0, True)
            down(1, 0, True)
            with pe.Fori(1, KD // 2) as it:
                for ml in range(2):
                    down(ml, 2 * it)

        def pe_chunk(pe, c):
            kind, u, i, name = CH[c]
            sl = (MIX0 + u) % 2
            bank = ps[:, bank_of(c), :]
            if bank_of(c) == 7:
                pe.wait_ge(proj_read, c)
                pe.wait_ge(rope_done, sum(i < c for i in ROPED))
            elif c >= 4:
                pe.wait_ge(proj_read, c - 3)
            if kind == "t":
                before = (lambda k: pe.wait_ge(g_lo, KD + k + 1)) if c == 0 else None
                pairs = [(wtile(sl, (i * KD + k) * P), moving(k)) for k in range(KD)]
                last = three_pass(bank, pairs, before)
            else:
                def wm(t, k):
                    return t[:, sl, :].rearrange("p (i k r) -> p i k r", i=2, k=KD)[:, :, k, :]
                ts = slice(i * P, i * P + P)
                out_ = bank[:, 0:256].rearrange("p (i r) -> p i r", i=2)
                last = three_pass(out_, [((xg_hi[:, k, ts], xg_lo[:, k, ts]), (wm(w_hi, k), wm(w_lo, k)))
                                         for k in range(KD)])
            last.then_inc(proj_psum, 1)

        def pe_swap(pe, c):
            r = ROPED.index(c)
            pe.wait_ge(proj_read, c + 1)
            if r >= 2:
                pe.wait_ge(rope_done, r - 1)
            mm(ps[:, swap_bank(c), :], swap_perm, pool[:, slot_of[CH[c][3]], :], start=True, stop=True).then_inc(swap_psum, 1)

        def pe_scores(pe, n):
            it, b = ITEMS[n], 2 * (n % 2)
            if n >= 2:
                pe.wait_ge(exp_ready, n - 1)
            if it[0] == "cmp":
                _, hh, g = it
                rows = slice(g * DH, g * DH + DH)
                for qt in range(TT):
                    mm(ps[:, b, qt * P:qt * P + P], pool[rows, Q_RAW + hh, qt * P:qt * P + P], k_cmp[rows, :],
                       start=True, stop=False)
                    last = mm(ps[:, b, qt * P:qt * P + NC], ident_b, cmp_b[:, qt * NC:qt * NC + NC],
                              start=False, stop=True)
                last.then_inc(scores_psum, 1)
                return
            if it[0] == "nsa":
                _, hh, g, qt = it
                rows, nk = slice(g * DH, g * DH + DH), (qt + 1) * P
                for i, keys in enumerate((KS, KW)):
                    mm(ps[:, b + i, 0:nk], pool[rows, Q_ROPE + hh, qt * P:qt * P + P], pool[rows, keys, 0:nk],
                       start=True, stop=False)
                    last = mm(ps[:, b + i, nk - P:nk], ident_b, causal_b, start=False, stop=True)
                last.then_inc(scores_psum, 1)
                return
            _, hp, hl, qt = it
            rows, nk = slice(hl * DH, hl * DH + DH), (qt + 1) * P
            if n == N_NSA:
                pe.wait_ge(rope_done, len(ROPED))
            for i in range(2):
                mm(ps[:, b + i, 0:nk], pool[rows, QD[hp] + 1 + i, qt * P:qt * P + P],
                   pool[rows, KDS[hp] + 1 + i, 0:nk], start=True, stop=False)
                one_hot, other = residue(i)
                mm(ps[:, b + i, 0:nk], one_hot, other[:, 0:nk], start=False, stop=False)
                mm(ps[:, b + i, nk - P:nk], ident_b, causal_b, start=False, stop=True)

        def pe_near_scores(pe, n):
            if n < N_NSA:
                return
            _, hp, hl, qt = ITEMS[n]
            rows, nk, k0 = slice(hl * DH, hl * DH + DH), (qt + 1) * P, max(qt - 1, 0) * P
            if n == N_NSA:
                pe.wait_ge(rope_done, len(ROPED))
            else:
                pe.wait_ge(exp_ready, n)
            n0 = nk - k0
            mm(ps[:, 7, 0:n0], pool[rows, QD[hp], qt * P:qt * P + P], pool[rows, KDS[hp], k0:nk], start=True, stop=False)
            if qt:
                mm(ps[:, 7, 0:P], ident_b, prev_b, start=False, stop=False)
            mm(ps[:, 7, n0 - P:n0], ident_b, causal_b, start=False, stop=True).then_inc(scores_psum, 1)

        def pe_transpose_probs(pe, n):
            it, e = ITEMS[n], n % 2
            pe.wait_ge(scaled_ready, n + 1)
            if n:
                pe.wait_ge(pt_act, n)
                pe.wait_ge(pt_dve, n)
            if n > N_NSA:
                pe.wait_ge(pt_near, n - N_NSA)
            if it[0] == "cmp":
                for qt in range(TT):
                    last = nc.tensor.transpose(ps[0:NC, 4 + qt // 2, qt * P:qt * P + P],
                                               probs[:, e, qt * NC:qt * NC + NC], ident)
                last.then_inc(trans_psum, 1)
                return
            qt = it[3]
            for i in range(2):
                for kt in range(qt + 1):
                    last = nc.tensor.transpose(ps[:, 4 + i, kt * P:kt * P + P],
                                               probs[:, e, i * T + kt * P:i * T + kt * P + P], ident)
            last.then_inc(trans_psum, 1)

        def pe_transpose_near(pe, n):
            if n < N_NSA:
                return
            it, e = ITEMS[n], n % 2
            pe.wait_ge(pt_act, n + 1)
            for kt in range(min(it[3] + 1, 2)):
                last = nc.tensor.transpose(ps[:, 4, kt * P:kt * P + P],
                                           probs[:, e, 2 * T + kt * P:2 * T + kt * P + P], ident)
            last.then_inc(near_psum, 1)

        def pe_values(pe, n):
            it, e = ITEMS[n], n % 2
            pe.wait_ge(pt_act, n + 1)
            pe.wait_ge(pt_dve, n + 1)
            if n >= N_NSA:
                pe.wait_ge(pt_near, n - N_NSA + 1)
            pair = n // 10 if n < N_NSA else 4 + (n - N_NSA) // 8
            if pair:
                pe.wait_ge(y_read, pair)
            if it[0] == "cmp":
                g = it[2]
                mm(ps[g * DH:g * DH + DH, 6, :], v_cmp[:, g, :], probs_t[0:NC, e, 0:T],
                   start=True, stop=False).then_inc(pv_psum, 1)
                return
            if it[0] == "nsa":
                _, hh, g, qt = it
                out_ = ps[g * DH:g * DH + DH, 6, qt * P:qt * P + P]
                for i in range(2):
                    for kt in range(qt + 1):
                        last = mm(out_, v_nsa[:, kt, i, g * DH:g * DH + DH],
                                  probs_t[:, e, i * T + kt * P:i * T + kt * P + P],
                                  start=False, stop=(i == 1 and kt == qt and qt == TT - 1))
                last.then_inc(pv_psum, 1)
                return
            _, hp, hl, qt = it
            out_ = ps[hl * DH:hl * DH + DH, 6, qt * P:qt * P + P]
            cols = slice(hp * P + hl * DH, hp * P + hl * DH + DH)
            terms = [(1 + i, kt, i * T + kt * P) for i in range(2) for kt in range(qt + 1)]
            terms += [(0, max(qt - 1, 0) + i, 2 * T + i * P) for i in range(min(qt + 1, 2))]
            for j, (g, kt, at) in enumerate(terms):
                last = mm(out_, v_dil[:, kt, g, cols], probs_t[:, e, at:at + P], start=(j == 0), stop=(j == len(terms) - 1))
            last.then_inc(pv_psum, 1)

        def pe_attend(pe, a, b):
            pe_scores(pe, a)
            pe_near_scores(pe, a)
            pe_scores(pe, a + 1)
            pe_near_scores(pe, a + 1)
            for n in range(a, b):
                pe_transpose_probs(pe, n)
                if n + 2 < b:
                    pe_scores(pe, n + 2)
                pe_transpose_near(pe, n)
                if n > a:
                    pe_values(pe, n - 1)
                if n + 2 < b:
                    pe_near_scores(pe, n + 2)
                kind, c = FILL.get(n, (None, None))
                if kind == "chunk":
                    pe.wait_ge(lo_ready, MIX0 + CH[c][1] + 1)
                    pe_chunk(pe, c)
                elif kind == "swap":
                    pe_swap(pe, c)
            pe_values(pe, b - 1)

        @block.tensor
        def _(pe):
            pe.wait_ge(const_landed, 16)
            pe.wait_ge(vec_landed, 16 * 5)
            nc.tensor.transpose(ps[:, 7, 0:64], vec_rows[:, :], ident[0:64, 0:64]).then_inc(gains_psum, 1)
            pe.wait_ge(x_landed, 16 * TT)
            for m in range(KD):
                if m == KD - 1:
                    pe.wait_ge(gains_ready, 1)
                for tt in range(TT):
                    last = nc.tensor.transpose(ps[:, m, tt * P:tt * P + P], x_nat[:, tt, m * P:m * P + P], ident)
                last.then_inc(xt_psum, 1)
            pe_ffn(pe, 0, 0, 0)
            swaps = []

            def swap_flush(upto):
                while swaps and swaps[0] < upto:
                    pe_swap(pe, swaps.pop(0))

            for step in STEPS:
                if step[0] == "chunk":
                    c = step[1]
                    pe.wait_ge(lo_ready, MIX0 + CH[c][1] + 1)
                    pe_chunk(pe, c)
                    if c >= 4:
                        swap_flush(c)
                    if c in ROPED:
                        swaps.append(c)
                elif step[0] == "rstd":
                    pe_col(pe, 1)
                elif step[0] == "row":
                    pe_row(pe, 1)
                elif step[0] == "gates":
                    pe.wait_ge(gate_ready, 1)
                    pe.wait_ge(row_ready, 2)
                    for tt in range(TT):
                        last = nc.tensor.transpose(ps[:, 6, tt * 24:tt * 24 + 24], probs[0:24, 0, tt * P:tt * P + P],
                                                   ident[0:24, 0:24])
                    last.then_inc(gatet_psum, 1)
                elif step[0] == "hidden":
                    pe.wait_ge(tok_ready, 1)
                    pe.wait_ge(var_ready, 2)
                    pe.wait_ge(w1_landed, 32)
                    for kv in range(2):
                        for p in range(16):
                            last = mm(ps[0:DH, 7, kv * P:kv * P + P], probs_t[:, kv, p * DH:p * DH + DH],
                                      cmp_w1_tiles[kv][:, p, :], start=(p == 0), stop=(p == 15))
                        last.then_inc(hidden_psum, 1)
                elif step[0] == "hidden_t":
                    pe.wait_ge(hid_ready, 2)
                    for kv in range(2):
                        last = nc.tensor.transpose(ps[:, 7, 256 + kv * DH:256 + kv * DH + DH], hid[:, kv, :],
                                                   ident[0:DH, 0:DH])
                    last.then_inc(hidt_psum, 1)
                elif step[0] == "cmp_kv":
                    pe.wait_ge(hidt_ready, 1)
                    pe.wait_ge(small_landed, 16 * 2)
                    for g in range(2):
                        mm(ps[g * DH:g * DH + DH, 7, 384:384 + NC], w2[:, 0, :], hid_t[:, 0, g * NC:g * NC + NC],
                           start=True, stop=True)
                    for g in range(2):
                        last = mm(ps[0:NC, 7, g * DH:g * DH + DH], hid_t[:, 1, g * NC:g * NC + NC], w2[:, 1, :],
                                  start=True, stop=True)
                    last.then_inc(cmp_psum, 1)
                elif step[0] == "rope_rest":
                    swap_flush(len(CH))
                    pe.wait_ge(proj_read, N_CH1)
                    pe.wait_ge(rope_done, sum(c < N_CH1 for c in ROPED))
                    pe.wait_ge(gatet_ready, 1)
                    pe.wait_ge(cmp_ready, 1)
                elif step[0] == "attend":
                    if step[1] == 0:
                        pe.wait_ge(small_landed, 16 * 2)
                    pe_attend(pe, step[1], step[2])
            pe.wait_ge(exp_ready, len(ITEMS))
            pe.wait_ge(pt_act, len(ITEMS))
            pe.wait_ge(pt_dve, len(ITEMS))
            pe.wait_ge(y_read, 6)
            for m in range(KD):
                g0, b0 = merge_banks(m)
                for u in merge_units_before(m):
                    j = MIX0 + u
                    pe.wait_ge(lo_ready, j + 1)
                    if u == U_GM[m]:
                        if m >= 2:
                            pe.wait_ge(gm_scaled, m - 1)
                        three_pass(ps[:, g0, :], [(wtile(j % 2, k * P), moving(k)) for k in range(KD)])
                        last = three_pass(ps[:, g0 + 1, :], [(wtile(j % 2, (KD + k) * P), moving(k)) for k in range(KD)])
                        last.then_inc(gm_psum, 1)
                        continue
                    for ml in range(2):
                        b0 = merge_banks(m + ml)[1]
                        if m:
                            pe.wait_ge(merge_read, m + ml - 1)
                        else:
                            pe.wait_ge(y_lo_ready, 6)
                        three_pass(ps[:, b0, :], [(wtile(j % 2, c * 256 + ml * P), (y_hi[:, c, :], y_lo[:, c, :]))
                                                  for c in range(4)])
                        last = three_pass(ps[:, b0 + 1, :], [(wtile(j % 2, c * 256 + ml * P), (y_hi[:, c, :], y_lo[:, c, :]))
                                                             for c in range(4, 6)])
                        last.then_inc(br_psum, 1)
            for m in range(KD):
                j = MIX0 + U_WO[m // 2]
                pe.wait_ge(lo_ready, j + 1)
                if m < 2:
                    pe.wait_ge(merge_read, KD)
                else:
                    pe.wait_ge(x_new, 2 * KD + m - 1)
                before = (lambda k: pe.wait_ge(m_lo, k + 1)) if m == 0 else None
                three_pass(ps[:, 4 + m % 2, :], [(wtile(j % 2, k * 256 + (m % 2) * P), (merged_hi[:, k, :], merged_lo[:, k, :]))
                                                 for k in range(KD)], before).then_inc(wo_psum, 1)
            pe_ffn(pe, 1, FFN2, 2)
            pe_col(pe, 3)
            pe.wait_ge(z_ready, KD)
            pe.wait_ge(var_ready, 4)
            for tt in range(TT):
                for m in range(KD):
                    last = nc.tensor.transpose(ps[:, 2 * tt + m // 4, (m % 4) * P:(m % 4) * P + P],
                                               xT[:, m, tt * P:tt * P + P], ident)
                last.then_inc(fin_psum, 1)


_INS = ["x", "positions", "norm_ffn1", "ffn1_w_in", "ffn1_w_out", "norm_mix", "w_in", "cmp_pos", "cmp_w1",
        "cmp_w2", "w_branch_nsa", "w_branch_dil", "w_out", "norm_ffn2", "ffn2_w_in", "ffn2_w_out", "norm_final"]


def kernel(**inputs):
    import concourse.bacc as bacc
    from concourse.bass_utils import run_bass_kernel_spmd

    nc = bacc.Bacc("TRN2", target_bir_lowering=False, num_devices=1)
    arrays, args = {}, []

    def give(name, a):
        arrays[name] = a
        args.append(nc.dram_tensor(name, a.shape, mybir.dt.from_np(a.dtype), kind="ExternalInput").ap())

    for name in _INS:
        give(f"in_{name}", np.ascontiguousarray(inputs[name]))
    f, b = shape_constants()
    give("shape_constants", f)
    give("shape_masks", b)
    args.append(nc.dram_tensor("out_0", (1, T, D), F32, kind="ExternalOutput").ap())
    build(nc, *args)
    r = run_bass_kernel_spmd(nc, [arrays], core_ids=[0])
    return r.results[0]["out_0"]
```

```python
from contextlib import ExitStack

import numpy as np

import concourse.bass as bass
from concourse import mybir

ALU = mybir.AluOpType
ACT = mybir.ActivationFunctionType
AX = mybir.AxisListType
F32 = mybir.dt.float32
F32R = mybir.dt.float32r
BF16 = mybir.dt.bfloat16
I32 = mybir.dt.int32

P = 128
T = 512
D = 1024
FF = 2816
TT = T // P
KD = D // P
FT = FF // P
HALF = FT // 2
DH = 64
HPG = 4
NCMP = 31
NC = 32
KCOL = 512
GCOL = KCOL + 6 * P
DCOL = GCOL + 24
DW = 3 * 256
MCOL = DCOL + 3 * DW
SCALE = DH ** -0.5
EPS = 1e-6
BIG = 2.0 ** 100
THETA = 500000.0
TWO_PI = (6.28125, 0.0019350051879882812, 3.0199159819e-07)
MAGIC = 12582912.0
CLS = 4
BAND = T + CLS - 1
SLOT = 16 * P
NG = 24
VCOL = 2 * P + NG


def shape_constants():
    f = np.zeros((P, 2 * P + 4), np.float32)
    f[:, 0:P] = np.eye(P)
    f[:, P:2 * P] = 1.0
    for head in range(2):
        for i in range(8):
            freq = np.float32(THETA) ** np.float32(-2 * i / 16)
            f[head * DH + i, 2 * P] = -freq
            f[head * DH + 8 + i, 2 * P] = freq
    q = np.arange(P)[:, None]
    k = np.arange(P)[None, :]
    b = np.zeros((P, 4 * P + BAND), np.float32)
    b[:, 0:P] = np.eye(P)
    b[:, P:2 * P] = np.where(k <= q, 0, -BIG)
    b[:, 2 * P:3 * P] = np.where((k <= q) & ((q - k) % 4 == 0), 0, -BIG)
    n = np.arange(NC)[None, :]
    for qt in range(TT):
        ok = (n * 16 + 31 <= qt * P + q) & (n < NCMP)
        b[:, 3 * P + qt * NC:3 * P + (qt + 1) * NC] = np.where(ok, 0, -BIG)
    back = 4 * q - (np.arange(BAND)[None, :] - 3)
    b[:, 4 * P:] = np.where((back >= 0) & (back <= P), 0, -BIG)
    return f, b


def build(nc, x, positions, norm_ffn1, ffn1_w_in, ffn1_w_out, norm_mix, w_in, cmp_pos, cmp_w1, cmp_w2,
          w_branch_nsa, w_branch_dil, w_out, norm_ffn2, ffn2_w_in, ffn2_w_out, norm_final,
          consts, masks, out):
    outer = ExitStack()
    with outer:
        def sem(name):
            return outer.enter_context(nc.semaphore(name))

        def sb(name, shape, dt=F32, scope=outer):
            return scope.enter_context(nc.sbuf_tensor(name, shape, dt))

        xT = sb("xT", [P, KD, T])
        xg_hi = sb("xg_hi", [P, KD, T], F32R)
        xg_lo = sb("xg_lo", [P, KD, T], F32R)
        w_raw = sb("w_raw", [P, 2, KD * VCOL])
        w_hi = sb("w_hi", [P, 2, KD * VCOL], F32R)
        w_lo = sb("w_lo", [P, 2, KD * VCOL], F32R)
        rstd_row = sb("rstd_row", [P, T])
        rstd_col = sb("rstd_col", [P, TT + CLS])
        cos_t = sb("cos_t", [P, T])
        sin_t = sb("sin_t", [P, T])
        sumsq = sb("sumsq", [P, T])
        square = sb("square", [P, 2, T])
        tmp_a = sb("tmp_a", [P, T])
        tmp_b = sb("tmp_b", [P, T])
        const = sb("const", [P, 2 * P + 4])
        vec_rows = sb("vec_rows", [64, P])
        vec_cols = sb("vec_cols", [P, 64])
        warm = sb("warm", [P, 1])
        norm_s = sb("norm_s", [P, 4, TT + CLS])
        gains = vec_cols[:, 0:32].rearrange("p (n m) -> p n m", n=4)
        pos_t = vec_cols[:, 32:64].rearrange("p (v j) -> p v j", v=2)
        ident = const[:, 0:P]
        ones = const[:, P:2 * P]
        freq = const[:, 2 * P:2 * P + 1]

        with ExitStack() as scope:
            x_nat = sb("x_nat", [P, TT, D], F32, scope)
        with ExitStack() as scope:
            p_hi = sb("p_hi", [P, FT, T], F32R, scope)
            p_lo = sb("p_lo", [P, FT, T], F32R, scope)
        y_scope = ExitStack()
        y = sb("y", [P, 6, T], F32, y_scope)
        with ExitStack() as scope:
            pool = sb("pool", [P, 16, T], F32, scope)
            v_nsa = sb("v_nsa", [P, TT, 2, P], F32, scope)
            v_dil = sb("v_dil", [P, TT, 3, 256], F32, scope)
            k_cmp = sb("k_cmp", [P, P], F32, scope)
            v_cmp = sb("v_cmp", [NC, 2, DH], F32, scope)
            probs = sb("probs", [P, 2, 2 * T], F32, scope)
            probs_t = sb("probs_t", [P, 2, 2 * T], F32, scope)
            gates = sb("gates", [P, TT, 24], F32, scope)
            stat = sb("stat", [P, 2, 4, 4], F32, scope)
            mask = sb("mask", [P, 4 * P + BAND], BF16, scope)
            w2 = sb("w2", [P, 2, DH], F32, scope)
            hid = sb("hid", [DH, 2, P], F32, scope)
            hid_t = sb("hid_t", [P, 2, DH], F32, scope)
        with ExitStack() as scope:
            slots = [sb(f"slot_{i}", [P, T], F32R, scope) for i in range(28)]
        y_parts = [(slots[10 + c], slots[i]) for c, i in enumerate((3, 7, 8, 9, 16, 17))]
        merged = [(slots[18 + m], slots[i]) for m, i in enumerate((0, 1, 2, 4, 5, 6, 26, 27))]
        y_scope.close()
        cmp_w1_tiles = [probs[:, :, :].rearrange("p a c -> p (a c)").rearrange("p (j h) -> p j h", h=P),
                        v_dil[:, :, :, :].rearrange("p a b c -> p (a b c)")[:, 0:SLOT].rearrange("p (j h) -> p j h", h=P)]
        ident_b = mask[:, 0:P]
        causal_b = mask[:, P:2 * P]
        class_b = mask[:, 2 * P:3 * P]
        band_b = mask[:, 4 * P:4 * P + BAND]
        cmp_b = mask[:, 3 * P:4 * P]

        def of_class(t, r):
            return t.rearrange("p (i r) -> p r i", r=CLS)[:, r, :]

        ps = outer.enter_context(nc.psum_tensor("ps", [P, 8, T], F32))

        def ktiles(w):
            return w.rearrange("(k p) c -> p k c", p=P)

        win = ktiles(w_in[0])
        MU = []

        def columns(cols, c):
            MU.append((c * len(cols) * KD, [((i * KD * c, KD, c), win[:, :, at:at + c])
                                            for i, at in enumerate(cols)], True))
            return len(MU) - 1

        U_CTOK = columns([KCOL, KCOL + P], P)
        U_K = columns([KCOL + 2 * P, KCOL + 4 * P], P)
        MU.append((KD * VCOL, [((0, KD, VCOL), win[:, :, at:at + c], 0, to)
                               for at, c, to in ((KCOL + 3 * P, P, 0), (KCOL + 5 * P, P, P), (GCOL, NG, 2 * P))], True))
        U_V = len(MU) - 1
        U_Q = []
        wq = win[:, :, 0:KCOL].rearrange("p k (g c) -> p k g c", g=2)
        for u in range(2):
            MU.append((SLOT, [((i * KD * P, KD, P), wq[:, :, g, (2 * u + i) * DH:(2 * u + i + 1) * DH], 0, g * DH)
                              for i in range(2) for g in range(2)], True))
            U_Q.append(len(MU) - 1)
        U_VD = [columns([DCOL + 2 * DW + g * 256, DCOL + 2 * DW + g * 256 + P], P) for g in range(3)]
        U_QK = [[columns([DCOL + g * 256 + hp * P, DCOL + DW + g * 256 + hp * P], P) for g in range(3)]
                for hp in range(2)]
        nsa_w = w_branch_nsa[0].rearrange("(g h d) c -> g d h c", g=2, d=DH)
        dil_w = ktiles(w_branch_dil[0])
        U_GM, U_BR = {}, {}

        def gate_unit(m):
            if m < KD:
                U_GM[m] = columns([MCOL + m * P, MCOL + D + m * P], P)

        gate_unit(0)
        gate_unit(1)
        for mm in range(KD // 2):
            gate_unit(2 * mm + 2)
            cs = slice(mm * 256, mm * 256 + 256)
            MU.append((6 * 256, [((0, 4, 256), nsa_w[0][:, :, cs], 0), ((0, 4, 256), nsa_w[1][:, :, cs], DH),
                                 ((1024, 2, 256), dil_w[:, :, cs])], True))
            U_BR[mm] = len(MU) - 1
            gate_unit(2 * mm + 3)
        wo = ktiles(w_out[0])
        U_WO = []
        for mm in range(KD // 2):
            cs = slice(mm * 256, mm * 256 + 256)
            MU.append((SLOT, [((h * 1024, 4, 256), wo[:, 4 * h:4 * h + 4, cs]) for h in range(2)], True))
            U_WO.append(len(MU) - 1)

        FU = FT + 2 * KD
        MIX0 = FU
        FFN2 = MIX0 + len(MU)
        N_UNITS = FFN2 + FU
        landed_at = []
        total = [0, 0]
        for j in range(N_UNITS):
            n = len(MU[j - MIX0][1]) if MIX0 <= j < FFN2 else 2
            total[j % 2] += 16 * n
            landed_at.append(total[j % 2])

        landed = [sem("weights_landed_0"), sem("weights_landed_1")]
        hi_ready = sem("weight_hi_ready")
        lo_ready = sem("weight_lo_ready")
        w1_landed = sem("cmp_w1_landed")
        hidden_psum = sem("cmp_hidden_in_psum")
        const_landed = sem("const_landed")
        vec_landed = sem("gains_and_cmp_pos_landed")
        x_landed = [sem(f"x_features_landed_{h}") for h in range(2)]
        gains_psum = sem("gains_in_psum")
        gains_ready = sem("gains_ready")
        pos_landed = sem("positions_landed")
        small_landed = sem("mixer_constants_landed")
        tokens_landed = sem("shifted_tokens_landed")
        out_landed = sem("out_landed")
        xt_psum = sem("x_transposed_in_psum")
        x_new = sem("residual_ready")
        g_hi = sem("xg_hi_ready")
        g_lo = sem("xg_lo_ready")
        sq_ready = sem("square_ready")
        acc_done = sem("square_added")
        col_psum = sem("mean_square_in_psum")
        var_ready = sem("variance_ready")
        std_ready = sem("std_ready")
        diag_ready = sem("rstd_diagonal_ready")
        row_psum = sem("rstd_row_in_psum")
        row_ready = sem("rstd_row_ready")
        dve_chain = sem("vector_step")
        rope_args = sem("rope_arguments_ready")
        rope_sines = sem("rope_sines_ready")
        ffn_sems = [{n: sem(f"ffn{i}_{n}") for n in
                     ("unit_done", "gate_scaled", "value_scaled", "silu_ready", "prod_ready", "prod_hi",
                      "prod_lo")} for i in range(2)]
        proj_psum = sem("projection_in_psum")
        proj_read = sem("projection_read")
        swap_landed = sem("rope_pairs_swapped")
        sin_ready = sem("rope_sin_part_ready")
        cos_ready = sem("rope_cos_part_ready")
        rope_done = sem("rope_done")
        padded = sem("padding_cleared")
        tok_ready = sem("cmp_tokens_ready")
        hid_ready = sem("cmp_hidden_ready")
        hidt_psum = sem("cmp_hidden_t_in_psum")
        hidt_ready = sem("cmp_hidden_t_ready")
        cmp_psum = sem("cmp_kv_in_psum")
        cmp_ready = sem("cmp_kv_ready")
        gate_ready = sem("gates_ready")
        scores_psum = sem("scores_in_psum")
        bias_ready = sem("minus_max_ready")
        exp_ready = sem("exp_ready")
        factor_ready = sem("factor_ready")
        scaled_ready = sem("probs_scaled")
        trans_psum = sem("probs_t_in_psum")
        pt_act = sem("probs_t_copied_by_scalar")
        pt_dve = sem("probs_t_copied_by_vector")
        pv_psum = sem("pv_in_psum")
        y_read = sem("y_read")
        y_hi_ready = sem("y_hi_ready")
        y_lo_ready = sem("y_lo_ready")
        gm_psum = sem("merge_gate_in_psum")
        br_psum = sem("branches_in_psum")
        gm_scaled = sem("merge_gate_scaled")
        sig_ready = sem("merge_gate_ready")
        merge_read = sem("merge_banks_read")
        merged_ready = sem("merged_ready")
        m_hi = sem("merged_hi_ready")
        m_lo = sem("merged_lo_ready")
        wo_psum = sem("w_out_in_psum")
        z_ready = sem("final_gained")
        fin_psum = sem("final_in_psum")
        fin_act = sem("final_by_scalar")
        fin_dve = sem("final_by_vector")

        ITEMS = []
        for hh in range(HPG):
            for g in range(2):
                ITEMS.append(("cmp", hh, g))
                ITEMS += [("nsa", hh, g, qt) for qt in range(TT)]
        N_NSA = len(ITEMS)
        for hp in range(2):
            for hl in range(2):
                ITEMS += [("dil", hp, hl, r) for r in range(CLS)]

        def ends_pair(n):
            if n < N_NSA:
                return n // 10 if n % 10 == 9 else None
            return 4 + (n - N_NSA) // 8 if (n - N_NSA) % 8 == 7 else None

        Q_ROPE, Q_RAW, KS, KW = 0, 4, 8, 9
        QD = [10, 0]
        KDS = [13, 4]

        CH = [("t", U_CTOK, 0, "tok0"), ("t", U_CTOK, 1, "tok1"), ("t", U_K, 0, "ks"), ("t", U_K, 1, "kw")]
        CH += [("n", U_V, tt, "v") for tt in range(TT)]
        CH += [("t", U_Q[u], i, f"q{2 * u + i}") for u in range(2) for i in range(2)]
        N_CH1 = len(CH)
        CH += [("n", U_VD[g], tt, f"vd{g}") for g in range(3) for tt in range(TT)]
        CH += [("t", U_QK[0][g], i, f"{'qk'[i]}d0{g}") for g in range(3) for i in range(2)]
        N_CH2 = len(CH)
        CH += [("t", U_QK[1][g], i, f"{'qk'[i]}d1{g}") for g in range(3) for i in range(2)]
        N_CH3 = len(CH)
        CH += [("t", U_GM[m], i, f"gm{2 * m + i}") for m in range(2) for i in range(2)]
        slot_of = {"tok0": 10, "tok1": 11, "ks": KS, "kw": KW}
        slot_of |= {f"q{i}": Q_RAW + i for i in range(4)}
        slot_of |= {f"{'qk'[i]}d{hp}{g}": (QD, KDS)[i][hp] + g for i in range(2) for hp in range(2) for g in range(3)}
        roped_slot = {n: (Q_ROPE + int(n[1]) if n[0] == "q" and len(n) == 2 else s)
                      for n, s in slot_of.items() if not n.startswith("tok")}
        ROPED = [c for c, ch in enumerate(CH) if ch[3] in roped_slot]
        last_chunk = {}
        for c, ch in enumerate(CH):
            last_chunk[ch[1]] = c

        def final_view(tt):
            return w_raw[:, tt // 2, (tt % 2) * D:(tt % 2) * D + D]

        def tile_of(t, m):
            return t[:, bass.ds(m, 1), :].rearrange("p a t -> p (a t)")

        def before_in_slot(j):
            return j - 2

        def release(j):
            if j < MIX0:
                return ffn_sems[0]["unit_done"], j + 1
            if j >= FFN2:
                return ffn_sems[1]["unit_done"], j - FFN2 + 1
            u = j - MIX0
            if u in last_chunk:
                return proj_psum, last_chunk[u] + 1
            for m, unit in U_GM.items():
                if u == unit:
                    return gm_psum, m - 1
            for m2, unit in U_BR.items():
                if u == unit:
                    return br_psum, 2 * m2 + 2
            return wo_psum, 2 * U_WO.index(u) + 2

        def width_of(j):
            if MIX0 <= j < FFN2:
                return MU[j - MIX0][0]
            return SLOT if j - (FFN2 if j >= FFN2 else 0) < FT else HALF * P

        def ends_unit(c):
            return last_chunk[CH[c][1]] == c

        def chunks(a, b):
            return [("chunk", c) for c in range(a, b)]

        N_PRE = N_CH1 + 1
        C_V, C_Q = 4, 8
        STEPS = [("first_chunks",), ("chunk", 2, (0, KD // 2)), ("rstd",), ("chunk", 2, (KD // 2, KD)),
                 ("chunk", 3, (0, KD // 2)), ("row",), ("chunk", 3, (KD // 2, KD))]
        STEPS += chunks(C_V, C_Q + 1) + [("gates",), ("chunk", C_Q + 1), ("hidden",), ("chunk", C_Q + 2),
                                         ("hidden_t",), ("chunk", C_Q + 3), ("cmp_kv",)] + chunks(N_CH1, N_PRE) + [("read_rest",),
                                         ("attend", 0, len(ITEMS))]
        def pieces_of(c):
            k = KD // 2 if CH[c][0] == "n" else KD // 4
            return [(c, at, at + k) for at in range(0, KD, k)]

        PIECES = [piece for c in range(N_PRE, len(CH)) for piece in pieces_of(c)]
        N_QKV = sum(c < N_CH3 for c, _, _ in PIECES)
        QKV_STEPS, LAST_STEP = N_NSA + 2, len(ITEMS) - 2
        FILL, done = {}, 0
        for n in range(-1, len(ITEMS)):
            if done == len(PIECES):
                break
            goal = (N_QKV * n / QKV_STEPS if n <= QKV_STEPS else
                    N_QKV + (len(PIECES) - N_QKV) * (n - QKV_STEPS) / (LAST_STEP - QKV_STEPS))
            two = n == -1 or done + 1.5 < goal or (n < N_NSA and n % 5 == 2)
            took = [piece for piece in PIECES[done:done + 1 + two] if piece[0] == PIECES[done][0]]
            FILL[n] = (took[0][0], (took[0][1], took[-1][2]))
            done += len(took)

        def filled(n):
            c, part = FILL.get(n, (0, (0, 0)))
            return c if part[1] == KD else None

        def fill_of(c):
            return [n for n, (cc, _) in FILL.items() if cc == c]

        assert done == len(PIECES) and max(fill_of(N_CH2 - 1)) < N_NSA - 2 and max(fill_of(N_CH3 - 1)) < N_NSA + 5 \
            and max(FILL) < len(ITEMS) - 1
        assert max(fill_of(N_CH2)) >= 18 and max(fill_of(N_CH3 - 2)) >= 28

        def by_class(name):
            return name in ("vd1", "vd2")

        def bank_of(c):
            return c % 4 if c < N_PRE else 7

        def wo_bank(m):
            return m % 2 + (4 if m >= 4 else 0)

        def splits_y(n):
            return n - N_NSA - 9 if 0 <= n - N_NSA - 9 < 5 else None

        def merge_banks(m):
            return ((7, 2), 0) if m % 2 == 0 else ((6, 3), 4)

        def gate_args(m):
            return (tmp_a[:, :], tmp_b[:, :]) if m % 2 == 0 else (square[:, 0, :], square[:, 1, :])

        block = outer.enter_context(nc.Block())

        def load(sp, j, s, pieces):
            for piece in pieces:
                (at, k, c), src = piece[0], piece[1]
                p0 = piece[2] if len(piece) > 2 else 0
                rows = src.shape[0]
                dst = w_raw[p0:p0 + rows, s, at:at + k * c].rearrange("p (k c) -> p k c", k=k)
                if len(piece) > 3:
                    dst = dst[:, :, piece[3]:piece[3] + src.shape[2]]
                sp.dma_start(dst, src).then_inc(landed[s], 16)

        def sync_ffn(sp, base, wi, wd, before=None):
            wi, wd = ktiles(wi[0]), ktiles(wd[0])
            k0 = base

            def up(i, s, wait):
                f = 2 * i + s
                if wait:
                    sp.wait_ge(lo_ready, k0 + f - 1)
                load(sp, None, (base + s) % 2,
                     [((0, KD, P), wi[:, :, bass.ds(f * P, P)]), ((KD * P, KD, P), wi[:, :, bass.ds(f * P + FF, P)])])

            for s in range(2):
                if before:
                    before(s)
                up(0, s, base > 0)
            with sp.Fori(1, FT // 2) as i:
                for s in range(2):
                    up(i, s, True)
            with sp.Fori(0, KD) as m:
                for s in range(2):
                    sp.wait_ge(lo_ready, k0 + FT + 2 * m + s - 1)
                    load(sp, None, (base + s) % 2,
                         [((0, 6, P), wd[:, s * HALF:s * HALF + 6, bass.ds(m * P, P)]),
                          ((6 * P, 5, P), wd[:, s * HALF + 6:(s + 1) * HALF, bass.ds(m * P, P)])])

        @block.sync
        def _(sp):
            xv = x[0].rearrange("(t p) d -> p t d", p=P)

            def x_half(h):
                cols = slice(h * D // 2, (h + 1) * D // 2)
                for tt in range(TT):
                    sp.dma_start(x_nat[:, tt, cols], xv[:, tt, cols]).then_inc(x_landed[h], 16)

            sync_ffn(sp, 0, ffn1_w_in, ffn1_w_out, x_half)
            for u, (_, pieces, _) in enumerate(MU):
                j = MIX0 + u
                sp.wait_ge(lo_ready, j - 1)
                load(sp, j, j % 2, pieces)
                if u == U_Q[0]:
                    sp.wait_ge(proj_read, 2)
                    for kv in range(2):
                        for par in range(2):
                            for g in range(2):
                                sp.dma_start(pool[par * DH:par * DH + DH, 12 + 2 * kv + g, 0:T - par],
                                             pool[g * DH:g * DH + DH, 10 + kv, par:T]).then_inc(tokens_landed, 16)
            sync_ffn(sp, FFN2, ffn2_w_in, ffn2_w_out)
            ov = out[0].rearrange("(t p) d -> p t d", p=P)
            for tt in range(TT):
                sp.wait_ge(fin_act, tt + 1)
                sp.wait_ge(fin_dve, tt + 1)
                sp.dma_start(ov[:, tt, :], final_view(tt)).then_inc(out_landed, 16)
            sp.wait_ge(out_landed, 16 * TT)

        def pool_squares(pe, n):
            for m in range(KD if n < 3 else KD - 1):
                v = KD * n + m
                pe.wait_ge(sq_ready, v + 1)
                if m == 0:
                    if n:
                        pe.wait_ge(col_psum, n)
                    nc.gpsimd.tensor_copy(sumsq[:, :], square[:, m % 2, :]).then_inc(acc_done, 1)
                else:
                    pe.wait_ge(acc_done, v)
                    nc.gpsimd.tensor_tensor(sumsq[:, :], sumsq[:, :], square[:, m % 2, :], ALU.add).then_inc(acc_done, 1)

        def pool_rope(pl, c):
            r = ROPED.index(c)
            x = pool[:, slot_of[CH[c][3]], :]
            pl.wait_ge(proj_read, c + 1)
            if r:
                pl.wait_ge(rope_done, r)
            for at in (0, DH):
                for i, j in ((0, 8), (8, 0)):
                    pl.dma_start(tmp_a[at + i:at + i + 8, :], x[at + j:at + j + 8, :]).then_inc(swap_landed, 16)
            nc.gpsimd.tensor_tensor(tmp_b[:, :], x, cos_t[:, :], ALU.mult).then_inc(cos_ready, 1)
            pl.wait_ge(swap_landed, 64 * (r + 1))
            nc.gpsimd.tensor_tensor(tmp_a[:, :], tmp_a[:, :], sin_t[:, :], ALU.mult).then_inc(sin_ready, 1)
            pl.wait_ge(cos_ready, r + 1)
            pl.wait_ge(sin_ready, r + 1)
            nc.gpsimd.tensor_tensor(pool[:, roped_slot[CH[c][3]], :], tmp_a[:, :], tmp_b[:, :], ALU.add).then_inc(rope_done, 1)

        @block.gpsimd
        def _(pl):
            pl.dma_start(cos_t[:, :].bitcast(I32), positions.broadcast_to([P, T])).then_inc(pos_landed, 16)
            pool_squares(pl, 0)
            pool_squares(pl, 1)
            pl.wait_ge(ffn_sems[0]["unit_done"], FU)
            pl.dma_start(mask[:, :], masks).then_inc(small_landed, 16)
            for kv, dst in enumerate(cmp_w1_tiles):
                pl.dma_start(dst, cmp_w1[0, kv].rearrange("(j q) h -> q j h", q=P)).then_inc(w1_landed, 16)
            pl.dma_start(w2[:, :, :], cmp_w2[0].rearrange("v h d -> h v d")).then_inc(small_landed, 16)
            nc.gpsimd.memset(k_cmp[:, :], 0.0)
            nc.gpsimd.memset(probs_t[:, :, :], 0.0).then_inc(padded, 1)
            for c in range(len(CH)):
                if c in ROPED:
                    pool_rope(pl, c)
            pool_squares(pl, 2)
            pool_squares(pl, 3)

        def act_split(act, j, it=0):
            s, k = j % 2, j
            if j >= N_UNITS:
                return
            act.wait_ge(landed[s], landed_at[j] + 32 * it)
            if k >= 2:
                done, value = release(before_in_slot(j))
                act.wait_ge(done, value + 2 * it)
            w = width_of(j)
            nc.scalar.activation(w_hi[:, s, 0:w], w_raw[:, s, 0:w], ACT.Copy).then_inc(hi_ready, 1)

        def act_first_hi(act, m):
            act.wait_ge(xt_psum, m + 1)
            nc.scalar.activation(xg_hi[:, m, :], ps[:, m, :], ACT.Copy, scale=gains[:, 0, m:m + 1]).then_inc(g_hi, 1)

        def act_square(act, m):
            act.wait_ge(x_new, m + 1)
            if m >= 2:
                act.wait_ge(acc_done, m - 1)
            nc.scalar.activation(square[:, m % 2, :], xT[:, m, :], ACT.Square).then_inc(sq_ready, 1)

        def act_gain(act, n, m0, it=0):
            m, v = m0 + it, KD * n + m0 + it
            act.wait_ge(x_new, v + 1)
            if KD * n + m0 >= 2:
                act.wait_ge(acc_done, v - 1)
            if n < 3:
                nc.scalar.activation(tile_of(xg_hi, m), tile_of(xT, m), ACT.Copy,
                                     scale=gains[:, n, bass.ds(m, 1)]).then_inc(g_hi, 1)
            nc.scalar.activation(square[:, m0 % 2, :], tile_of(xT, m), ACT.Square).then_inc(sq_ready, 1)
            if n == 3:
                nc.scalar.activation(tile_of(xT, m), tile_of(xT, m), ACT.Copy,
                                     scale=gains[:, n, bass.ds(m, 1)]).then_inc(z_ready, 1)

        def act_std(act, n):
            act.wait_ge(var_ready, n + 1)
            w = TT + CLS if n == 1 else TT
            nc.scalar.activation(norm_s[:, 1, 0:w], norm_s[:, 0, 0:w], ACT.Sqrt).then_inc(std_ready, 1)

        def act_ffn(act, i, base, norm):
            S = ffn_sems[i]

            def evac(f):
                act.wait_ge(S["gate_scaled"], f + 1)
                nc.scalar.activation(tmp_a[:, :], tmp_a[:, :], ACT.Silu).then_inc(S["silu_ready"], 1)
                act.wait_ge(S["prod_ready"], f + 1)
                nc.scalar.activation(tile_of(p_hi, f), tmp_b[:, :], ACT.Copy).then_inc(S["prod_hi"], 1)

            act_std(act, norm)
            act_split(act, base + 2)
            act_split(act, base + 3)
            evac(0)
            evac(1)
            with act.Fori(1, FT // 2 - 1) as it:
                for s in range(2):
                    act_split(act, base + s + 2, it)
                    evac(2 * it + s)
            for s in range(2):
                act_split(act, base + FT + s)
                evac(FT - 2 + s)
                if i == 0 and s:
                    act.wait_ge(rope_args, 1)
                    nc.scalar.activation(sin_t[:, :], sin_t[:, :], ACT.Sin, scale=0.5).then_inc(rope_sines, 1)
                    nc.scalar.activation(cos_t[:, :], cos_t[:, :], ACT.Sin).then_inc(rope_sines, 1)
            with act.Fori(0, KD // 2 - 1) as it:
                for ml in range(2):
                    act_split(act, base + FT + 2 * ml + 2, 2 * it)
                    act_split(act, base + FT + 2 * ml + 3, 2 * it)
                    act_gain(act, norm + 1, ml, 2 * it)
            for ml in range(2):
                for h in range(2):
                    act_split(act, base + FU - 2 + 2 * ml + h)
                act_gain(act, norm + 1, KD - 2 + ml)
                if ml == 0:
                    nc.scalar.activation(warm[:, :], ones[:, 0:1], ACT.Sqrt)

        def act_exp(act, n):
            it, e, b = ITEMS[n], n % 2, 2 * (n % 2)
            act.wait_ge(bias_ready, n + 1)
            if n >= 2:
                act.wait_ge(trans_psum, n - 1)
            if it[0] == "cmp":
                nc.scalar.activation(probs[:, e, 0:P], probs[:, e, 0:P], ACT.Exp, scale=SCALE).then_inc(exp_ready, 1)
                return
            nk = (it[3] + 1) * P
            parts = [(0, nk, 0), (1, nk, 1)] if it[0] == "nsa" else [(0, T, 0), (1, 2 * P, 0)]
            for i, w, m in parts:
                last = nc.scalar.activation(probs[:, e, i * T:i * T + w], ps[:, b + i, 0:w], ACT.Exp,
                                            bias=stat[:, e, 1, m:m + 1], scale=SCALE,
                                            accum_out=stat[:, e, 2, i:i + 1])
            last.then_inc(exp_ready, 1)

        def act_copy_probs(act, n):
            it, e = ITEMS[n], n % 2
            act.wait_ge(trans_psum, n + 1)
            if n >= 2:
                act.wait_ge(pv_psum, n - 1)
            if it[0] == "cmp":
                nc.scalar.activation(probs_t[0:NC, e, 0:256], ps[0:NC, 4, 0:256], ACT.Copy).then_inc(pt_act, 1)
            else:
                nk = (it[3] + 1) * P if it[0] == "nsa" else T
                nc.scalar.activation(probs_t[:, e, 0:nk], ps[:, 4, 0:nk], ACT.Copy).then_inc(pt_act, 1)

        def act_y(act, n):
            act.wait_ge(pv_psum, n + 1)
            src, dst = ps[:, 6, :], y[:, ends_pair(n), :]
            if n >= N_NSA:
                src, dst = src.rearrange("p (r i) -> p r i", r=CLS), dst.rearrange("p (i r) -> p r i", r=CLS)
            nc.scalar.activation(dst, src, ACT.Copy).then_inc(y_read, 1)

        def act_sigmoid(act, m):
            if m >= 2:
                act.wait_ge(gm_scaled, m - 1)
            for i in range(2):
                last = nc.scalar.activation(gate_args(m)[i], gate_args(m)[i], ACT.Sigmoid)
            last.then_inc(sig_ready, 1)

        def act_split_y(act, c):
            act.wait_ge(y_read, c + 1)
            act.wait_ge(scores_psum, N_NSA + 8)
            nc.scalar.activation(y_parts[c][0][:, :], y[:, c, :], ACT.Copy).then_inc(y_hi_ready, 1)

        def act_attend(act, a, b):
            act_exp(act, a)
            act_exp(act, a + 1)
            for n in range(a, b):
                act_copy_probs(act, n)
                if n + 2 < b:
                    act_exp(act, n + 2)
                if n > a and ends_pair(n - 1) is not None:
                    act_y(act, n - 1)
                c = filled(n - 1)
                if c is not None and ends_unit(c):
                    act_split(act, MIX0 + CH[c][1] + 2)
                if splits_y(n) is not None:
                    act_split_y(act, splits_y(n))
            act_y(act, b - 1)
            act_split_y(act, 5)

        @block.scalar
        def _(act):
            act.dma_start(const[:, :], consts).then_inc(const_landed, 16)
            for i, g in enumerate([norm_ffn1[0], norm_mix[0], norm_ffn2[0], norm_final]):
                act.dma_start(vec_rows[i * KD:i * KD + KD, :], g.rearrange("(m p) -> m p", p=P)).then_inc(vec_landed, 16)
            act.dma_start(vec_rows[32:64, :], cmp_pos[0].rearrange("v (j r) d -> (v j) (r d)", r=2)).then_inc(vec_landed, 16)
            act.wait_ge(gains_ready, 1)
            for m in range(KD):
                act_first_hi(act, m)
                if m == 1:
                    act_split(act, 0)
                if m == 3:
                    act_square(act, 0)
                    act_square(act, 1)
            act_split(act, 1)
            for m in range(2, KD):
                act_square(act, m)
            act_ffn(act, 0, 0, 0)
            for step in STEPS:
                if step[0] == "first_chunks":
                    act_split(act, MIX0 + 2)
                elif step[0] == "chunk":
                    if step[-1] != (0, KD // 2) and ends_unit(step[1]):
                        act_split(act, MIX0 + CH[step[1]][1] + 2)
                elif step[0] == "rstd":
                    act_std(act, 1)
                elif step[0] == "gates":
                    act.wait_ge(proj_read, C_Q)
                    g = gates[:, :, :].rearrange("p t c -> p (t c)")
                    nc.scalar.activation(g, g, ACT.Sigmoid).then_inc(gate_ready, 1)
                elif step[0] == "hidden":
                    for kv in range(2):
                        act.wait_ge(hidden_psum, 2)
                        nc.scalar.activation(hid[:, kv, :], ps[0:DH, 7, kv * P:kv * P + P],
                                             ACT.Silu).then_inc(hid_ready, 1)
                elif step[0] == "attend":
                    act_attend(act, step[1], step[2])
            act.wait_ge(proj_read, len(CH))
            act_sigmoid(act, 0)
            act_sigmoid(act, 1)
            for m in range(KD):
                if m % 2 == 0 and m + 2 < KD:
                    act_split(act, MIX0 + U_GM[m + 2] + 2)
                act.wait_ge(merged_ready, m + 1)
                nc.scalar.activation(merged[m][0][:, :], gate_args(m)[0], ACT.Copy).then_inc(m_hi, 1)
                if m % 2:
                    act_split(act, MIX0 + U_BR[m // 2] + 2)
                if m + 2 < KD:
                    act_sigmoid(act, m + 2)
                    if m % 2:
                        act_split(act, MIX0 + U_GM[m + 2] + 2)
            for m in range(KD):
                act_gain(act, 2, m)
                if m % 2:
                    act_split(act, MIX0 + U_WO[m // 2] + 2)
            act_ffn(act, 1, FFN2, 2)
            for tt in range(TT):
                if tt == 0:
                    act_std(act, 3)
                act.wait_ge(fin_psum, tt + 1)
                act.wait_ge(row_ready, 4)
                nc.scalar.activation(final_view(tt)[:, 0:T], ps[:, 2 * tt, :], ACT.Copy,
                                     scale=rstd_col[:, tt:tt + 1]).then_inc(fin_act, 1)

        chain = [0]

        def link(dve, ins):
            chain[0] += 1
            ins.then_inc(dve_chain, 1)
            dve.wait_ge(dve_chain, chain[0])

        V = nc.vector

        def dve_split(dve, j, it=0, half=None):
            s, k = j % 2, j
            if j >= N_UNITS:
                return
            w = width_of(j)
            c = slice(0, w) if half is None else slice(half * w // 2, (half + 1) * w // 2)
            dve.wait_ge(hi_ready, k + 1 + 2 * it)
            lo = V.tensor_tensor(w_lo[:, s, c], w_raw[:, s, c], w_hi[:, s, c].bitcast(F32), ALU.subtract)
            if half != 0:
                lo.then_inc(lo_ready, 1)

        def dve_gain(dve, n, m0, it=0):
            m, v = m0 + it, KD * n + m0 + it
            if n < 3:
                dve.wait_ge(g_hi, v + 1)
                V.scalar_tensor_tensor(out=tile_of(xg_lo, m), in0=tile_of(xT, m), scalar=gains[:, n, bass.ds(m, 1)],
                                       in1=tile_of(xg_hi, m).bitcast(F32), op0=ALU.mult,
                                       op1=ALU.subtract).then_inc(g_lo, 1)

        def dve_rstd(dve, n):
            w = TT + CLS if n == 1 else TT
            var, std, inv, t = (norm_s[:, i, 0:w] for i in range(4))
            dve.wait_ge(col_psum, n + 1)
            V.tensor_scalar(var, ps[:, 7, 0:2 * w].rearrange("p (t two) -> p t two", two=2)[:, :, 0],
                            1.0 / D, EPS, ALU.mult, ALU.add).then_inc(var_ready, 1)
            dve.wait_ge(std_ready, n + 1)
            link(dve, V.reciprocal(inv, std))
            link(dve, V.tensor_tensor(t, inv, inv, ALU.mult))
            link(dve, V.tensor_tensor(t, t, var, ALU.mult))
            link(dve, V.tensor_scalar(t, t, -0.5, 1.5, ALU.mult, ALU.add))
            if n == 3:
                V.tensor_tensor(rstd_col[:, 0:w], inv, t, ALU.mult).then_inc(row_ready, 1)
                return
            link(dve, V.tensor_tensor(rstd_col[:, 0:w], inv, t, ALU.mult))
            for tt in range(TT):
                last = V.tensor_scalar(tmp_a[:, tt * P:tt * P + P], ident, rstd_col[:, tt:tt + 1], None, ALU.mult)
            last.then_inc(diag_ready, 1)

        def dve_row(dve, n):
            dve.wait_ge(row_psum, n + 1)
            V.tensor_copy(rstd_row[:, :], ps[:, 6, :]).then_inc(row_ready, 1)
            dve.wait_ge(row_ready, n + 1)

        def dve_ffn(dve, i, base, norm):
            S = ffn_sems[i]

            def evac(f, s):
                dve.wait_ge(S["unit_done"], f + 1)
                V.tensor_tensor(tmp_a[:, :], ps[:, 2 * s, :], rstd_row[:, :], ALU.mult).then_inc(S["gate_scaled"], 1)
                if not (isinstance(f, int) and f == 0):
                    dve.wait_ge(S["prod_lo"], f)
                V.tensor_tensor(tmp_b[:, :], ps[:, 2 * s + 1, :], rstd_row[:, :], ALU.mult).then_inc(S["value_scaled"], 1)
                dve.wait_ge(S["silu_ready"], f + 1)
                dve.wait_ge(S["value_scaled"], f + 1)
                V.tensor_tensor(tmp_b[:, :], tmp_a[:, :], tmp_b[:, :], ALU.mult).then_inc(S["prod_ready"], 1)
                dve.wait_ge(S["prod_hi"], f + 1)
                V.tensor_tensor(tile_of(p_lo, f), tmp_b[:, :], tile_of(p_hi, f).bitcast(F32),
                                ALU.subtract).then_inc(S["prod_lo"], 1)

            def residual(m0, it=0):
                v = KD * (norm + 1) + m0 + it
                dve.wait_ge(S["unit_done"], FT + 2 * (m0 + it + 1))
                V.scalar_tensor_tensor(out=tile_of(xT, m0 + it), in0=ps[:, 4 + m0 % 2, :], scalar=0.5,
                                       in1=tile_of(xT, m0 + it), op0=ALU.mult, op1=ALU.add).then_inc(x_new, 1)
                dve_gain(dve, norm + 1, m0, it)

            dve_rstd(dve, norm)
            dve_split(dve, base + 2)
            dve_row(dve, norm)
            evac(0, 0)
            dve_split(dve, base + 3)
            evac(1, 1)
            if i == 0:
                dve_rope_tables(dve, 0)
            with dve.Fori(1, FT // 2 - 1) as it:
                for s in range(2):
                    dve_split(dve, base + s + 2, it)
                    evac(2 * it + s, s)
            for s in range(2):
                dve_split(dve, base + FT + s)
                evac(FT - 2 + s, s)
                if i == 0:
                    dve_rope_tables(dve, 1 + s)
            with dve.Fori(0, KD // 2 - 1) as it:
                for ml in range(2):
                    dve_split(dve, base + FT + 2 * ml + 2, 2 * it)
                    dve_split(dve, base + FT + 2 * ml + 3, 2 * it)
                    residual(ml, 2 * it)
            for ml in range(2):
                for h in range(2):
                    dve_split(dve, base + FU - 2 + 2 * ml + h)
                residual(KD - 2 + ml)

        def dve_rope_tables(dve, part):
            angle = sin_t[:, :]
            if part == 0:
                dve.wait_ge(pos_landed, 16)
                link(dve, V.tensor_copy(angle, cos_t[:, :].bitcast(I32)))
                link(dve, V.tensor_scalar(angle, angle, freq, None, ALU.mult))
            elif part == 1:
                turns = tmp_a[:, :]
                link(dve, V.tensor_scalar(turns, angle, float(1 / (2 * np.pi)), MAGIC, ALU.mult, ALU.add))
                link(dve, V.tensor_scalar(turns, turns, MAGIC, None, ALU.subtract))
                for piece in TWO_PI:
                    link(dve, V.scalar_tensor_tensor(out=angle, in0=turns, scalar=-piece, in1=angle,
                                                     op0=ALU.mult, op1=ALU.add))
                link(dve, V.scalar_tensor_tensor(out=turns, in0=angle, scalar=-1.0, in1=angle,
                                                 op0=ALU.mult, op1=ALU.max))
                V.tensor_scalar(cos_t[:, :], turns, -0.5, float(np.pi / 2), ALU.mult, ALU.add).then_inc(rope_args, 1)
                dve.wait_ge(rope_args, 1)
            else:
                dve.wait_ge(rope_sines, 2)
                link(dve, V.scalar_tensor_tensor(out=tmp_a[:, :], in0=sin_t[:, :], scalar=2.0, in1=cos_t[:, :],
                                                 op0=ALU.mult, op1=ALU.mult))
                link(dve, V.tensor_tensor(cos_t[:, :], sin_t[:, :], sin_t[:, :], ALU.mult))
                link(dve, V.tensor_scalar(cos_t[:, :], cos_t[:, :], -2.0, 1.0, ALU.mult, ALU.add))
                link(dve, V.tensor_copy(sin_t[:, :], tmp_a[:, :]))

        def dve_chunk(dve, c):
            kind, _, i, name = CH[c]
            dve.wait_ge(proj_psum, c + 1)
            b = bank_of(c)
            if kind == "n":
                dst = v_nsa[:, i, :, :].rearrange("p a c -> p (a c)") if name == "v" else v_dil[:, i, int(name[2]), :]
                at = TT + i if by_class(name) else i
                if name == "v":
                    V.tensor_scalar(gates[:, i, :], ps[:, b, 256:VCOL], rstd_col[:, i:i + 1], None, ALU.mult)
                V.tensor_scalar(dst, ps[:, b, 0:256], rstd_col[:, at:at + 1], None, ALU.mult).then_inc(proj_read, 1)
            elif name in ("gm0", "gm1", "gm2", "gm3"):
                if name == "gm0":
                    dve.wait_ge(rope_done, len(ROPED))
                m = int(name[2]) // 2
                V.tensor_tensor(gate_args(m)[i], ps[:, b, :], rstd_row[:, :], ALU.mult).then_inc(proj_read, 1)
            else:
                V.tensor_tensor(pool[:, slot_of[name], :], ps[:, b, :], rstd_row[:, :], ALU.mult).then_inc(proj_read, 1)

        def dve_tokens(dve):
            dve.wait_ge(tokens_landed, 16 * 8)
            dve.wait_ge(padded, 1)
            for kv in range(2):
                for g in range(2):
                    tv = pool[:, 12 + 2 * kv + g, :].rearrange("p (n j two) -> p j n two", n=NC, j=8)
                    av = probs_t[:, kv, 0:2 * 512].rearrange("p (j g n) -> p j g n", j=16, g=2)
                    for h in range(2):
                        last = V.tensor_tensor(
                            av[:, 8 * h:8 * h + 8, g, 0:NCMP], tv[:, :, h:h + NCMP, 0],
                            pos_t[:, kv, 8 * h:8 * h + 8].unsqueeze(2).broadcast_to([P, 8, NCMP]), ALU.add)
            last.then_inc(tok_ready, 1)

        def dve_prepare(dve, n):
            it, e, b = ITEMS[n], n % 2, 2 * (n % 2)
            dve.wait_ge(scores_psum, n + 1)
            if it[0] == "cmp":
                sc = ps[:, b, :].rearrange("p (q k) -> p q k", q=TT)[:, :, 0:NC]
                link(dve, V.tensor_reduce(stat[:, e, 0, 0:4], sc, AX.X, ALU.max))
                link(dve, V.tensor_scalar(stat[:, e, 0, 0:4], stat[:, e, 0, 0:4], -1e28, None, ALU.max))
                if n >= 2:
                    dve.wait_ge(trans_psum, n - 1)
                V.tensor_tensor(probs[:, e, 0:P].rearrange("p (q n) -> p q n", q=TT), sc,
                                stat[:, e, 0, 0:4].unsqueeze(2).broadcast_to([P, TT, NC]),
                                ALU.subtract).then_inc(bias_ready, 1)
                return
            nk = (it[3] + 1) * P
            if it[0] == "nsa":
                link(dve, V.tensor_reduce(stat[:, e, 0, 0:2], ps[:, b:b + 2, 0:nk], AX.X, ALU.max))
                V.tensor_scalar(stat[:, e, 1, 0:2], stat[:, e, 0, 0:2], -SCALE, None, ALU.mult).then_inc(bias_ready, 1)
            else:
                V.tensor_reduce(stat[:, e, 0, 0:1], ps[:, b, :], AX.X, ALU.max)
                link(dve, V.tensor_reduce(stat[:, e, 0, 1:2], ps[:, b + 1, 0:2 * P], AX.X, ALU.max))
                V.tensor_scalar(stat[:, e, 1, 0:1], stat[:, e, 0, 0:1], stat[:, e, 0, 1:2], -SCALE,
                                ALU.max, ALU.mult).then_inc(bias_ready, 1)

        def dve_factor(dve, n):
            it, e = ITEMS[n], n % 2
            dve.wait_ge(exp_ready, n + 1)
            if it[0] == "cmp":
                h = it[2] * HPG + it[1]
                link(dve, V.tensor_reduce(stat[:, e, 2, 0:4], probs[:, e, 0:P].rearrange("p (q n) -> p q n", q=TT),
                                          AX.X, ALU.add))
                link(dve, V.tensor_scalar(stat[:, e, 2, 0:4], stat[:, e, 2, 0:4], 0.5, None, ALU.max))
                link(dve, V.reciprocal(stat[:, e, 0, 0:4], stat[:, e, 2, 0:4]))
                V.tensor_tensor(stat[:, e, 3, 0:4], stat[:, e, 0, 0:4], gates[:, :, 3 * h], ALU.mult).then_inc(factor_ready, 1)
                dve.wait_ge(factor_ready, n + 1)
                v = probs[:, e, 0:P].rearrange("p (q n) -> p q n", q=TT)
                V.tensor_tensor(v, v, stat[:, e, 3, 0:4].unsqueeze(2).broadcast_to([P, TT, NC]),
                                ALU.mult).then_inc(scaled_ready, 1)
            elif it[0] == "nsa":
                h = it[2] * HPG + it[1]
                link(dve, V.reciprocal(stat[:, e, 0, 0:2], stat[:, e, 2, 0:2]))
                V.tensor_tensor(stat[:, e, 3, 0:2], stat[:, e, 0, 0:2], gates[:, it[3], 3 * h + 1:3 * h + 3],
                                ALU.mult).then_inc(factor_ready, 1)
                dve.wait_ge(factor_ready, n + 1)
                nk = (it[3] + 1) * P
                V.tensor_scalar(probs[:, e, 0:nk], probs[:, e, 0:nk], stat[:, e, 3, 0:1], None, ALU.mult)
                V.tensor_scalar(probs[:, e, T:T + nk], probs[:, e, T:T + nk], stat[:, e, 3, 1:2], None,
                                ALU.mult).then_inc(scaled_ready, 1)
            else:
                link(dve, V.tensor_tensor(stat[:, e, 2, 3:4], stat[:, e, 2, 0:1], stat[:, e, 2, 1:2], ALU.add))
                V.reciprocal(stat[:, e, 3, 0:1], stat[:, e, 2, 3:4]).then_inc(factor_ready, 1)
                dve.wait_ge(factor_ready, n + 1)
                v = probs[:, e, 0:T + 2 * P]
                V.tensor_scalar(v, v, stat[:, e, 3, 0:1], None, ALU.mult).then_inc(scaled_ready, 1)

        def dve_copy_probs(dve, n):
            it, e = ITEMS[n], n % 2
            dve.wait_ge(trans_psum, n + 1)
            if n >= 2:
                dve.wait_ge(pv_psum, n - 1)
            if it[0] == "cmp":
                V.tensor_copy(probs_t[0:NC, e, 256:T], ps[0:NC, 5, 256:T]).then_inc(pt_dve, 1)
                return
            nk = (it[3] + 1) * P if it[0] == "nsa" else 2 * P
            V.tensor_copy(probs_t[:, e, T:T + nk], ps[:, 5, 0:nk]).then_inc(pt_dve, 1)

        def dve_split_y(dve, c):
            dve.wait_ge(y_hi_ready, c + 1)
            V.tensor_tensor(y_parts[c][1][:, :], y[:, c, :], y_parts[c][0][:, :].bitcast(F32),
                            ALU.subtract).then_inc(y_lo_ready, 1)

        def dve_attend(dve, a, b):
            dve_prepare(dve, a)
            dve_prepare(dve, a + 1)
            dve.wait_ge(gate_ready, 1)
            dve_factor(dve, a)
            for n in range(a, b):
                if n + 1 < b:
                    dve_factor(dve, n + 1)
                dve_copy_probs(dve, n)
                c = filled(n - 1)
                if c is not None:
                    dve_chunk(dve, c)
                if n + 2 < b:
                    dve_prepare(dve, n + 2)
                if c is not None and ends_unit(c):
                    dve_split(dve, MIX0 + CH[c][1] + 2, half=0)
                c = filled(n - 2)
                if c is not None and ends_unit(c):
                    dve_split(dve, MIX0 + CH[c][1] + 2, half=1)
                if splits_y(n - 1) is not None:
                    dve_split_y(dve, splits_y(n - 1))
            if filled(b - 2) is not None:
                dve_split(dve, MIX0 + CH[filled(b - 2)][1] + 2, half=1)

        @block.vector
        def _(dve):
            dve.wait_ge(const_landed, 16)
            dve.wait_ge(gains_psum, 1)
            V.tensor_copy(vec_cols[:, :], ps[:, 7, 0:64]).then_inc(gains_ready, 1)
            dve.wait_ge(gains_ready, 1)
            for m in range(KD):
                if m == 2:
                    dve_split(dve, 0)
                dve.wait_ge(g_hi, m + 1)
                V.scalar_tensor_tensor(out=xg_lo[:, m, :], in0=ps[:, m, :], scalar=gains[:, 0, m:m + 1],
                                       in1=xg_hi[:, m, :].bitcast(F32), op0=ALU.mult, op1=ALU.subtract).then_inc(g_lo, 1)
                if m < 2:
                    V.tensor_copy(xT[:, m, :], ps[:, m, :]).then_inc(x_new, 1)
            for m in range(2, KD):
                V.tensor_copy(xT[:, m, :], ps[:, m, :]).then_inc(x_new, 1)
            dve_split(dve, 1)
            dve_ffn(dve, 0, 0, 0)
            for step in STEPS:
                if step[0] == "rstd":
                    dve_rstd(dve, 1)
                    dve_split(dve, MIX0 + 2)
                elif step[0] == "row":
                    dve_row(dve, 1)
                    dve_chunk(dve, 0)
                    dve_chunk(dve, 1)
                    dve_chunk(dve, 2)
                elif step[0] == "chunk":
                    c = step[1]
                    if c > 2 and step[-1] != (0, KD // 2):
                        dve_chunk(dve, c)
                        if ends_unit(c) and c != C_Q + 3:
                            dve_split(dve, MIX0 + CH[c][1] + 2)
                    if c == C_Q:
                        dve_tokens(dve)
                elif step[0] == "hidden_t":
                    dve.wait_ge(hidt_psum, 1)
                    V.tensor_copy(hid_t[:, :, :].rearrange("p a c -> p (a c)"), ps[:, 7, 256:384]).then_inc(hidt_ready, 1)
                elif step[0] == "cmp_kv":
                    dve.wait_ge(cmp_psum, 1)
                    V.tensor_copy(k_cmp[:, 0:NC], ps[:, 7, 384:384 + NC])
                    V.tensor_copy(v_cmp[:, :, :].rearrange("p a c -> p (a c)"), ps[0:NC, 7, 0:P]).then_inc(cmp_ready, 1)
                    dve_split(dve, MIX0 + CH[C_Q + 3][1] + 2)
                elif step[0] == "attend":
                    dve_attend(dve, step[1], step[2])
            dve_split_y(dve, 5)
            for m in range(KD):
                if m % 2 == 0 and m + 2 < KD:
                    dve_split(dve, MIX0 + U_GM[m + 2] + 2)
                b0 = merge_banks(m)[1]
                ga, gb = gate_args(m)
                dve.wait_ge(sig_ready, m + 1)
                dve.wait_ge(br_psum, m + 1)
                V.tensor_tensor(ga, ps[:, b0, :], ga, ALU.mult)
                V.tensor_tensor(gb, ps[:, b0 + 1, :], gb, ALU.mult).then_inc(merge_read, 1)
                dve.wait_ge(merge_read, m + 1)
                V.tensor_tensor(ga, ga, gb, ALU.add).then_inc(merged_ready, 1)
                dve.wait_ge(m_hi, m + 1)
                V.tensor_tensor(merged[m][1][:, :], ga, merged[m][0][:, :].bitcast(F32),
                                ALU.subtract).then_inc(m_lo, 1)
                if m % 2:
                    dve_split(dve, MIX0 + U_BR[m // 2] + 2)
                if m + 2 < KD:
                    g0, g1 = merge_banks(m + 2)[0]
                    dve.wait_ge(gm_psum, m + 1)
                    dve.wait_ge(m_lo, m + 1)
                    V.tensor_tensor(ga, ps[:, g0, :], rstd_row[:, :], ALU.mult)
                    V.tensor_tensor(gb, ps[:, g1, :], rstd_row[:, :], ALU.mult).then_inc(gm_scaled, 1)
                    if m % 2:
                        dve_split(dve, MIX0 + U_GM[m + 2] + 2)
            for m in range(KD):
                dve.wait_ge(wo_psum, m + 1)
                V.tensor_tensor(xT[:, m, :], ps[:, wo_bank(m), :], xT[:, m, :], ALU.add).then_inc(x_new, 1)
                dve_gain(dve, 2, m)
                if m % 2:
                    dve_split(dve, MIX0 + U_WO[m // 2] + 2)
            dve_ffn(dve, 1, FFN2, 2)
            dve_rstd(dve, 3)
            dve.wait_ge(row_ready, 4)
            for tt in range(TT):
                dve.wait_ge(fin_psum, tt + 1)
                V.tensor_scalar(final_view(tt)[:, T:D], ps[:, 2 * tt + 1, :], rstd_col[:, tt:tt + 1], None,
                                ALU.mult).then_inc(fin_dve, 1)

        mm = nc.tensor.matmul

        def three_pass(out, pairs, before=None, first=True, final=True):
            for i, ((ah, al), (bh, bl)) in enumerate(pairs):
                if before:
                    before(i)
                mm(out, ah, bh, start=(first and i == 0), stop=False)
                mm(out, ah, bl, start=False, stop=False)
                last = mm(out, al, bh, start=False, stop=(final and i == len(pairs) - 1))
            return last

        def wtile(s, at, c=P):
            return w_hi[:, s, at:at + c], w_lo[:, s, at:at + c]

        def pe_col(pe, n):
            pe.wait_ge(acc_done, KD * (n + 1))
            for tt in range(TT):
                last = mm(ps[:, 7, 2 * tt:2 * tt + 2], sumsq[:, tt * P:tt * P + P], ones[:, 0:2], start=True, stop=True)
            if n == 1:
                for c in range(CLS):
                    last = mm(ps[:, 7, 2 * (TT + c):2 * (TT + c) + 2], of_class(sumsq[:, :], c), ones[:, 0:2],
                              start=True, stop=True)
            last.then_inc(col_psum, 1)

        def pe_row(pe, n):
            pe.wait_ge(diag_ready, n + 1)
            for tt in range(TT):
                last = mm(ps[:, 6, tt * P:tt * P + P], ones, tmp_a[:, tt * P:tt * P + P], start=True, stop=True)
            last.then_inc(row_psum, 1)

        def part_of(hi_lo):
            return hi_lo[0][:, :], hi_lo[1][:, :]

        def pe_final(tt, m):
            return nc.tensor.transpose(ps[:, 2 * tt + m // 4, (m % 4) * P:(m % 4) * P + P],
                                       xT[:, m, tt * P:tt * P + P], ident)

        def pe_final_early(pe):
            pe.wait_ge(z_ready, KD - 1)
            for tt in range(TT):
                for m in range(KD - 1):
                    if m < 4 or tt < 2:
                        pe_final(tt, m)

        def moving(k):
            return xg_hi[:, k, :], xg_lo[:, k, :]

        def two_products(out, sl, before):
            for k in range(KD):
                before(k)
                for i in range(2):
                    last = three_pass(out[i], [(wtile(sl, (i * KD + k) * P), moving(k))], first=k == 0, final=k == KD - 1)
                    if k == KD - 1:
                        yield last

        def pe_ffn(pe, i, base, norm):
            S = ffn_sems[i]
            k0 = base

            def up(f, s, steps=()):
                sl = (base + s) % 2
                pe.wait_ge(lo_ready, k0 + f + 1)
                if norm == 0 and isinstance(f, int) and f < 2:
                    pe.wait_ge(x_new, 2 * f + 2)
                if isinstance(f, int) and f == 0:
                    last = list(two_products((ps[:, 0, :], ps[:, 1, :]), sl,
                                             lambda k: pe.wait_ge(g_lo, KD * norm + k + 1)))[1]
                    last.then_inc(S["unit_done"], 1)
                    return
                if not (isinstance(f, int) and f < 2):
                    pe.wait_ge(S["value_scaled"], f - 1)
                u, v = ([(wtile(sl, (i * KD + k) * P), moving(k)) for k in range(KD)] for i in range(2))
                if steps:
                    three_pass(ps[:, 2 * s, :], u[:KD // 2], final=False)
                    steps[0]()
                    three_pass(ps[:, 2 * s, :], u[KD // 2:], first=False)
                    steps[1]()
                else:
                    three_pass(ps[:, 2 * s, :], u)
                three_pass(ps[:, 2 * s + 1, :], v).then_inc(S["unit_done"], 1)

            def down(m0, it=0, first=False, between=None):
                bank = ps[:, 4 + m0 % 2, :]
                v = KD * (norm + 1) + m0 + it
                if not first:
                    pe.wait_ge(x_new, v - 1)
                for h in range(2):
                    sl = (base + h) % 2
                    pe.wait_ge(lo_ready, k0 + FT + 2 * (m0 + it) + h + 1)
                    if first:
                        pe.wait_ge(S["prod_lo"], (h + 1) * HALF)
                    for t in range(HALF):
                        (ah, al), f = wtile(sl, t * P), h * HALF + t
                        mm(bank, ah, p_hi[:, f, :], start=(f == 0), stop=False)
                        mm(bank, ah, p_lo[:, f, :], start=False, stop=False)
                        last = mm(bank, al, p_hi[:, f, :], start=False, stop=(f == FT - 1))
                    last.then_inc(S["unit_done"], 1)
                    if between and h == 0:
                        between()

            up(0, 0)
            up(1, 1, (lambda: pe_col(pe, norm), lambda: pe_row(pe, norm)))
            with pe.Fori(1, FT // 2) as it:
                for s in range(2):
                    up(2 * it + s, s)
            down(0, 0, True)
            down(1, 0, True)
            with pe.Fori(1, KD // 2 - 1) as it:
                for ml in range(2):
                    down(ml, 2 * it)
            down(KD - 2)
            down(KD - 1, between=(lambda: pe_final_early(pe)) if i else None)

        def pe_chunk(pe, c, part=(0, KD)):
            kind, u, i, name = CH[c]
            sl = (MIX0 + u) % 2
            bank = ps[:, bank_of(c), :]
            if part[0] == 0 and bank_of(c) == 7:
                pe.wait_ge(proj_read, c)
            elif part[0] == 0 and c >= 4:
                pe.wait_ge(proj_read, c - 3)
            if kind == "t":
                pairs = [(wtile(sl, (i * KD + k) * P), moving(k)) for k in range(*part)]
                last = three_pass(bank, pairs, first=part[0] == 0, final=part[1] == KD)
            else:
                def wm(t, k):
                    if name == "v":
                        return t[:, sl, k * VCOL:(k + 1) * VCOL]
                    return t[:, sl, 0:SLOT].rearrange("p (i k r) -> p i k r", i=2, k=KD)[:, :, k, :]

                def tokens(t, k):
                    return of_class(t[:, k, :], i) if by_class(name) else t[:, k, i * P:i * P + P]

                out_ = bank[:, 0:VCOL] if name == "v" else bank[:, 0:256].rearrange("p (i r) -> p i r", i=2)
                last = three_pass(out_, [((tokens(xg_hi, k), tokens(xg_lo, k)), (wm(w_hi, k), wm(w_lo, k)))
                                         for k in range(*part)], first=part[0] == 0, final=part[1] == KD)
            if part[1] == KD:
                last.then_inc(proj_psum, 1)

        def pe_scores(pe, n):
            it, b = ITEMS[n], 2 * (n % 2)
            if n >= 2:
                pe.wait_ge(exp_ready, n - 1)
            if it[0] == "cmp":
                _, hh, g = it
                rows = slice(g * DH, g * DH + DH)
                for qt in range(TT):
                    mm(ps[:, b, qt * P:qt * P + P], pool[rows, Q_RAW + hh, qt * P:qt * P + P], k_cmp[rows, :],
                       start=True, stop=False)
                    last = mm(ps[:, b, qt * P:qt * P + NC], ident_b, cmp_b[:, qt * NC:qt * NC + NC],
                              start=False, stop=True)
                last.then_inc(scores_psum, 1)
                return
            if it[0] == "nsa":
                _, hh, g, qt = it
                if g == 0 and qt == 0:
                    pe.wait_ge(rope_done, 3 + hh)
                rows, nk = slice(g * DH, g * DH + DH), (qt + 1) * P
                for i, keys in enumerate((KS, KW)):
                    mm(ps[:, b + i, 0:nk], pool[rows, Q_ROPE + hh, qt * P:qt * P + P], pool[rows, keys, 0:nk],
                       start=True, stop=False)
                    last = mm(ps[:, b + i, nk - P:nk], ident_b, causal_b, start=False, stop=True)
                last.then_inc(scores_psum, 1)
                return
            _, hp, hl, c = it
            rows = slice(hl * DH, hl * DH + DH)
            if n == N_NSA:
                pe.wait_ge(rope_done, ROPED.index(N_CH2))
            if n == N_NSA + 8:
                pe.wait_ge(rope_done, len(ROPED))
            q, k = ([pool[rows, s[hp] + g, :] for g in range(3)] for s in (QD, KDS))
            mm(ps[:, b, :], of_class(q[0], c), k[0], start=True, stop=False)
            mm(ps[:, b, :], ident_b, band_b[:, CLS - 1 - c:CLS - 1 - c + T], start=False, stop=True)
            for g, kept in ((1, causal_b), (2, class_b)):
                out_ = ps[:, b + 1, (g - 1) * P:g * P]
                mm(out_, of_class(q[g], c), of_class(k[g], c), start=True, stop=False)
                last = mm(out_, ident_b, kept, start=False, stop=True)
            last.then_inc(scores_psum, 1)

        def pe_transpose_probs(pe, n):
            it, e = ITEMS[n], n % 2
            pe.wait_ge(scaled_ready, n + 1)
            if n:
                pe.wait_ge(pt_act, n)
                pe.wait_ge(pt_dve, n)
            if it[0] == "cmp":
                for qt in range(TT):
                    last = nc.tensor.transpose(ps[0:NC, 4 + qt // 2, qt * P:qt * P + P],
                                               probs[:, e, qt * NC:qt * NC + NC], ident)
                last.then_inc(trans_psum, 1)
                return
            for i in range(2):
                for kt in range(it[3] + 1 if it[0] == "nsa" else (TT, 2)[i]):
                    last = nc.tensor.transpose(ps[:, 4 + i, kt * P:kt * P + P],
                                               probs[:, e, i * T + kt * P:i * T + kt * P + P], ident)
            last.then_inc(trans_psum, 1)

        def pe_values(pe, n):
            it, e = ITEMS[n], n % 2
            pe.wait_ge(pt_act, n + 1)
            pe.wait_ge(pt_dve, n + 1)
            pair = n // 10 if n < N_NSA else 4 + (n - N_NSA) // 8
            if pair:
                pe.wait_ge(y_read, pair)
            if it[0] == "cmp":
                g = it[2]
                mm(ps[g * DH:g * DH + DH, 6, :], v_cmp[:, g, :], probs_t[0:NC, e, 0:T],
                   start=True, stop=False).then_inc(pv_psum, 1)
                return
            if it[0] == "nsa":
                _, hh, g, qt = it
                out_ = ps[g * DH:g * DH + DH, 6, qt * P:qt * P + P]
                for i in range(2):
                    for kt in range(qt + 1):
                        last = mm(out_, v_nsa[:, kt, i, g * DH:g * DH + DH],
                                  probs_t[:, e, i * T + kt * P:i * T + kt * P + P],
                                  start=False, stop=(i == 1 and kt == qt and qt == TT - 1))
                last.then_inc(pv_psum, 1)
                return
            _, hp, hl, c = it
            out_ = ps[hl * DH:hl * DH + DH, 6, c * P:c * P + P]
            cols = slice(hp * P + hl * DH, hp * P + hl * DH + DH)
            terms = [(0, kt, kt * P) for kt in range(TT)] + [(1, c, T), (2, c, T + P)]
            for j, (g, kt, at) in enumerate(terms):
                last = mm(out_, v_dil[:, kt, g, cols], probs_t[:, e, at:at + P], start=(j == 0), stop=(j == len(terms) - 1))
            last.then_inc(pv_psum, 1)

        def pe_fill(pe, n):
            c, part = FILL[n]
            pe.wait_ge(lo_ready, MIX0 + CH[c][1] + 1)
            pe_chunk(pe, c, part)

        def pe_attend(pe, a, b):
            pe_scores(pe, a)
            pe_scores(pe, a + 1)
            pe_fill(pe, -1)
            for n in range(a, b):
                pe_transpose_probs(pe, n)
                if n + 2 < b:
                    pe_scores(pe, n + 2)
                if n > a:
                    pe_values(pe, n - 1)
                if n in FILL:
                    pe_fill(pe, n)
            pe.wait_ge(lo_ready, MIX0 + U_GM[2] + 1)
            pe.wait_ge(proj_read, len(CH))
            pe_merge_gate(pe, 2, 0)
            pe_values(pe, b - 1)
            pe_merge_gate(pe, 2, 1)

        def pe_merge_gate(pe, m, i):
            sl = (MIX0 + U_GM[m]) % 2
            last = three_pass(ps[:, merge_banks(m)[0][i], :], [(wtile(sl, (i * KD + k) * P), moving(k)) for k in range(KD)])
            if i:
                last.then_inc(gm_psum, 1)

        @block.tensor
        def _(pe):
            pe.wait_ge(const_landed, 16)
            for h in range(2):
                pe.wait_ge(x_landed[h], 16 * TT)
                for m in range(h * KD // 2, (h + 1) * KD // 2):
                    if m == KD - 1:
                        pe.wait_ge(gains_ready, 1)
                    for tt in range(TT):
                        last = nc.tensor.transpose(ps[:, m, tt * P:tt * P + P], x_nat[:, tt, m * P:m * P + P], ident)
                    last.then_inc(xt_psum, 1)
                if h == 0:
                    pe.wait_ge(vec_landed, 16 * 5)
                    nc.tensor.transpose(ps[:, 7, 0:64], vec_rows[:, :], ident[0:64, 0:64]).then_inc(gains_psum, 1)
            pe_ffn(pe, 0, 0, 0)
            for step in STEPS:
                if step[0] == "first_chunks":
                    pe.wait_ge(lo_ready, MIX0 + 1)
                    for last in two_products((ps[:, 0, :], ps[:, 1, :]), MIX0 % 2,
                                             lambda k: pe.wait_ge(g_lo, KD + k + 1)):
                        last.then_inc(proj_psum, 1)
                elif step[0] == "chunk":
                    c = step[1]
                    pe.wait_ge(lo_ready, MIX0 + CH[c][1] + 1)
                    pe_chunk(pe, c, *step[2:])
                elif step[0] == "rstd":
                    pe_col(pe, 1)
                elif step[0] == "row":
                    pe_row(pe, 1)
                elif step[0] == "hidden":
                    pe.wait_ge(tok_ready, 1)
                    pe.wait_ge(var_ready, 2)
                    pe.wait_ge(w1_landed, 32)
                    for kv in range(2):
                        for p in range(16):
                            last = mm(ps[0:DH, 7, kv * P:kv * P + P], probs_t[:, kv, p * DH:p * DH + DH],
                                      cmp_w1_tiles[kv][:, p, :], start=(p == 0), stop=(p == 15))
                        last.then_inc(hidden_psum, 1)
                elif step[0] == "hidden_t":
                    pe.wait_ge(hid_ready, 2)
                    for kv in range(2):
                        last = nc.tensor.transpose(ps[:, 7, 256 + kv * DH:256 + kv * DH + DH], hid[:, kv, :],
                                                   ident[0:DH, 0:DH])
                    last.then_inc(hidt_psum, 1)
                elif step[0] == "cmp_kv":
                    pe.wait_ge(hidt_ready, 1)
                    pe.wait_ge(small_landed, 16 * 2)
                    for g in range(2):
                        mm(ps[g * DH:g * DH + DH, 7, 384:384 + NC], w2[:, 0, :], hid_t[:, 0, g * NC:g * NC + NC],
                           start=True, stop=True)
                    for g in range(2):
                        last = mm(ps[0:NC, 7, g * DH:g * DH + DH], hid_t[:, 1, g * NC:g * NC + NC], w2[:, 1, :],
                                  start=True, stop=True)
                    last.then_inc(cmp_psum, 1)
                elif step[0] == "read_rest":
                    pe.wait_ge(proj_read, N_PRE)
                    pe.wait_ge(cmp_ready, 1)
                elif step[0] == "attend":
                    if step[1] == 0:
                        pe.wait_ge(small_landed, 16 * 2)
                    pe_attend(pe, step[1], step[2])
            pe.wait_ge(exp_ready, len(ITEMS))
            pe.wait_ge(pt_act, len(ITEMS))
            pe.wait_ge(pt_dve, len(ITEMS))
            pe.wait_ge(y_read, 6)
            for p in range(KD // 2):
                for m in (2 * p + 2, None, 2 * p + 3):
                    if m is None:
                        j = MIX0 + U_BR[p]
                        pe.wait_ge(lo_ready, j + 1)
                        for ml in range(2):
                            b0 = merge_banks(ml)[1]
                            if p:
                                pe.wait_ge(merge_read, 2 * p + ml - 1)
                            else:
                                pe.wait_ge(y_lo_ready, 6)
                            three_pass(ps[:, b0, :], [(wtile(j % 2, c * 256 + ml * P), part_of(y_parts[c]))
                                                      for c in range(4)])
                            three_pass(ps[:, b0 + 1, :], [(wtile(j % 2, c * 256 + ml * P), part_of(y_parts[c]))
                                                          for c in range(4, 6)]).then_inc(br_psum, 1)
                    elif 2 < m < KD:
                        pe.wait_ge(lo_ready, MIX0 + U_GM[m] + 1)
                        if m >= 4:
                            pe.wait_ge(gm_scaled, m - 3)
                        pe_merge_gate(pe, m, 0)
                        pe_merge_gate(pe, m, 1)
            pe.wait_ge(lo_ready, MIX0 + U_WO[0] + 1)
            pe.wait_ge(merge_read, KD - 1)
            sl = (MIX0 + U_WO[0]) % 2
            for k in range(KD):
                pe.wait_ge(m_lo, k + 1)
                for m in range(2):
                    last = three_pass(ps[:, m, :], [(wtile(sl, k * 256 + m * P), part_of(merged[k]))],
                                      first=k == 0, final=k == KD - 1)
                    if k == KD - 1:
                        last.then_inc(wo_psum, 1)
            for m in range(2, KD):
                sl = (MIX0 + U_WO[m // 2]) % 2
                pe.wait_ge(lo_ready, MIX0 + U_WO[m // 2] + 1)
                if m not in (4, 5):
                    pe.wait_ge(x_new, 2 * KD + m - 1)
                three_pass(ps[:, wo_bank(m), :], [(wtile(sl, k * 256 + (m % 2) * P), part_of(merged[k]))
                                                  for k in range(KD)]).then_inc(wo_psum, 1)
            pe_ffn(pe, 1, FFN2, 2)
            pe.wait_ge(acc_done, KD * 3 + KD - 1)
            for tt in range(TT):
                mm(ps[:, 7, 2 * tt:2 * tt + 2], sumsq[:, tt * P:tt * P + P], ones[:, 0:2], start=(tt == 0), stop=False)
            pe.wait_ge(x_new, KD * 4)
            for m in range(4, KD - 1):
                pe_final(2, m)
            pe.wait_ge(sq_ready, KD * 4)
            for tt in range(TT):
                last = mm(ps[:, 7, 2 * tt:2 * tt + 2], square[:, (KD - 1) % 2, tt * P:tt * P + P], ones[:, 0:2],
                          start=False, stop=(tt == TT - 1))
            last.then_inc(col_psum, 1)
            pe.wait_ge(z_ready, KD)
            for tt in range(TT - 1):
                pe_final(tt, KD - 1).then_inc(fin_psum, 1)
            pe.wait_ge(var_ready, 4)
            for m in range(4, KD):
                last = pe_final(TT - 1, m)
            last.then_inc(fin_psum, 1)


_INS = ["x", "positions", "norm_ffn1", "ffn1_w_in", "ffn1_w_out", "norm_mix", "w_in", "cmp_pos", "cmp_w1",
        "cmp_w2", "w_branch_nsa", "w_branch_dil", "w_out", "norm_ffn2", "ffn2_w_in", "ffn2_w_out", "norm_final"]


def kernel(**inputs):
    import concourse.bacc as bacc
    from concourse.bass_utils import run_bass_kernel_spmd

    nc = bacc.Bacc("TRN2", target_bir_lowering=False, num_devices=1)
    arrays, args = {}, []

    def give(name, a):
        arrays[name] = a
        args.append(nc.dram_tensor(name, a.shape, mybir.dt.from_np(a.dtype), kind="ExternalInput").ap())

    for name in _INS:
        give(f"in_{name}", np.ascontiguousarray(inputs[name]))
    f, b = shape_constants()
    give("shape_constants", f)
    give("shape_masks", b)
    args.append(nc.dram_tensor("out_0", (1, T, D), F32, kind="ExternalOutput").ap())
    build(nc, *args)
    r = run_bass_kernel_spmd(nc, [arrays], core_ids=[0])
    return r.results[0]["out_0"]
```
